# Optimizing a Trainium2 kernel written in Bass

```python
import math, functools
import jax, jax.numpy as jnp
from jax import lax
import numpy as np

D_MODEL = 1024
BATCH = 1
SEQ = 1024
DEPTH = 1
DEC_BATCH = 8
DEC_SEQ = 1
PAST_LEN = 512
PAGE_SIZE = 128

BR_WIDTH = 512
N_BRANCH = 4
DN_HEADS = 4
DN_DK = 128
DN_DV = 128
DN_QKV = 2 * DN_HEADS * DN_DK + DN_HEADS * DN_DV
DN_CHUNK = 64
CONV_W = 4
LRU_WIDTH = 512
LRU_BLOCKS = 8
LRU_BW = LRU_WIDTH // LRU_BLOCKS
LRU_C = 8.0
FOX_HEADS = 4
FOX_HD = 128
Q_BLOCK = 128
FOX_F_BIAS = 3.0
MEM_TOKENS = 256
MEM_HEADS = 4
MEM_HD = 128
EPS = 1e-6
F32 = jnp.float32

IN_SIZES = (
    DN_QKV, DN_HEADS * DN_DV, DN_HEADS, DN_HEADS,
    LRU_WIDTH, LRU_WIDTH,
    FOX_HEADS * FOX_HD, FOX_HEADS * FOX_HD, FOX_HEADS * FOX_HD, FOX_HEADS, FOX_HEADS * FOX_HD,
    MEM_HEADS * MEM_HD, MEM_HEADS * MEM_HD,
    N_BRANCH * D_MODEL)
IN_OFFSETS = tuple(int(o) for o in np.cumsum(IN_SIZES)[:-1])
N_IN = int(sum(IN_SIZES))
FOX_F_OFF = int(sum(IN_SIZES[:9]))

kernel_name = 'hybrid_gdn_rglru_fox_mem_step'

def rms_norm(x, w):
    xf = x.astype(F32)
    y = xf * lax.rsqrt(jnp.mean(xf * xf, axis=-1, keepdims=True) + EPS)
    return (y * w.astype(F32)).astype(x.dtype)

def l2norm(x):
    xf = x.astype(F32)
    return (xf * lax.rsqrt(jnp.sum(xf * xf, axis=-1, keepdims=True) + EPS)).astype(x.dtype)

def causal_conv(x, buf, w):
    k_w = w.shape[0]
    s = x.shape[1]
    xp = jnp.concatenate([buf.astype(x.dtype), x], axis=1)
    y = xp[:, 0:s] * w[0]
    for j in range(1, k_w):
        y = y + xp[:, j:j + s] * w[j]
    return y, xp[:, -(k_w - 1):]

def gated_delta_rule(q, k, v, beta, log_alpha, s0):
    bn, s, h, dk = q.shape
    dv = v.shape[-1]
    c = DN_CHUNK if s % DN_CHUNK == 0 else s
    n = s // c

    def chunks(t):
        t = t.astype(F32).reshape((bn, n, c, h) + t.shape[3:])
        return jnp.moveaxis(t, (1, 3), (0, 2))

    qc, kc, vc = chunks(q), chunks(k), chunks(v)
    bc, gc = chunks(beta), chunks(log_alpha)
    g = jnp.cumsum(gc, axis=-1)
    idx = jnp.arange(c)
    incl = idx[:, None] >= idx[None, :]
    strict = idx[:, None] > idx[None, :]
    decay = jnp.exp(jnp.where(incl, g[..., :, None] - g[..., None, :], -jnp.inf))
    kk = jnp.einsum('nbhid,nbhjd->nbhij', kc, kc)
    lower = jnp.eye(c, dtype=F32) + jnp.where(strict, bc[..., :, None] * decay * kk, 0.0)
    rhs = jnp.concatenate([bc[..., None] * vc, (bc * jnp.exp(g))[..., None] * kc], axis=-1)
    sol = lax.linalg.triangular_solve(lower, rhs, left_side=True, lower=True, unit_diagonal=True)
    u0, w = sol[..., :dv], sol[..., dv:]
    qk = decay * jnp.einsum('nbhid,nbhjd->nbhij', qc, kc)
    kdec = jnp.exp(g[..., -1:] - g)[..., None] * kc
    gend = jnp.exp(g[..., -1])

    def step(st, inp):
        u0_n, w_n, q_n, qk_n, kdec_n, g_n, gend_n = inp
        u = u0_n - jnp.einsum('bhcd,bhvd->bhcv', w_n, st)
        o = (jnp.exp(g_n)[..., None] * jnp.einsum('bhcd,bhvd->bhcv', q_n, st)
             + jnp.einsum('bhij,bhjv->bhiv', qk_n, u))
        st_new = gend_n[..., None, None] * st + jnp.einsum('bhcv,bhcd->bhvd', u, kdec_n)
        return st_new, o

    s_fin, o = lax.scan(step, s0.astype(F32), (u0, w, qc, qk, kdec, g, gend))
    o = jnp.moveaxis(o, (0, 2), (1, 3)).reshape(bn, s, h, dv)
    return o, s_fin

def _affine_combine(left, right):
    a1, b1 = left
    a2, b2 = right
    return a1 * a2, a2 * b1 + b2

def rg_lru(xc, h0, w_r, b_r, w_i, b_i, lam):
    bn, s, wd = xc.shape
    xf = xc.astype(F32)
    xb = xf.reshape(bn, s, LRU_BLOCKS, LRU_BW)
    r = jax.nn.sigmoid(jnp.einsum('bsne,nef->bsnf', xb, w_r.astype(F32)).reshape(bn, s, wd) + b_r)
    i = jax.nn.sigmoid(jnp.einsum('bsne,nef->bsnf', xb, w_i.astype(F32)).reshape(bn, s, wd) + b_i)
    log_a = -LRU_C * r * jax.nn.softplus(-lam.astype(F32))
    a = jnp.exp(log_a)
    bx = jnp.sqrt(-jnp.expm1(2.0 * log_a)) * (i * xf)
    a_cum, b_cum = lax.associative_scan(_affine_combine, (a, bx), axis=1)
    hseq = a_cum * h0.astype(F32)[:, None, :] + b_cum
    return hseq, hseq[:, -1]

def fox_block(q, cq, qpos, k, v, ck, kpos):
    sc = jnp.einsum('bqhd,bkhd->bhqk', q, k, preferred_element_type=F32) * (FOX_HD ** -0.5)
    sc = sc + jnp.swapaxes(cq, 1, 2)[..., :, None] - jnp.swapaxes(ck, 1, 2)[..., None, :]
    sc = jnp.where(kpos[None, :] <= qpos[:, None], sc, -jnp.inf)
    p = jax.nn.softmax(sc, axis=-1)
    return jnp.einsum('bhqk,bkhd->bqhd', p.astype(v.dtype), v)

def fox_sweep(q, cq, qpos, k, v, ck, kpos):
    bn, sq, h, hd = q.shape
    if sq % Q_BLOCK:
        return fox_block(q, cq, qpos, k, v, ck, kpos)
    nb = sq // Q_BLOCK
    qb = jnp.moveaxis(q.reshape(bn, nb, Q_BLOCK, h, hd), 1, 0)
    cqb = jnp.moveaxis(cq.reshape(bn, nb, Q_BLOCK, h), 1, 0)
    qposb = qpos.reshape(nb, Q_BLOCK)
    out = lax.map(lambda blk: fox_block(blk[0], blk[1], blk[2], k, v, ck, kpos), (qb, cqb, qposb))
    return jnp.moveaxis(out, 0, 1).reshape(bn, sq, h, hd)

def fox_prompt(q, k, v, logf):
    s = q.shape[1]
    c = jnp.cumsum(logf.astype(F32), axis=1)
    pos = jnp.arange(s)
    return fox_sweep(q, c, pos, k, v, c, pos)

def fox_sample(q, k, v, logf, cache_k_l, cache_v_l, cache_logf_l, page_table):
    bd, sn = q.shape[:2]
    past = page_table.shape[1] * cache_k_l.shape[1]
    kp = cache_k_l[page_table].reshape(bd, past, FOX_HEADS, FOX_HD).astype(k.dtype)
    vp = cache_v_l[page_table].reshape(bd, past, FOX_HEADS, FOX_HD).astype(v.dtype)
    lp = cache_logf_l[page_table].reshape(bd, past, FOX_HEADS).astype(F32)
    k_all = jnp.concatenate([kp, k], axis=1)
    v_all = jnp.concatenate([vp, v], axis=1)
    c = jnp.cumsum(jnp.concatenate([lp, logf.astype(F32)], axis=1), axis=1)
    kpos = jnp.arange(past + sn)
    qpos = past + jnp.arange(sn)
    return fox_sweep(q, c[:, past:], qpos, k_all, v_all, c, kpos)

def memory_kv(mem, mem_norm_w, w_mem_kv, mem_kn_w):
    bn, m, _ = mem.shape
    mn = rms_norm(mem, mem_norm_w)
    kv = jnp.einsum('bmd,de->bme', mn, w_mem_kv)
    mk, mv = jnp.split(kv, [MEM_HEADS * MEM_HD], axis=-1)
    mk = rms_norm(mk.reshape(bn, m, MEM_HEADS, MEM_HD), mem_kn_w)
    return mk, mv.reshape(bn, m, MEM_HEADS, MEM_HD)

def mem_attend(q, mk, mv):
    sc = jnp.einsum('bqhd,bmhd->bhqm', q, mk, preferred_element_type=F32) * (MEM_HD ** -0.5)
    p = jax.nn.softmax(sc, axis=-1)
    return jnp.einsum('bhqm,bmhd->bqhd', p.astype(mv.dtype), mv)

def hybrid_layer(x, lw, dn_s0, dn_buf0, lru_h0, lru_buf0, mem_k, mem_v, fox_attend):
    bn, s, _ = x.shape
    h = rms_norm(x, lw['norm_w'])
    proj = jnp.einsum('bsd,de->bse', h, lw['w_in']) + lw['b_in']
    (dn_qkv, dn_z, dn_b, dn_a, lru_x, lru_g, fq, fk, fv, ff, fg, mq, mg, mgate) = jnp.split(proj, IN_OFFSETS, axis=-1)

    qkv, dn_buf = causal_conv(dn_qkv, dn_buf0, lw['dn_conv_w'])
    qkv = jax.nn.silu(qkv)
    q, k, v = jnp.split(qkv, [DN_HEADS * DN_DK, 2 * DN_HEADS * DN_DK], axis=-1)
    q = l2norm(q.reshape(bn, s, DN_HEADS, DN_DK)) * (DN_DK ** -0.5)
    k = l2norm(k.reshape(bn, s, DN_HEADS, DN_DK))
    v = v.reshape(bn, s, DN_HEADS, DN_DV)
    beta = jax.nn.sigmoid(dn_b.astype(F32))
    log_alpha = -jnp.exp(lw['dn_A_log'].astype(F32)) * jax.nn.softplus(dn_a.astype(F32) + lw['dn_dt_bias'].astype(F32))
    o, dn_s = gated_delta_rule(q, k, v, beta, log_alpha, dn_s0)
    o = rms_norm(o, lw['dn_onorm_w']) * jax.nn.silu(dn_z.reshape(bn, s, DN_HEADS, DN_DV).astype(F32))
    out_a = o.reshape(bn, s, BR_WIDTH).astype(x.dtype)

    xc, lru_buf = causal_conv(lru_x, lru_buf0, lw['lru_conv_w'])
    hseq, lru_h = rg_lru(xc + lw['lru_conv_b'], lru_h0, lw['lru_w_r'], lw['lru_b_r'],
                         lw['lru_w_i'], lw['lru_b_i'], lw['lru_lambda'])
    out_b = (hseq * jax.nn.silu(lru_g.astype(F32))).astype(x.dtype)

    fq = rms_norm(fq.reshape(bn, s, FOX_HEADS, FOX_HD), lw['fox_qn_w'])
    fk = rms_norm(fk.reshape(bn, s, FOX_HEADS, FOX_HD), lw['fox_kn_w'])
    fv = fv.reshape(bn, s, FOX_HEADS, FOX_HD)
    logf = jax.nn.log_sigmoid(ff.astype(F32))
    o = fox_attend(fq, fk, fv, logf)
    out_c = (o.reshape(bn, s, BR_WIDTH) * jax.nn.silu(fg)).astype(x.dtype)

    mq = rms_norm(mq.reshape(bn, s, MEM_HEADS, MEM_HD), lw['mem_qn_w'])
    o = mem_attend(mq, mem_k, mem_v)
    out_m = (o.reshape(bn, s, BR_WIDTH) * jax.nn.silu(mg)).astype(x.dtype)

    branches = jnp.stack([out_a, out_b, out_c, out_m], axis=2)
    up = jnp.einsum('bsnw,nwd->bsnd', branches, lw['w_branch'])
    gates = jax.nn.sigmoid(mgate.reshape(bn, s, N_BRANCH, D_MODEL))
    merged = jnp.sum(gates * up, axis=2)
    y = x + jnp.einsum('bsd,de->bse', merged, lw['w_out'])
    return y, dn_s, dn_buf, lru_h, lru_buf, fk, fv, logf

def setup_inputs(seed: int = 0) -> dict:
    key = jax.random.key(seed)
    keys = jax.random.split(key, 48)
    kit = iter([keys[i] for i in range(48)])

    def nrm(shape, scale):
        return scale * jax.random.normal(next(kit), shape, F32)

    def gain(shape):
        return 1.0 + nrm(shape, 0.1)

    n_pages = PAST_LEN // PAGE_SIZE
    in_use = DEC_BATCH * n_pages
    n_pool = in_use + (in_use + 3) // 4
    page_table = jax.random.permutation(next(kit), n_pool)[:in_use].reshape(DEC_BATCH, n_pages).astype(jnp.int32)

    x_prompt = nrm((BATCH, SEQ, D_MODEL), 1.0)
    x_sample = nrm((DEC_BATCH, DEC_SEQ, D_MODEL), 1.0)
    mem_prompt = nrm((BATCH, MEM_TOKENS, D_MODEL), 1.0)

    cache_fox_k = nrm((DEPTH, n_pool, PAGE_SIZE, FOX_HEADS, FOX_HD), 1.0)
    cache_fox_v = nrm((DEPTH, n_pool, PAGE_SIZE, FOX_HEADS, FOX_HD), 1.0)
    cache_fox_logf = jax.nn.log_sigmoid(FOX_F_BIAS + nrm((DEPTH, n_pool, PAGE_SIZE, FOX_HEADS), 1.0))
    cache_mem_k = nrm((DEPTH, DEC_BATCH, MEM_TOKENS, MEM_HEADS, MEM_HD), 1.0)
    cache_mem_v = nrm((DEPTH, DEC_BATCH, MEM_TOKENS, MEM_HEADS, MEM_HD), 1.0)
    state_dn = nrm((DEPTH, DEC_BATCH, DN_HEADS, DN_DV, DN_DK), 0.5)
    state_dn_conv = nrm((DEPTH, DEC_BATCH, CONV_W - 1, DN_QKV), 1.0)
    state_lru_h = nrm((DEPTH, DEC_BATCH, LRU_WIDTH), 0.5)
    state_lru_conv = nrm((DEPTH, DEC_BATCH, CONV_W - 1, LRU_WIDTH), 1.0)

    norm_w = gain((DEPTH, D_MODEL))
    w_in = nrm((DEPTH, D_MODEL, N_IN), D_MODEL ** -0.5)
    b_in = nrm((DEPTH, N_IN), 0.02).at[:, FOX_F_OFF:FOX_F_OFF + FOX_HEADS].add(FOX_F_BIAS)
    dn_conv_w = nrm((DEPTH, CONV_W, DN_QKV), 0.5)
    dn_A_log = jnp.log(jax.random.uniform(next(kit), (DEPTH, DN_HEADS), F32, 1.0, 16.0))
    dt = jnp.exp(jax.random.uniform(next(kit), (DEPTH, DN_HEADS), F32, math.log(1e-3), math.log(1e-1)))
    dn_dt_bias = dt + jnp.log(-jnp.expm1(-dt))
    dn_onorm_w = gain((DEPTH, DN_DV))
    lru_conv_w = nrm((DEPTH, CONV_W, LRU_WIDTH), 0.5)
    lru_conv_b = nrm((DEPTH, LRU_WIDTH), 0.02)
    lru_w_r = nrm((DEPTH, LRU_BLOCKS, LRU_BW, LRU_BW), LRU_BW ** -0.5)
    lru_b_r = nrm((DEPTH, LRU_WIDTH), 0.02)
    lru_w_i = nrm((DEPTH, LRU_BLOCKS, LRU_BW, LRU_BW), LRU_BW ** -0.5)
    lru_b_i = nrm((DEPTH, LRU_WIDTH), 0.02)
    a_c = jax.random.uniform(next(kit), (DEPTH, LRU_WIDTH), F32, 0.9, 0.999)
    sig = a_c ** (1.0 / LRU_C)
    lru_lambda = jnp.log(sig) - jnp.log1p(-sig)
    fox_qn_w = gain((DEPTH, FOX_HD))
    fox_kn_w = gain((DEPTH, FOX_HD))
    mem_norm_w = gain((DEPTH, D_MODEL))
    w_mem_kv = nrm((DEPTH, D_MODEL, 2 * MEM_HEADS * MEM_HD), D_MODEL ** -0.5)
    mem_qn_w = gain((DEPTH, MEM_HD))
    mem_kn_w = gain((DEPTH, MEM_HD))
    w_branch = nrm((DEPTH, N_BRANCH, BR_WIDTH, D_MODEL), BR_WIDTH ** -0.5)
    w_out = nrm((DEPTH, D_MODEL, D_MODEL), D_MODEL ** -0.5)

    return {'x_prompt': x_prompt, 'x_sample': x_sample,
            'cache_fox_k': cache_fox_k, 'cache_fox_v': cache_fox_v, 'cache_fox_logf': cache_fox_logf,
            'cache_mem_k': cache_mem_k, 'cache_mem_v': cache_mem_v,
            'state_dn': state_dn, 'state_dn_conv': state_dn_conv,
            'state_lru_h': state_lru_h, 'state_lru_conv': state_lru_conv,
            'page_table': page_table, 'mem_prompt': mem_prompt,
            'norm_w': norm_w, 'w_in': w_in, 'b_in': b_in,
            'dn_conv_w': dn_conv_w, 'dn_A_log': dn_A_log, 'dn_dt_bias': dn_dt_bias, 'dn_onorm_w': dn_onorm_w,
            'lru_conv_w': lru_conv_w, 'lru_conv_b': lru_conv_b, 'lru_w_r': lru_w_r, 'lru_b_r': lru_b_r,
            'lru_w_i': lru_w_i, 'lru_b_i': lru_b_i, 'lru_lambda': lru_lambda,
            'fox_qn_w': fox_qn_w, 'fox_kn_w': fox_kn_w,
            'mem_norm_w': mem_norm_w, 'w_mem_kv': w_mem_kv, 'mem_qn_w': mem_qn_w, 'mem_kn_w': mem_kn_w,
            'w_branch': w_branch, 'w_out': w_out}

def reference(x_prompt, x_sample, cache_fox_k, cache_fox_v, cache_fox_logf, cache_mem_k, cache_mem_v,
              state_dn, state_dn_conv, state_lru_h, state_lru_conv, page_table, mem_prompt,
              norm_w, w_in, b_in, dn_conv_w, dn_A_log, dn_dt_bias, dn_onorm_w,
              lru_conv_w, lru_conv_b, lru_w_r, lru_b_r, lru_w_i, lru_b_i, lru_lambda,
              fox_qn_w, fox_kn_w, mem_norm_w, w_mem_kv, mem_qn_w, mem_kn_w, w_branch, w_out):
    bp = x_prompt.shape[0]
    yp, ys = x_prompt, x_sample
    names = ('fox_k', 'fox_v', 'fox_logf', 'mem_k', 'mem_v', 'dn', 'dn_conv', 'lru_h', 'lru_conv')
    accp = {n: [] for n in names}
    accs = {n: [] for n in names}
    for l in range(DEPTH):
        lw = {'norm_w': norm_w[l], 'w_in': w_in[l], 'b_in': b_in[l],
              'dn_conv_w': dn_conv_w[l], 'dn_A_log': dn_A_log[l], 'dn_dt_bias': dn_dt_bias[l],
              'dn_onorm_w': dn_onorm_w[l], 'lru_conv_w': lru_conv_w[l], 'lru_conv_b': lru_conv_b[l],
              'lru_w_r': lru_w_r[l], 'lru_b_r': lru_b_r[l], 'lru_w_i': lru_w_i[l], 'lru_b_i': lru_b_i[l],
              'lru_lambda': lru_lambda[l], 'fox_qn_w': fox_qn_w[l], 'fox_kn_w': fox_kn_w[l],
              'mem_qn_w': mem_qn_w[l], 'w_branch': w_branch[l], 'w_out': w_out[l]}

        mk, mv = memory_kv(mem_prompt, mem_norm_w[l], w_mem_kv[l], mem_kn_w[l])
        yp, dn_s, dn_b, lh, lb, fk, fv, lf = hybrid_layer(
            yp, lw,
            jnp.zeros((bp, DN_HEADS, DN_DV, DN_DK), F32),
            jnp.zeros((bp, CONV_W - 1, DN_QKV), x_prompt.dtype),
            jnp.zeros((bp, LRU_WIDTH), F32),
            jnp.zeros((bp, CONV_W - 1, LRU_WIDTH), x_prompt.dtype),
            mk, mv, fox_prompt)
        for n, val in zip(names, (fk, fv, lf, mk, mv, dn_s, dn_b, lh, lb)):
            accp[n].append(val)

        fox_fn = functools.partial(fox_sample, cache_k_l=cache_fox_k[l], cache_v_l=cache_fox_v[l],
                                   cache_logf_l=cache_fox_logf[l], page_table=page_table)
        ys, dn_s, dn_b, lh, lb, fk, fv, lf = hybrid_layer(
            ys, lw, state_dn[l], state_dn_conv[l], state_lru_h[l], state_lru_conv[l],
            cache_mem_k[l], cache_mem_v[l], fox_fn)
        for n, val in zip(('fox_k', 'fox_v', 'fox_logf', 'dn', 'dn_conv', 'lru_h', 'lru_conv'),
                          (fk, fv, lf, dn_s, dn_b, lh, lb)):
            accs[n].append(val)

    return (yp, ys,
            jnp.stack(accp['fox_k']), jnp.stack(accp['fox_v']), jnp.stack(accp['fox_logf']),
            jnp.stack(accp['mem_k']), jnp.stack(accp['mem_v']),
            jnp.stack(accp['dn']), jnp.stack(accp['dn_conv']),
            jnp.stack(accp['lru_h']), jnp.stack(accp['lru_conv']),
            jnp.stack(accs['fox_k']), jnp.stack(accs['fox_v']), jnp.stack(accs['fox_logf']),
            jnp.stack(accs['dn']), jnp.stack(accs['dn_conv']),
            jnp.stack(accs['lru_h']), jnp.stack(accs['lru_conv']))


_drawn_inputs = setup_inputs


def setup_inputs(seed=0):
    import zlib

    import numpy as np

    out = dict(_drawn_inputs(seed))
    spreads = {}
    factors = {'cache_fox_logf': 4.012,
     'lru_b_r': 8.0,
     'lru_b_i': 8.0,
     'fox_qn_w': 7.924,
     'mem_qn_w': 8.0}
    for name, (base, spread) in spreads.items():
        noise = np.random.default_rng([zlib.crc32(name.encode()), seed]).standard_normal(out[name].shape)
        drawn = base * np.exp(spread * noise) if base else spread * noise
        out[name] = __import__('jax').numpy.asarray(drawn.astype(out[name].dtype))
    for name, factor in factors.items():
        out[name] = (out[name] * factor).astype(out[name].dtype)
    return out
```

```python
from contextlib import ExitStack

import concourse.bass as bass
from concourse import mybir

F32 = mybir.dt.float32
F32R = mybir.dt.float32r
I32 = mybir.dt.int32
I8 = mybir.dt.int8
ALU = mybir.AluOpType
ACT = mybir.ActivationFunctionType
AX = mybir.AxisListType

P = 128
D = 1024
KD = D // P
SEQ = 1024
NB = 8
TOK = SEQ + NB
G3 = TOK // 3
TT8 = SEQ // P
H = 4
BW = 512
CONV = 4
CH = 128
NCH = SEQ // CH
MEM = 256
PAGES = 4
PAGE = 128
PAST = PAGES * PAGE
EPS = 1e-6
LRU_C = 8.0
SCALE = float(P) ** -0.5
NEG = -1e30
RSQRT_SEED = float(0x5F3759DF)

OFF = {}
_o = 0
for _n, _w in (("dn_qkv", 1536), ("dn_z", 512), ("dn_b", 4), ("dn_a", 4), ("lru_x", 512), ("lru_g", 512),
               ("fq", 512), ("fk", 512), ("fv", 512), ("ff", 4), ("fg", 512), ("mq", 512), ("mg", 512),
               ("gate", 4096)):
    OFF[_n] = _o
    _o += _w
BROW = {}
_r = 0
for _n, _w in (("dn_qkv", 12), ("dn_z", 4), ("lru_x", 4), ("lru_g", 4), ("fq", 4), ("fk", 4), ("fv", 4),
               ("fg", 4), ("mq", 4), ("mg", 4), ("gate", 32)):
    BROW[_n] = _r
    _r += _w
NBROW = _r
PROW = {}
_r = 0
for _n, _w in (("dn_conv_w", 48), ("lru_conv_w", 16), ("lru_conv_b", 4), ("lru_b_r", 4), ("lru_b_i", 4),
               ("lru_lambda", 4), ("fox_qn_w", 1), ("mem_qn_w", 1), ("dn_onorm_w", 1), ("norm_w", 8),
               ("mem_norm_w", 8)):
    PROW[_n] = _r
    _r += _w
NPROW = _r


class Steps:

    def __init__(self, eng, sem, state):
        self.eng, self.sem, self.state = eng, sem, state

    def step(self, ins):
        ins.then_inc(self.sem, 1)
        self.state[0] += 1

    def wait(self):
        self.eng.wait_ge(self.sem, self.state[0])

    def do(self, ins):
        self.step(ins)
        self.wait()


def heads(ap):
    return ap.rearrange("p (h d) -> p h d", h=H)


def rsqrt(v, x, y, t):
    eng = v.eng
    yi, yf = y.bitcast(I32), y
    v.do(eng.tensor_scalar(yi, x.bitcast(I32), 1, None, ALU.logical_shift_right))
    v.do(eng.tensor_scalar(yi, yi, -1.0, RSQRT_SEED, ALU.mult, ALU.add))
    for _ in range(3):
        v.do(eng.tensor_tensor(t, yf, yf, ALU.mult))
        v.do(eng.scalar_tensor_tensor(t, t, -0.5, x, ALU.mult, ALU.mult))
        v.do(eng.scalar_tensor_tensor(yf, t, 1.5, yf, ALU.add, ALU.mult))


def log1p_exp(v, z, u, s, s2, acc):
    eng = v.eng
    v.do(eng.tensor_scalar(s, u, 2.0, None, ALU.add))
    v.do(eng.reciprocal(s, s))
    v.do(eng.tensor_tensor(s, s, u, ALU.mult))
    v.do(eng.tensor_tensor(s2, s, s, ALU.mult))
    v.do(eng.tensor_scalar(acc, s2, 1.0 / 17, None, ALU.mult))
    for c in (15, 13, 11, 9, 7, 5, 3):
        v.do(eng.scalar_tensor_tensor(acc, acc, 1.0 / c, s2, ALU.add, ALU.mult))
    v.do(eng.scalar_tensor_tensor(acc, acc, 1.0, s, ALU.add, ALU.mult))
    v.do(eng.tensor_scalar(s, z, 0.0, None, ALU.max))
    v.do(eng.scalar_tensor_tensor(acc, acc, 2.0, s, ALU.mult, ALU.add))


class Kernel:

    def __init__(self, nc, ins, outs, ctx):
        self.nc, self.i, self.o, self.ctx = nc, ins, outs, ctx
        sb = lambda n, s, d=F32: ctx.enter_context(nc.sbuf_tensor(n, s, d))
        sem = lambda n: ctx.enter_context(nc.semaphore(n))
        self.hH, self.hL = sb("hH", [P, KD, TOK], F32R), sb("hL", [P, KD, TOK], F32R)
        self.raw = sb("w_raw", [P, 2, KD, P])
        self.wH, self.wL = sb("wH", [P, 2, KD, P], F32R), sb("wL", [P, 2, KD, P], F32R)
        self.ident = sb("ident", [P, P])
        self.ones = sb("ones", [P, 1])
        self.bias, self.hbias = sb("bias", [P, NBROW]), sb("half_bias", [P, NBROW])
        self.par, self.hpar = sb("par", [P, NPROW]), sb("half_par", [P, NPROW])
        self.TK = sb("token_scalars", [P, TT8, 3, H])
        self.knw, self.mknw = sb("fox_kn_bc", [P, P]), sb("mem_kn_bc", [P, P])
        self.qnw, self.mqnw = sb("fox_qn_bc", [P, P]), sb("mem_qn_bc", [P, P])
        self.alpha = sb("decode_alpha_beta", [P, 2, H, NB])
        self.convs = sb("conv_states", [P, 16, 32])
        self.ps = ctx.enter_context(nc.psum_tensor("ps", [P, 8, 512], F32))
        self.merged = sb("merged", [P, KD, TOK])
        self.OT_space = ExitStack()
        self.OT = self.OT_space.enter_context(nc.sbuf_tensor("branch_in", [P, H, TOK], F32))
        self.w_loaded = [sem("w_loaded0"), sem("w_loaded1")]
        self.w_hi, self.w_lo = sem("w_hi"), sem("w_lo")
        self.tile_done = sem("tile_done")
        self.evac_act, self.evac_dve = sem("evac_act"), sem("evac_dve")
        self.tiles = []
        self.at_load = self.at_hi = self.at_lo = 0
        self.v_sem, self.v_n = sem("vector_step"), [0]
        self.a_sem, self.a_n = sem("scalar_step"), [0]
        self.p_sem, self.p_n = sem("pool_step"), [0]
        self.stored, self.n_stored = sem("stored"), 0
        self.y_out = [sem("y_out0"), sem("y_out1")]
        self.stage = []

    def sem(self, name):
        s = self.nc.alloc_semaphore(name=name)
        self.stage.append(s)
        return s

    def stage_ends(self):
        self.nc.clear_and_free_semaphores(self.stage)
        self.nc.all_engine_barrier()
        self.stage = []

    def V(self, eng):
        return Steps(eng, self.v_sem, self.v_n)

    def A(self, eng):
        return Steps(eng, self.a_sem, self.a_n)

    def G(self, eng):
        return Steps(eng, self.p_sem, self.p_n)

    def store(self, eng, dst, src):
        eng.dma_start(dst, src).then_inc(self.stored, 16)
        self.n_stored += 16

    def plan(self, src, nk, evac):
        self.tiles.append((src, nk, evac))

    def plan_in(self, name, n, evac="act"):
        for t in range(n):
            a = OFF[name] + t * P
            self.plan(self.i["w_in"][0, :, a:a + P].rearrange("(k p) c -> p k c", p=P), KD, evac)

    def loads(self, sp, upto):
        for t in range(self.at_load, min(upto, len(self.tiles))):
            src, nk, _ = self.tiles[t]
            if t >= 2:
                sp.wait_ge(self.w_lo, t - 1)
            sp.dma_start(self.raw[:, t % 2, 0:nk], src).then_inc(self.w_loaded[t % 2], 16)
            self.at_load = t + 1

    def split_hi(self, act, upto):
        for t in range(self.at_hi, min(upto, len(self.tiles))):
            nk = self.tiles[t][1]
            act.wait_ge(self.w_loaded[t % 2], 16 * (t // 2 + 1))
            if t >= 2:
                act.wait_ge(self.tile_done, t - 1)
            act.activation(self.wH[:, t % 2, 0:nk], self.raw[:, t % 2, 0:nk], ACT.Identity).then_inc(self.w_hi, 1)
            self.at_hi = t + 1

    def split_lo(self, pool, upto):
        for t in range(self.at_lo, min(upto, len(self.tiles))):
            nk = self.tiles[t][1]
            pool.wait_ge(self.w_hi, t + 1)
            pool.tensor_tensor(self.wL[:, t % 2, 0:nk], self.raw[:, t % 2, 0:nk],
                               self.wH[:, t % 2, 0:nk].bitcast(F32), ALU.subtract).then_inc(self.w_lo, 1)
            self.at_lo = t + 1

    def psum(self, t):
        return self.ps[:, 3 * (t % 2):3 * (t % 2) + 3, 0:G3]

    def emptied(self, t):
        kind = self.tiles[t][2]
        n = sum(1 for x in self.tiles[:t + 1] if x[2] == kind)
        return (self.evac_act if kind == "act" else self.evac_dve), n

    def project(self, pe, t, xH, xL, groups=3, cols=None):
        _, nk, _ = self.tiles[t]
        pe.wait_ge(self.w_lo, t + 1)
        if t >= 2:
            pe.wait_ge(*self.emptied(t - 2))
        width = TOK // 3 if groups == 3 else cols
        for k in range(nk):
            for n, (w, x) in enumerate(((self.wH, xH), (self.wH, xL), (self.wL, xH))):
                for g in range(groups):
                    last = pe.matmul(self.ps[:, 3 * (t % 2) + g, 0:width], w[:, t % 2, k],
                                     x[:, k, g * width:(g + 1) * width],
                                     start=(k == 0 and n == 0), stop=(k == nk - 1 and n == 2))
        last.then_inc(self.tile_done, 1)


def setup(K):
    nc, i = K.nc, K.i
    with ExitStack() as c:
        sb = lambda n, s, d=F32: c.enter_context(nc.sbuf_tensor(n, s, d))
        X = sb("x_rows", [P, TT8 + 1, D])
        SQ = sb("x_square", [P, D])
        SS, RS, TM = sb("x_ss", [P, 9]), sb("x_rstd", [P, 9]), sb("x_tm", [P, 9])
        BR, PR = sb("bias_rows", [NBROW, P]), sb("par_rows", [NPROW, P])
        ST = sb("state_rows", [24, 1536])
        SL = sb("lru_state_rows", [32, 512])
        x_in, par_in = K.sem("x_in"), K.sem("par_in")
        made, squared, scaled = K.sem("constants_made"), K.sem("x_squared"), K.sem("x_scaled")
        tabT, tab = K.sem("tables_transposed"), K.sem("tables_ready")
        filled = K.sem("x_ss_filled")
        xT, hi, lo = K.sem("x_transposed"), K.sem("h_hi"), K.sem("h_lo")
        par_dmas = []

        def par(dst, src):
            par_dmas.append((dst, src))

        rows = lambda ap: ap.rearrange("(r p) -> r p", p=P)
        segments = [("dn_qkv", 16), ("lru_x", 20), ("fg", 4), ("mq", 40)]
        b = i["b_in"][0]
        for name, n in segments:
            par(BR[BROW[name]:BROW[name] + n, :], rows(b[OFF[name]:OFF[name] + n * P]))
        par(PR[PROW["dn_conv_w"]:PROW["dn_conv_w"] + 48, :], i["dn_conv_w"][0].rearrange("j (t p) -> (j t) p", p=P))
        par(PR[PROW["lru_conv_w"]:PROW["lru_conv_w"] + 16, :], i["lru_conv_w"][0].rearrange("j (t p) -> (j t) p", p=P))
        for name, n in (("lru_conv_b", 4), ("lru_b_r", 4), ("lru_b_i", 4), ("lru_lambda", 4), ("fox_qn_w", 1),
                        ("mem_qn_w", 1), ("dn_onorm_w", 1), ("norm_w", 8), ("mem_norm_w", 8)):
            par(PR[PROW[name]:PROW[name] + n, :], rows(i[name][0]))
        par(ST[:], i["state_dn_conv"][0].rearrange("b j c -> (b j) c"))
        par(SL[0:24, :], i["state_lru_conv"][0].rearrange("b j c -> (b j) c"))
        par(SL[24:32, :], i["state_lru_h"][0])
        for dst, name in ((K.knw, "fox_kn_w"), (K.mknw, "mem_kn_w"), (K.qnw, "fox_qn_w"), (K.mqnw, "mem_qn_w")):
            par(dst[:], i[name][0:1].broadcast_to([P, P]))

        with nc.Block(no_gpsimd_drain=True) as block:
            @block.sync
            def _(sp):
                for t in range(TT8):
                    sp.dma_start(X[:, t], i["x_prompt"][0, t * P:(t + 1) * P]).then_inc(x_in, 16)
                sp.dma_start(X[0:NB, TT8], i["x_sample"][:, 0]).then_inc(x_in, 16)
                K.loads(sp, 2)
                for src, dst in (("state_dn_conv", "dn_conv_s"), ("state_lru_conv", "lru_conv_s")):
                    K.store(sp, K.o[dst][0, :, 0:2], i[src][0, :, 1:3])

            @block.gpsimd
            def _(pool):
                pool.memset(K.ident[:], 0.0).then_inc(made, 1)
                pool.wait_ge(made, 1)
                pool.affine_select(out=K.ident[:], in_=K.ident[:], compare_op=ALU.not_equal, fill=1.0, base=0,
                                   pattern=[[-1, P]], channel_multiplier=1).then_inc(made, 1)
                pool.memset(K.ones[:], 1.0).then_inc(made, 1)
                K.split_lo(pool, 1)

            @block.scalar
            def _(act):
                for dst, src in par_dmas:
                    act.dma_start(dst, src).then_inc(par_in, 16)
                act.wait_ge(x_in, 16 * 9)
                act.wait_ge(filled, 1)
                a = K.A(act)
                for t in range(9):
                    n = P if t < TT8 else NB
                    act.activation(SQ[0:n], X[0:n, t], ACT.Square, accum_out=SS[0:n, t:t + 1]).then_inc(squared, 1)
                    act.wait_ge(squared, t + 1)
                K.split_hi(act, 1)
                act.wait_ge(tabT, 1)
                a.do(act.activation(K.bias[:], K.ps[:, 6, 0:NBROW], ACT.Identity))
                a.do(act.activation(K.par[:], K.ps[:, 6, 128:128 + NPROW], ACT.Identity))
                act.activation(K.hbias[:], K.bias[:], ACT.Identity, scale=0.5).then_inc(tab, 1)
                act.activation(K.hpar[:], K.par[:], ACT.Identity, scale=0.5).then_inc(tab, 1)
                act.activation(K.convs[:, 0:12, 0:24], K.ps[:, 7, 0:12 * 24].rearrange("p (t r) -> p t r", t=12),
                               ACT.Identity).then_inc(tab, 1)
                act.activation(K.convs[:, 12:16, :], K.ps[:, 7, 288:288 + 128].rearrange("p (t r) -> p t r", t=4),
                               ACT.Identity).then_inc(tab, 1)
                for k in range(KD):
                    q = 3 * (k % 2)
                    act.wait_ge(xT, k + 1)
                    w = K.par[:, PROW["norm_w"] + k:PROW["norm_w"] + k + 1]
                    act.activation(K.hH[:, k, 0:SEQ].rearrange("p (a b) -> p a b", a=2), K.ps[:, q:q + 2, :],
                                   ACT.Identity, scale=w)
                    act.activation(K.hH[:, k, SEQ:TOK], K.ps[:, q + 2, 0:NB], ACT.Identity, scale=w).then_inc(hi, 1)

            @block.vector
            def _(dve):
                v = K.V(dve)
                dve.memset(SS[:], 1.0).then_inc(filled, 1)
                dve.wait_ge(squared, 9)
                v.do(dve.tensor_scalar(SS[:], SS[:], 1.0 / D, EPS, ALU.mult, ALU.add))
                rsqrt(v, SS[:], RS[:], TM[:])
                for t in range(9):
                    n = P if t < TT8 else NB
                    dve.tensor_scalar(X[0:n, t], X[0:n, t], RS[0:n, t:t + 1], None, ALU.mult).then_inc(scaled, 1)
                for k in range(KD):
                    q = 3 * (k % 2)
                    dve.wait_ge(hi, k + 1)
                    w = K.par[:, PROW["norm_w"] + k:PROW["norm_w"] + k + 1]
                    dve.scalar_tensor_tensor(
                        K.hL[:, k, 0:SEQ].rearrange("p (a b) -> p a b", a=2), K.ps[:, q:q + 2, :], w,
                        K.hH[:, k, 0:SEQ].bitcast(F32).rearrange("p (a b) -> p a b", a=2), ALU.mult, ALU.subtract)
                    dve.scalar_tensor_tensor(K.hL[:, k, SEQ:TOK], K.ps[:, q + 2, 0:NB], w,
                                             K.hH[:, k, SEQ:TOK].bitcast(F32), ALU.mult,
                                             ALU.subtract).then_inc(lo, 1)

            @block.tensor
            def _(pe):
                pe.wait_ge(made, 3)
                pe.wait_ge(par_in, 16 * len(par_dmas))
                pe.transpose(K.ps[:, 6, 0:NBROW], BR[:], K.ident[0:NBROW, 0:NBROW])
                pe.transpose(K.ps[:, 6, 128:128 + NPROW], PR[:], K.ident[0:NPROW, 0:NPROW])
                for t in range(12):
                    pe.transpose(K.ps[:, 7, 24 * t:24 * t + 24], ST[:, t * P:(t + 1) * P], K.ident[0:24, 0:24])
                for t in range(4):
                    last = pe.transpose(K.ps[:, 7, 288 + 32 * t:320 + 32 * t], SL[:, t * P:(t + 1) * P],
                                        K.ident[0:32, 0:32])
                last.then_inc(tabT, 1)
                pe.wait_ge(scaled, 9)
                for k in range(KD):
                    q = 3 * (k % 2)
                    if k >= 2:
                        pe.wait_ge(lo, k - 1)
                    for t in range(TT8):
                        pe.transpose(K.ps[:, q + t // 4, (t % 4) * P:(t % 4 + 1) * P], X[:, t, k * P:(k + 1) * P],
                                     K.ident[:])
                    pe.transpose(K.ps[:, q + 2, 0:NB], X[0:NB, TT8, k * P:(k + 1) * P],
                                 K.ident[0:NB, 0:NB]).then_inc(xT, 1)


def small_columns(K):
    nc, i = K.nc, K.i
    DNA, FF, DNB = 0, 32, 64
    M = 96
    with ExitStack() as c:
        sb = lambda n, s, d=F32: c.enter_context(nc.sbuf_tensor(n, s, d))
        W = sb("sw", [P, KD, M])
        WH, WL = sb("swH", [P, KD, M], F32R), sb("swL", [P, KD, M], F32R)
        col = sb("sw_cols", [M, 8])
        Z, T1, U, S, S2, SP = (sb(n, [M, TOK]) for n in ("sz", "st1", "su", "ss", "ss2", "ssp"))
        SC, MK = sb("s_scan", [M, SEQ]), sb("s_mask", [M, SEQ])
        EX = sb("s_exp", [M, NB])
        VT = sb("s_value_rows", [P, TT8 + 1, M])
        loaded, prep, split = K.sem("sw_loaded"), K.sem("sw_prepared"), K.sem("sw_split")
        done, z, t1, u = K.sem("sw_done"), K.sem("sz_ready"), K.sem("st1_ready"), K.sem("su_ready")
        val, beta, tr, out = K.sem("s_values"), K.sem("s_beta"), K.sem("s_transposed"), K.sem("s_out")
        K.rows_out = K.sem("rows_out")
        with nc.Block(no_gpsimd_drain=True) as block:
            @block.gpsimd
            def _(pool):
                g = K.G(pool)
                pool.memset(W[:], 0.0)
                pool.memset(col[:], 0.0)
                pool.memset(MK[:], 1.0).then_inc(prep, 1)
                pool.wait_ge(prep, 1)
                pool.memset(MK[0:32].rearrange("p (a b) -> p a b", b=CH)[:, :, 0:1], 0.0)
                pool.memset(col[0:32, 3:4], 1.0)
                pool.memset(col[32:64, 3:4], -1.0)
                pool.memset(col[64:96, 3:4], -1.0).then_inc(prep, 1)

            @block.sync
            def _(sp):
                sp.wait_ge(prep, 2)
                for name, r in (("dn_a", DNA), ("ff", FF), ("dn_b", DNB)):
                    a = OFF[name]
                    sp.dma_start(W[:, :, r:r + 4], i["w_in"][0, :, a:a + 4].rearrange("(k p) c -> p k c", p=P)
                                 ).then_inc(loaded, 16)
                    sp.dma_start(col[r:r + 4, 0:1], i["b_in"][0, a:a + 4].rearrange("(c a) -> c a", a=1)
                                 ).then_inc(loaded, 16)
                sp.dma_start(col[0:4, 1:2], i["dn_dt_bias"][0].rearrange("(c a) -> c a", a=1)).then_inc(loaded, 16)
                sp.dma_start(col[0:4, 2:3], i["dn_A_log"][0].rearrange("(c a) -> c a", a=1)).then_inc(loaded, 16)
                sp.wait_ge(out, 1)
                for t in range(TT8):
                    K.store(sp, K.o["fox_logf"][0, 0, t * P:(t + 1) * P], VT[:, t, FF:FF + 4])
                K.store(sp, K.o["fox_logf_s"][0, :, 0], VT[0:NB, TT8, FF:FF + 4])
                sp.dma_start(K.d_rows[0], SC[DNA:DNA + 4]).then_inc(K.rows_out, 16)
                sp.dma_start(K.d_rows[1], SC[FF:FF + 4]).then_inc(K.rows_out, 16)
                sp.dma_start(K.d_rows[2], SC[DNB:DNB + 4]).then_inc(K.rows_out, 16)
                sp.dma_start(K.d_ab[0], EX[DNA:DNA + 4]).then_inc(K.rows_out, 16)
                sp.dma_start(K.d_ab[1], EX[DNB:DNB + 4]).then_inc(K.rows_out, 16)
                sp.dma_start(K.d_lf, VT[0:NB, TT8, FF:FF + 4]).then_inc(K.rows_out, 16)
                sp.wait_ge(K.rows_out, 96)
                sp.dma_start(K.alpha[:].rearrange("p a h b -> p (a h b)"),
                             K.d_ab.rearrange("a h b -> (a h b)").unsqueeze(0).broadcast_to([P, 64])
                             ).then_inc(K.rows_out, 16)
                sp.wait_ge(K.rows_out, 112)
                sp.wait_ge(K.stored, K.n_stored)
                K.loads(sp, 2)

            @block.scalar
            def _(act):
                a = K.A(act)
                act.wait_ge(loaded, 16 * 8)
                a.do(act.activation(WH[:], W[:], ACT.Identity))
                act.activation(col[:, 5:6], col[:, 2:3], ACT.Exp).then_inc(split, 1)
                act.wait_ge(done, 1)
                act.wait_ge(split, 3)
                act.activation(Z[:].rearrange("p (a b) -> p a b", a=3), K.ps[0:M, 0:3, 0:G3], ACT.Identity,
                               scale=col[:, 3:4], bias=col[:, 4:5]).then_inc(z, 1)
                act.wait_ge(t1, 1)
                act.activation(U[:], T1[:], ACT.Exp).then_inc(u, 1)
                act.wait_ge(val, 2)
                act.activation(SC[DNB:DNB + 32], SP[DNB:DNB + 32, 0:SEQ], ACT.Exp)
                act.activation(EX[:], SP[:, SEQ:TOK], ACT.Exp).then_inc(beta, 1)
                act.wait_ge(tr, 1)
                for t in range(TT8):
                    act.activation(K.TK[:, t], K.ps[:, t // 4, (t % 4) * M:(t % 4 + 1) * M].rearrange(
                        "p (g m) -> p g m", g=3)[:, :, 0:H], ACT.Identity)
                act.activation(VT[:, 0:TT8].rearrange("p (a b) m -> p a b m", a=2),
                               K.ps[:, 2:4, 0:4 * M].rearrange("p a (b m) -> p a b m", m=M), ACT.Identity)
                act.activation(VT[0:NB, TT8], K.ps[0:NB, 4, 0:M], ACT.Identity).then_inc(out, 1)

            @block.vector
            def _(dve):
                v = K.V(dve)
                dve.wait_ge(split, 1)
                dve.tensor_tensor(WL[:], W[:], WH[:].bitcast(F32), ALU.subtract).then_inc(split, 1)
                v.do(dve.scalar_tensor_tensor(col[:, 4:5], col[:, 0:1], col[:, 3:4], col[:, 1:2], ALU.mult, ALU.add))
                dve.tensor_scalar(col[:, 5:6], col[:, 5:6], -1.0, None, ALU.mult).then_inc(split, 1)
                dve.wait_ge(split, 3)
                dve.wait_ge(z, 1)
                v.do(dve.tensor_scalar(T1[:], Z[:], -1.0, None, ALU.mult))
                dve.tensor_tensor(T1[:], T1[:], Z[:], ALU.min).then_inc(t1, 1)
                dve.wait_ge(u, 1)
                log1p_exp(v, Z[:], U[:], S[:], S2[:], SP[:])
                dve.tensor_scalar(SP[:], SP[:], col[:, 5:6], None, ALU.mult).then_inc(val, 1)
                dve.wait_ge(val, 1)
                dve.tensor_tensor_scan(SC[:], MK[:], SP[:, 0:SEQ], 0.0, ALU.mult, ALU.add).then_inc(val, 1)

            @block.tensor
            def _(pe):
                pe.wait_ge(split, 2)
                for k in range(KD):
                    for n, (w, x) in enumerate(((WH, K.hH), (WH, K.hL), (WL, K.hH))):
                        for g in range(3):
                            last = pe.matmul(K.ps[0:M, g, 0:G3], w[:, k], x[:, k, g * G3:(g + 1) * G3],
                                             start=(k == 0 and n == 0), stop=(k == KD - 1 and n == 2))
                last.then_inc(done, 1)
                pe.wait_ge(beta, 1)
                for t in range(TT8):
                    pe.transpose(K.ps[:, t // 4, (t % 4) * M:(t % 4 + 1) * M], SC[:, t * P:(t + 1) * P],
                                 K.ident[0:M, 0:M])
                    pe.transpose(K.ps[:, 2 + t // 4, (t % 4) * M:(t % 4 + 1) * M], SP[:, t * P:(t + 1) * P],
                                 K.ident[0:M, 0:M])
                pe.transpose(K.ps[0:NB, 4, 0:M], SP[:, SEQ:TOK], K.ident[0:M, 0:M]).then_inc(tr, 1)


def conv_tiles(K, t0, n, name, state0, par, silu, OUT, tag, prompt_out, sample_out):
    nc = K.nc
    PAD = CONV - 1
    taps = PROW[name]
    with ExitStack() as c:
        sb = lambda n_, s, d=F32: c.enter_context(nc.sbuf_tensor(tag + n_, s, d))
        XI = sb("_in", [P, 2, PAD + TOK])
        TH = sb("_th", [P, 2, TOK]) if silu else None
        XL = sb("_last", [P, n, PAD + NB])
        XR = sb("_last_rows", [PAD + NB, n * P])
        padded, conv, th, fin = (K.sem(tag + x) for x in ("_padded", "_conv", "_tanh", "_silu"))
        last_cols, last_tr, last_ev = (K.sem(tag + x) for x in ("_lastc", "_lastt", "_laste"))

        def tap(j, t):
            return par[:, taps + j * n + t:taps + j * n + t + 1]

        with nc.Block(no_gpsimd_drain=True) as block:
            @block.sync
            def _(sp):
                K.loads(sp, t0 + n + 2)
                sp.wait_ge(last_ev, 1)
                K.store(sp, K.o[prompt_out][0, 0], XR[0:PAD])
                K.store(sp, K.o[sample_out][0, :, 2], XR[PAD:PAD + NB])
                sp.wait_ge(K.stored, K.n_stored)

            @block.gpsimd
            def _(pool):
                pool.memset(XI[:, :, 0:PAD], 0.0).then_inc(padded, 1)
                K.split_lo(pool, t0 + n + 1)

            @block.scalar
            def _(act):
                for j in range(n + 1):
                    if j < n:
                        t = t0 + j
                        K.split_hi(act, t + 2)
                        act.wait_ge(K.tile_done, t + 1)
                        if j >= 2:
                            act.wait_ge(conv, j - 1)
                        b = BROW[CONV_OF[name]] + j
                        act.activation(XI[:, j % 2, PAD:].rearrange("p (a b) -> p a b", a=3), K.psum(t), ACT.Identity,
                                       bias=K.bias[:, b:b + 1]).then_inc(K.evac_act, 1)
                    if silu and j >= 1:
                        act.wait_ge(conv, j)
                        if j >= 3:
                            act.wait_ge(fin, j - 2)
                        act.activation(TH[:, (j - 1) % 2], OUT(j - 1), ACT.Tanh).then_inc(th, 1)
                act.wait_ge(last_tr, 1)
                act.activation(XR[:].rearrange("p (a b) -> p a b", b=512),
                               K.ps[0:PAD + NB, 0:n // 4, :], ACT.Identity).then_inc(last_ev, 1)

            @block.vector
            def _(dve):
                v = K.V(dve)
                dve.wait_ge(padded, 1)
                for j in range(n + 1):
                    if j < n:
                        dve.wait_ge(*K.emptied(t0 + j))
                        x, y = XI[:, j % 2], OUT(j)[:, 0:SEQ]
                        xs, ys = XI[:, j % 2, PAD + SEQ:], OUT(j)[:, SEQ:TOK]
                        st = K.convs[:, state0 + j, 0:24].rearrange("p (b j) -> p j b", j=PAD)
                        if silu:
                            v.step(dve.tensor_scalar(y, x[:, PAD:PAD + SEQ], tap(3, j), None, ALU.mult))
                            v.step(dve.tensor_scalar(ys, xs, tap(3, j), None, ALU.mult))
                        else:
                            cb = K.par[:, PROW["lru_conv_b"] + j:PROW["lru_conv_b"] + j + 1]
                            v.step(dve.tensor_scalar(y, x[:, PAD:PAD + SEQ], tap(3, j), cb, ALU.mult, ALU.add))
                            v.step(dve.tensor_scalar(ys, xs, tap(3, j), cb, ALU.mult, ALU.add))
                        v.step(dve.tensor_copy(XL[:, j], x[:, SEQ:SEQ + PAD + NB]))
                        for k in range(PAD):
                            v.wait()
                            v.step(dve.scalar_tensor_tensor(y, x[:, k:k + SEQ], tap(k, j), y, ALU.mult, ALU.add))
                            ins = dve.scalar_tensor_tensor(ys, st[:, k], tap(k, j), ys, ALU.mult, ALU.add)
                            if k == PAD - 1:
                                ins.then_inc(conv, 1)
                            else:
                                v.step(ins)
                    if silu and j >= 1:
                        dve.wait_ge(th, j)
                        dve.scalar_tensor_tensor(OUT(j - 1), TH[:, (j - 1) % 2], 1.0, OUT(j - 1), ALU.add,
                                                 ALU.mult).then_inc(fin, 1)
                if not silu:
                    dve.wait_ge(conv, n)

            @block.tensor
            def _(pe):
                for j in range(n):
                    K.project(pe, t0 + j, K.hH, K.hL)
                pe.wait_ge(conv, n)
                pe.wait_ge(*K.emptied(t0 + n - 1))
                for j in range(n):
                    last = pe.transpose(K.ps[0:PAD + NB, j // 4, (j % 4) * P:(j % 4 + 1) * P], XL[:, j], K.ident[:])
                last.then_inc(last_tr, 1)


CONV_OF = {"dn_conv_w": "dn_qkv", "lru_conv_w": "lru_x"}


def gate_branch(K, t0, name, OT, tag):
    nc = K.nc
    with ExitStack() as c:
        sb = lambda n_, s, d=F32: c.enter_context(nc.sbuf_tensor(tag + n_, s, d))
        G, TH = sb("_gx", [P, 2, TOK]), sb("_gth", [P, 2, TOK])
        th, prod, hi = K.sem(tag + "_gth"), K.sem(tag + "_gprod"), K.sem(tag + "_ghi")
        with nc.Block(no_gpsimd_drain=True) as block:
            @block.sync
            def _(sp):
                K.loads(sp, t0 + 4 + 2)

            @block.gpsimd
            def _(pool):
                K.split_lo(pool, t0 + 4 + 1)

            @block.scalar
            def _(act):
                for j in range(5):
                    if j < 4:
                        t = t0 + j
                        K.split_hi(act, t + 2)
                        act.wait_ge(K.tile_done, t + 1)
                        if j >= 2:
                            act.wait_ge(prod, j - 1)
                        b = BROW[name] + j
                        act.activation(G[:, j % 2].rearrange("p (a b) -> p a b", a=3), K.psum(t), ACT.Identity,
                                       scale=0.5, bias=K.hbias[:, b:b + 1]).then_inc(K.evac_act, 1)
                        act.wait_ge(*K.emptied(t))
                        act.activation(TH[:, j % 2], G[:, j % 2], ACT.Tanh).then_inc(th, 1)
                    if j >= 1:
                        act.wait_ge(prod, j)
                        act.activation(K.brH[:, j - 1], OT[:, j - 1], ACT.Identity).then_inc(hi, 1)

            @block.vector
            def _(dve):
                v = K.V(dve)
                for j in range(5):
                    if j < 4:
                        dve.wait_ge(th, j + 1)
                        v.do(dve.scalar_tensor_tensor(G[:, j % 2], TH[:, j % 2], 1.0, G[:, j % 2], ALU.add, ALU.mult))
                        dve.tensor_tensor(OT[:, j], G[:, j % 2], OT[:, j], ALU.mult).then_inc(prod, 1)
                    if j >= 1:
                        dve.wait_ge(hi, j)
                        dve.wait_ge(prod, j)
                        v.step(dve.tensor_tensor(K.brL[:, j - 1], OT[:, j - 1], K.brH[:, j - 1].bitcast(F32),
                                                 ALU.subtract))

            @block.tensor
            def _(pe):
                for j in range(4):
                    K.project(pe, t0 + j, K.hH, K.hL)


def merge_branch(K, t0, n):
    nc = K.nc
    with ExitStack() as c:
        sb = lambda n_, s, d=F32: c.enter_context(nc.sbuf_tensor(f"m{n}" + n_, s, d))
        TH, TM = sb("_th", [P, 2, TOK]), sb("_tm", [P, 2, TOK])
        with nc.Block(no_gpsimd_drain=True) as block:
            @block.sync
            def _(sp):
                K.loads(sp, t0 + 16 + 2)

            @block.gpsimd
            def _(pool):
                K.split_lo(pool, t0 + (16 if n == 3 else 17))

            @block.scalar
            def _(act):
                for d in range(KD):
                    t = t0 + 2 * d
                    K.split_hi(act, t + 2)
                    act.wait_ge(K.tile_done, t + 1)
                    if d >= 2:
                        act.wait_ge(*K.emptied(t - 3))
                    b = BROW["gate"] + KD * n + d
                    act.activation(TH[:, d % 2].rearrange("p (a b) -> p a b", a=3), K.psum(t), ACT.Tanh,
                                   scale=0.5, bias=K.hbias[:, b:b + 1]).then_inc(K.evac_act, 1)
                    K.split_hi(act, min(t + 3, t0 + 16 if n == 3 else t + 3))

            @block.vector
            def _(dve):
                v = K.V(dve)
                for d in range(KD):
                    t = t0 + 2 * d
                    dve.wait_ge(*K.emptied(t))
                    dve.wait_ge(K.tile_done, t + 2)
                    o = K.merged[:, d] if n == 0 else TM[:, d % 2]
                    dve.scalar_tensor_tensor(o.rearrange("p (a b) -> p a b", a=3),
                                             TH[:, d % 2].rearrange("p (a b) -> p a b", a=3), 1.0, K.psum(t + 1),
                                             ALU.add, ALU.mult).then_inc(K.evac_dve, 1)
                    if n:
                        dve.wait_ge(*K.emptied(t + 1))
                        v.step(dve.tensor_tensor(K.merged[:, d], K.merged[:, d], o, ALU.add))

            @block.tensor
            def _(pe):
                for d in range(KD):
                    K.project(pe, t0 + 2 * d, K.hH, K.hL)
                    K.project(pe, t0 + 2 * d + 1, K.brH, K.brL)


def output(K, t0):
    nc, i = K.nc, K.i
    NE = D // P
    with ExitStack() as c:
        sb = lambda n_, s, d=F32: c.enter_context(nc.sbuf_tensor("o" + n_, s, d))
        WH, WL = sb("_wH", [P, KD, D], F32R), sb("_wL", [P, KD, D], F32R)
        X = sb("_x", [P, 2, D])
        x_in = [K.sem("ox_in0"), K.sem("ox_in1")]
        y_out = K.y_out
        hi, lo, done, y = K.sem("m_hi"), K.sem("m_lo"), K.sem("o_done"), K.sem("y_ready")
        with nc.Block(no_gpsimd_drain=True) as block:
            @block.sync
            def _(sp):
                K.loads(sp, len(K.tiles))
                for t in range(TT8 + 1):
                    if t >= 2:
                        sp.wait_ge(y_out[t % 2], 16 * (t // 2))
                    if t < TT8:
                        sp.dma_start(X[:, t % 2], i["x_prompt"][0, t * P:(t + 1) * P]).then_inc(x_in[t % 2], 16)
                    else:
                        sp.dma_start(X[0:NB, t % 2], i["x_sample"][:, 0]).then_inc(x_in[t % 2], 16)
                    if t >= 1:
                        s = t - 1
                        sp.wait_ge(y, s + 1)
                        sp.dma_start(K.o["y"][0, s * P:(s + 1) * P], X[:, s % 2]).then_inc(y_out[s % 2], 16)
                sp.wait_ge(y, TT8 + 1)
                sp.dma_start(K.o["y_s"][:, 0], X[0:NB, TT8 % 2]).then_inc(y_out[TT8 % 2], 16)
                sp.wait_ge(y_out[0], 16 * 5)
                sp.wait_ge(y_out[1], 16 * 4)
                sp.wait_ge(K.stored, K.n_stored)

            @block.gpsimd
            def _(pool):
                for e in range(NE):
                    t = t0 + e
                    pool.wait_ge(K.w_hi, t + 1)
                    pool.tensor_tensor(WL[:, :, e * P:(e + 1) * P], K.raw[:, t % 2],
                                       WH[:, :, e * P:(e + 1) * P].bitcast(F32), ALU.subtract).then_inc(K.w_lo, 1)

            @block.scalar
            def _(act):
                for k in range(KD):
                    act.activation(K.hH[:, k], K.merged[:, k], ACT.Identity, scale=0.5).then_inc(hi, 1)
                    e, t = k, t0 + k
                    act.wait_ge(K.w_loaded[t % 2], 16 * (t // 2 + 1))
                    act.activation(WH[:, :, e * P:(e + 1) * P], K.raw[:, t % 2], ACT.Identity).then_inc(K.w_hi, 1)

            @block.vector
            def _(dve):
                for k in range(KD):
                    dve.wait_ge(hi, k + 1)
                    dve.scalar_tensor_tensor(K.hL[:, k], K.merged[:, k], 0.5, K.hH[:, k].bitcast(F32), ALU.mult,
                                             ALU.subtract).then_inc(lo, 1)
                for t in range(TT8 + 1):
                    n = P if t < TT8 else NB
                    dve.wait_ge(x_in[t % 2], 16 * (t // 2 + 1))
                    dve.wait_ge(done, t + 1)
                    q = 2 * (t % 4)
                    dve.tensor_tensor(X[0:n, t % 2].rearrange("p (a b) -> p a b", a=2), K.ps[0:n, q:q + 2, :],
                                      X[0:n, t % 2].rearrange("p (a b) -> p a b", a=2), ALU.add).then_inc(y, 1)

            @block.tensor
            def _(pe):
                pe.wait_ge(lo, KD)
                pe.wait_ge(K.w_lo, t0 + NE)
                for t in range(TT8 + 1):
                    n = P if t < TT8 else NB
                    if t >= 4:
                        pe.wait_ge(y, t - 3)
                    q = 2 * (t % 4)
                    for k in range(KD):
                        for m, (x, w) in enumerate(((K.hH, WH), (K.hH, WL), (K.hL, WH))):
                            for e in range(2):
                                last = pe.matmul(K.ps[0:n, q + e, :], x[:, k, t * P:t * P + n],
                                                 w[:, k, 512 * e:512 * (e + 1)], start=(k == 0 and m == 0),
                                                 stop=(k == KD - 1 and m == 2))
                    last.then_inc(done, 1)


def level_masks(K, pool, LO, UP, made):
    n = 0
    for l in range(7):
        s = 1 << l
        for M in (LO, UP):
            pool.memset(M[:, l], 0).then_inc(made, 1)
            n += 1
            pool.wait_ge(made, n)
            lower = M is LO
            v = M[:, l].rearrange("p (b r) -> p b r", r=2 * s)
            v = v[:, :, 0:s] if lower else v[:, :, s:2 * s]
            pool.memset(v, 1).then_inc(made, 1)
            n += 1
            for base, mul in (((-s, 1), (2 * s - 1, -1)) if lower else ((0, 1), (s - 1, -1))):
                pool.wait_ge(made, n)
                pool.affine_select(out=v, in_=v, compare_op=ALU.is_ge, fill=0, base=base,
                                   pattern=[[-2 * s * mul, P // (2 * s)], [0, s]], channel_multiplier=mul
                                   ).then_inc(made, 1)
                n += 1
    return n


def delta_rule(K):
    nc = K.nc
    with ExitStack() as c:
        sb = lambda n_, s, d=F32: c.enter_context(nc.sbuf_tensor("d" + n_, s, d))
        hs = lambda n_: sb(n_, [P, H, P])
        two = lambda n_: [sb(n_ + str(q), [P, H, P]) for q in range(2)]
        LO, UP = sb("_lo", [P, 7, P], I8), sb("_up", [P, 7, P], I8)
        NEGM, STR = sb("_negm", [P, P]), sb("_strict", [P, P])
        SS, RN, TM = sb("_ss", [P, 2 * H]), sb("_rn", [P, 2 * H]), sb("_tm", [P, 2 * H])
        GC = sb("_gc", [P, 2, H, P])
        SC = sb("_sc", [P, 4, H])
        GE = sb("_ge", [P, 2, H])
        KN, QN, KT, QT, DT, W = hs("_kn"), hs("_qn"), hs("_kT"), hs("_qT"), hs("_dT"), hs("_w")
        VB, KBG, KD_, QG, QKT = two("_vb"), two("_kbg"), two("_kdec"), two("_qgT"), two("_qkT")
        X, Y, NU = two("_X"), two("_Y"), two("_NU")
        M1s = sb("_M1", [P, 2, H, P])
        M1 = [M1s[:, q] for q in range(2)]
        SQ = M1s[:].rearrange("p a h d -> p (a h) d")
        NWT, U, STG = KN, QN, DT
        ST = hs("_state")
        OS, OR, OM = sb("_os", [P, H]), sb("_or", [P, H]), sb("_om", [P, H])
        qkv = lambda r, h, cols: K.OT[:, h, cols] if r == 0 else K.merged[:, (r - 1) * H + h, cols]
        OT = K.OT
        made = K.sem("dn_masks")
        S = {n_: K.sem("dn_" + n_) for n_ in
             ("rows_in", "tok", "square", "scaled", "back", "backed", "gram", "nu", "diff", "decay", "w", "pool",
              "unit", "first", "firsted", "m1", "m1e", "dxy", "upd", "wT", "wTe", "u", "ue", "o", "osq", "on",
              "oT", "oTe", "ds", "state", "stg", "ge", "fin", "fine", "kd")}
        B = [K.ps[:, b].rearrange("p (h d) -> p h d", h=H) for b in range(8)]
        tokv = lambda ch, r: K.TK[:, ch, r]
        bc = lambda ap: ap.unsqueeze(2).broadcast_to([P, H, P])
        mb = lambda ap: ap.unsqueeze(1).broadcast_to([P, H, P])

        with nc.Block(no_gpsimd_drain=True) as block:
            @block.sync
            def _(sp):
                for ch in range(NCH):
                    if ch >= 1:
                        sp.wait_ge(S["pool"], ch)
                        sp.wait_ge(S["ge"], ch)
                    for q, r in ((0, 0), (1, 2)):
                        sp.dma_start(GC[:, q], K.d_rows[r, :, ch * CH:(ch + 1) * CH].unsqueeze(0).broadcast_to(
                            [P, H, CH])).then_inc(S["rows_in"], 16)
                sp.wait_ge(S["fine"], 1)
                K.store(sp, K.o["dn_state"][0, 0].rearrange("h v k -> v h k"), KN[:])
                sp.wait_ge(K.stored, K.n_stored)

            @block.gpsimd
            def _(pool):
                g = K.G(pool)
                level_masks(K, pool, LO, UP, made)
                g.step(pool.memset(NEGM[:], 0.0))
                g.step(pool.memset(STR[:], -1.0))
                g.do(pool.memset(ST[:], 0.0))
                g.step(pool.affine_select(out=NEGM[:], in_=NEGM[:], compare_op=ALU.is_ge, fill=NEG, base=0,
                                          pattern=[[1, P]], channel_multiplier=-1))
                g.do(pool.affine_select(out=STR[:], in_=STR[:], compare_op=ALU.is_gt, fill=0.0, base=0,
                                        pattern=[[1, P]], channel_multiplier=-1))
                pool.sem_inc(made, 1)
                for ch in range(NCH):
                    q = ch % 2
                    pool.wait_ge(S["rows_in"], 32 * (ch + 1))
                    if ch >= 1 and q == 0:
                        pool.wait_ge(S["state"], ch)
                    if q == 1:
                        pool.wait_ge(S["nu"], ch)
                    g.do(pool.tensor_tensor(DT[:], GC[:, 0], bc(tokv(ch, 0)), ALU.subtract))
                    pool.tensor_tensor(DT[:], DT[:], mb(NEGM[:]), ALU.add).then_inc(S["diff"], 1)
                    g.do(pool.tensor_tensor(W[:], GC[:, 1], mb(STR[:]), ALU.mult))
                    pool.wait_ge(S["decay"], ch + 1)
                    pool.tensor_tensor(W[:], W[:], DT[:], ALU.mult).then_inc(S["w"], 1)
                    pool.wait_ge(S["scaled"], ch + 1)
                    pool.wait_ge(S["kd"], ch + 1)
                    g.step(pool.tensor_tensor(KBG[q][:], KN[:], bc(SC[:, 0]), ALU.mult))
                    g.step(pool.tensor_tensor(KD_[q][:], KN[:], bc(SC[:, 1]), ALU.mult))
                    pool.wait_ge(S["backed"], ch + 1)
                    g.wait()
                    pool.tensor_tensor(QG[q][:], QT[:], GC[:, 0], ALU.mult).then_inc(S["pool"], 1)

            @block.scalar
            def _(act):
                a = K.A(act)

                def pre(ch):
                    q = ch % 2
                    act.wait_ge(S["diff"], ch + 1)
                    act.activation(DT[:], DT[:], ACT.Exp).then_inc(S["decay"], 1)
                    a.step(act.activation(SC[:, 2], tokv(ch, 0), ACT.Exp))
                    for h in range(H):
                        a.step(act.activation(SC[:, 1, h:h + 1], K.TK[:, ch, 0, h:h + 1], ACT.Exp, scale=-1.0,
                                              bias=GC[:, 0, h, CH - 1:CH]))
                    act.activation(GE[:, q], GC[:, 0, :, CH - 1:CH].rearrange("p h a -> p (h a)"), ACT.Exp
                                   ).then_inc(S["ge"], 1)
                    a.wait()
                    act.wait_ge(S["ge"], ch + 1)
                    act.activation(GC[:, 0], GC[:, 0], ACT.Exp).then_inc(S["unit"], 1)
                    act.wait_ge(S["tok"], ch + 1)
                    act.activation(M1s[:].rearrange("p a h d -> p a (h d)"), K.ps[:, 0:2], ACT.Square
                                   ).then_inc(S["square"], 1)
                    act.wait_ge(S["back"], ch + 1)
                    act.activation(KT[:], B[3], ACT.Identity)
                    act.activation(QT[:], B[4], ACT.Identity).then_inc(S["backed"], 1)
                    act.activation(X[q][:], mb(K.ident[:]), ACT.Identity)
                    act.activation(Y[q][:], mb(K.ident[:]), ACT.Identity).then_inc(S["first"], 1)

                for c0 in range(0, NCH, 2):
                    pre(c0)
                    pre(c0 + 1)
                    for l in range(6):
                        for q in range(2):
                            n = (c0 // 2 * 6 + l) * 2 + q + 1
                            act.wait_ge(S["m1"], n)
                            act.activation(M1[q], B[q], ACT.Identity).then_inc(S["m1e"], 1)
                    for ch in (c0, c0 + 1):
                        act.wait_ge(S["wT"], ch + 1)
                        act.activation(NWT[:], B[0], ACT.Identity, scale=-1.0).then_inc(S["wTe"], 1)
                        act.wait_ge(S["u"], ch + 1)
                        act.activation(U[:], B[1], ACT.Identity).then_inc(S["ue"], 1)
                        act.wait_ge(S["o"], ch + 1)
                        act.activation(M1[ch % 2], B[2], ACT.Square).then_inc(S["osq"], 1)
                        act.wait_ge(S["oT"], ch + 1)
                        act.activation(OT[:, :, ch * CH:(ch + 1) * CH], B[4], ACT.Identity,
                                       scale=K.par[:, PROW["dn_onorm_w"]:PROW["dn_onorm_w"] + 1]).then_inc(S["oTe"], 1)
                act.wait_ge(S["fin"], 1)
                act.activation(KN[:], B[5], ACT.Identity).then_inc(S["fine"], 1)

            @block.vector
            def _(dve):
                v = K.V(dve)
                dve.wait_ge(made, 57)

                def pre(ch):
                    q = ch % 2
                    dve.wait_ge(S["square"], ch + 1)
                    v.do(dve.tensor_reduce(SS[:], SQ, AX.X, ALU.add))
                    v.do(dve.tensor_scalar(SS[:], SS[:], EPS, None, ALU.add))
                    rsqrt(v, SS[:], RN[:], TM[:])
                    v.do(dve.tensor_scalar(RN[:, 0:H], RN[:, 0:H], SCALE, None, ALU.mult))
                    if ch >= 1:
                        dve.wait_ge(S["pool"], ch)
                    v.step(dve.tensor_tensor(QN[:], B[0], bc(RN[:, 0:H]), ALU.mult))
                    v.step(dve.tensor_tensor(KN[:], B[1], bc(RN[:, H:2 * H]), ALU.mult))
                    dve.tensor_tensor(VB[q][:], B[2], bc(tokv(ch, 2)), ALU.mult).then_inc(S["scaled"], 1)
                    dve.wait_ge(S["unit"], ch + 1)
                    dve.tensor_tensor(SC[:, 0], SC[:, 2], tokv(ch, 2), ALU.mult).then_inc(S["kd"], 1)
                    dve.wait_ge(S["gram"], ch + 1)
                    dve.wait_ge(S["w"], ch + 1)
                    v.step(dve.tensor_tensor(NU[q][:], B[5], W[:], ALU.mult))
                    dve.tensor_tensor(QKT[q][:], B[6], DT[:], ALU.mult).then_inc(S["nu"], 1)

                for c0 in range(0, NCH, 2):
                    pre(c0)
                    pre(c0 + 1)
                    for q in range(2):
                        ch = c0 + q
                        dve.wait_ge(S["firsted"], ch + 1)
                        dve.wait_ge(S["first"], ch + 1)
                        dve.wait_ge(S["nu"], ch + 1)
                        v.step(dve.copy_predicated(X[q][:], mb(LO[:, 0]), B[q]))
                        dve.copy_predicated(Y[q][:], mb(UP[:, 0]), NU[q][:]).then_inc(S["upd"], 1)
                    for l in range(1, 7):
                        for q in range(2):
                            n = (c0 // 2 * 6 + l - 1) * 2 + q + 1
                            dve.wait_ge(S["dxy"], n)
                            if l < 6:
                                v.step(dve.copy_predicated(X[q][:], mb(LO[:, l]), B[2 + q]))
                            dve.copy_predicated(Y[q][:], mb(UP[:, l]), B[4 + q]).then_inc(S["upd"], 1)
                    for q in range(2):
                        ch = c0 + q
                        if ch >= 1:
                            dve.wait_ge(S["state"], ch)
                        v.step(dve.tensor_tensor(STG[:], ST[:], bc(GE[:, q]), ALU.mult))
                        dve.wait_ge(S["osq"], ch + 1)
                        v.do(dve.tensor_reduce(OS[:], M1[q], AX.X, ALU.add))
                        v.do(dve.tensor_scalar(OS[:], OS[:], 1.0 / P, EPS, ALU.mult, ALU.add))
                        rsqrt(v, OS[:], OR[:], OM[:])
                        dve.tensor_tensor(M1[q], B[2], bc(OR[:]), ALU.mult).then_inc(S["on"], 1)
                        dve.wait_ge(S["ds"], ch + 1)
                        dve.tensor_tensor(ST[:], STG[:], B[3], ALU.add).then_inc(S["state"], 1)

            @block.tensor
            def _(pe):
                def pre(ch):
                    q = ch % 2
                    cols = slice(ch * CH, (ch + 1) * CH)
                    if ch >= 1:
                        pe.wait_ge(S["nu"], ch)
                        pe.wait_ge(S["scaled"], ch)
                        if ch - q:
                            pe.wait_ge(S["oTe"], ch - q)
                            pe.wait_ge(S["state"], ch - q)
                            pe.wait_ge(S["on"], ch - q)
                    for r in range(3):
                        for h in range(H):
                            last = pe.transpose(B[r][:, h], qkv(r, h, cols), K.ident[:])
                    last.then_inc(S["tok"], 1)
                    pe.wait_ge(S["scaled"], ch + 1)
                    if ch >= 1:
                        pe.wait_ge(S["backed"], ch)
                    for r, src in ((3, KN), (4, QN)):
                        for h in range(H):
                            last = pe.transpose(B[r][:, h], src[:, h], K.ident[:])
                    last.then_inc(S["back"], 1)
                    pe.wait_ge(S["backed"], ch + 1)
                    for r, src in ((5, KT), (6, QT)):
                        for h in range(H):
                            last = pe.matmul(B[r][:, h], KT[:, h], src[:, h], start=True, stop=True)
                    last.then_inc(S["gram"], 1)

                for c0 in range(0, NCH, 2):
                    pre(c0)
                    pre(c0 + 1)
                    for q in range(2):
                        ch = c0 + q
                        pe.wait_ge(S["nu"], ch + 1)
                        pe.wait_ge(S["scaled"], c0 + 2)
                        for h in range(H):
                            last = pe.matmul(B[q][:, h], NU[q][:, h], K.ident[:], start=True, stop=True)
                        last.then_inc(S["firsted"], 1)
                    for l in range(1, 7):
                        for q in range(2):
                            n = (c0 // 2 * 6 + l - 1) * 2 + q
                            pe.wait_ge(S["upd"], c0 // 2 * 14 + (l - 1) * 2 + q + 1)
                            for h in range(H):
                                last = pe.matmul(B[q][:, h], NU[q][:, h], X[q][:, h], start=True, stop=True)
                            last.then_inc(S["m1"], 1)
                        for q in range(2):
                            n = (c0 // 2 * 6 + l - 1) * 2 + q
                            pe.wait_ge(S["m1e"], n + 1)
                            for h in range(H):
                                if l < 6:
                                    pe.matmul(B[2 + q][:, h], Y[q][:, h], M1[q][:, h], start=True, stop=True)
                                last = pe.matmul(B[4 + q][:, h], M1[q][:, h], Y[q][:, h], start=True, stop=True)
                            last.then_inc(S["dxy"], 1)
                    for q in range(2):
                        ch = c0 + q
                        pe.wait_ge(S["upd"], c0 // 2 * 14 + 14)
                        pe.wait_ge(S["pool"], c0 + 2)
                        if q:
                            pe.wait_ge(S["wTe"], ch)
                        for h in range(H):
                            last = pe.matmul(B[0][:, h], KBG[q][:, h], Y[q][:, h], start=True, stop=True)
                        last.then_inc(S["wT"], 1)
                        pe.wait_ge(S["wTe"], ch + 1)
                        if ch:
                            pe.wait_ge(S["state"], ch)
                        for h in range(H):
                            pe.matmul(B[1][:, h], Y[q][:, h], VB[q][:, h], start=True, stop=False)
                            last = pe.matmul(B[1][:, h], NWT[:, h], ST[:, h], start=False, stop=True)
                        last.then_inc(S["u"], 1)
                        pe.wait_ge(S["ue"], ch + 1)
                        for h in range(H):
                            pe.matmul(B[2][:, h], QG[q][:, h], ST[:, h], start=True, stop=False)
                            last = pe.matmul(B[2][:, h], QKT[q][:, h], U[:, h], start=False, stop=True)
                        last.then_inc(S["o"], 1)
                        for h in range(H):
                            last = pe.matmul(B[3][:, h], KD_[q][:, h], U[:, h], start=True, stop=True)
                        last.then_inc(S["ds"], 1)
                        pe.wait_ge(S["on"], ch + 1)
                        if q:
                            pe.wait_ge(S["oTe"], ch)
                        for h in range(H):
                            last = pe.transpose(B[4][:, h], M1[q][:, h], K.ident[:])
                        last.then_inc(S["oT"], 1)
                pe.wait_ge(S["state"], NCH)
                for h in range(H):
                    last = pe.transpose(B[5][:, h], ST[:, h], K.ident[:])
                last.then_inc(S["fin"], 1)


def delta_decode(K):
    nc, i = K.nc, K.i
    S4 = [P, NB, H, P]
    with ExitStack() as c:
        sb = lambda n_, s, d=F32: c.enter_context(nc.sbuf_tensor("e" + n_, s, d))
        SD, KB, T = sb("_state", S4), sb("_row", S4), sb("_prod", S4)
        R = sb("_rows", [NB, 2, H, P])
        SS, RN, TM = sb("_ss", [NB, 2, H]), sb("_rn", [NB, 2, H]), sb("_tm", [NB, 2, H])
        SK, UU, O = sb("_sk", [P, NB, H]), sb("_u", [P, NB, H]), sb("_o", [P, NB, H])
        OR, OQ = sb("_or", [32, P]), sb("_oq", [32, P])
        OS, OR1, OM = sb("_os", [32, 1]), sb("_or1", [32, 1]), sb("_om", [32, 1])
        N = {x: K.sem("de_" + x) for x in ("s_in", "k_in", "q_in", "tr", "sq", "rows", "rows_out", "k_used",
                                           "new", "o", "oT", "osq", "on", "ob")}
        with nc.Block(no_gpsimd_drain=True) as block:
            @block.sync
            def _(sp):
                for b in range(NB):
                    sp.dma_start(SD[:, b], i["state_dn"][0, b].rearrange("h v k -> v h k")).then_inc(N["s_in"], 16)
                sp.wait_ge(N["rows"], 1)
                sp.dma_start(K.d_qk.rearrange("r b h d -> b r h d"), R[:]).then_inc(N["rows_out"], 16)
                sp.wait_ge(N["rows_out"], 16)
                row = lambda r: K.d_qk[r].rearrange("b h d -> (b h d)").unsqueeze(0).broadcast_to([P, NB * H * P])
                sp.dma_start(KB[:].rearrange("p b h d -> p (b h d)"), row(1)).then_inc(N["k_in"], 16)
                sp.wait_ge(N["k_used"], 1)
                sp.dma_start(KB[:].rearrange("p b h d -> p (b h d)"), row(0)).then_inc(N["q_in"], 16)
                sp.wait_ge(N["new"], 1)
                for b in range(NB):
                    K.store(sp, K.o["dn_state_s"][0, b].rearrange("h v k -> v h k"), SD[:, b])
                sp.wait_ge(K.stored, K.n_stored)

            @block.tensor
            def _(pe):
                for r in range(2):
                    for h in range(H):
                        x = K.OT if r == 0 else K.merged
                        last = pe.transpose(K.ps[0:NB, r, h * P:(h + 1) * P], x[:, h, SEQ:TOK], K.ident[:])
                last.then_inc(N["tr"], 1)
                pe.wait_ge(N["o"], 1)
                pe.transpose(K.ps[0:32, 2, 0:P], O[:].rearrange("p b h -> p (b h)"), K.ident[:]).then_inc(N["oT"], 1)
                pe.wait_ge(N["on"], 1)
                pe.transpose(K.ps[:, 3, 0:32], OR[:], K.ident[0:32, 0:32]).then_inc(N["ob"], 1)

            @block.scalar
            def _(act):
                act.wait_ge(N["tr"], 1)
                act.activation(R[:].rearrange("b r h d -> b r (h d)"), K.ps[0:NB, 0:2], ACT.Square).then_inc(N["sq"], 1)
                act.wait_ge(N["oT"], 1)
                act.activation(OQ[:], K.ps[0:32, 2, 0:P], ACT.Square, accum_out=OS[:]).then_inc(N["osq"], 1)
                act.wait_ge(N["ob"], 1)
                act.activation(K.OT[:, :, SEQ:TOK].rearrange("p h b -> p b h"),
                               K.ps[:, 3, 0:32].rearrange("p (b h) -> p b h", b=NB), ACT.Identity,
                               scale=K.par[:, PROW["dn_onorm_w"]:PROW["dn_onorm_w"] + 1])

            @block.vector
            def _(dve):
                v = K.V(dve)
                last = lambda ap: ap.unsqueeze(3).broadcast_to(S4)
                al, be = (K.alpha[:, q].rearrange("p h b -> p b h") for q in range(2))
                dve.wait_ge(N["sq"], 1)
                v.do(dve.tensor_reduce(SS[:], R[:], AX.X, ALU.add))
                v.do(dve.tensor_scalar(SS[:], SS[:], EPS, None, ALU.add))
                rsqrt(v, SS[:].rearrange("b r h -> b (r h)"), RN[:].rearrange("b r h -> b (r h)"),
                      TM[:].rearrange("b r h -> b (r h)"))
                v.do(dve.tensor_scalar(RN[:, 0], RN[:, 0], SCALE, None, ALU.mult))
                for r in range(2):
                    ins = dve.tensor_tensor(R[:, r], heads(K.ps[0:NB, r]),
                                            RN[:, r].unsqueeze(2).broadcast_to([NB, H, P]), ALU.mult)
                ins.then_inc(N["rows"], 1)
                dve.wait_ge(N["s_in"], 16 * NB)
                dve.wait_ge(N["k_in"], 16)
                flat = lambda x: x[:].rearrange("p b h d -> p (b h d)")
                flat3 = lambda x: x[:].rearrange("p b h d -> p (b h) d")
                v.do(dve.tensor_tensor(flat(T), flat(SD), flat(KB), ALU.mult))
                v.do(dve.tensor_reduce(SK[:].rearrange("p b h -> p (b h)"), flat3(T), AX.X, ALU.add))
                v.do(dve.tensor_tensor(SK[:], SK[:], al, ALU.mult))
                v.do(dve.tensor_tensor(UU[:], K.merged[:, H:2 * H, SEQ:TOK].rearrange("p h b -> p b h"), SK[:],
                                       ALU.subtract))
                v.do(dve.tensor_tensor(UU[:], UU[:], be, ALU.mult))
                for b in range(NB):
                    for h in range(H):
                        v.step(dve.tensor_scalar(SD[:, b, h], SD[:, b, h], K.alpha[:, 0, h, b:b + 1], None, ALU.mult))
                        ins = dve.tensor_scalar(T[:, b, h], KB[:, b, h], UU[:, b, h:h + 1], None, ALU.mult)
                        if (b, h) != (NB - 1, H - 1):
                            v.step(ins)
                ins.then_inc(N["k_used"], 1)
                dve.wait_ge(N["k_used"], 1)
                dve.tensor_tensor(flat(SD), flat(SD), flat(T), ALU.add).then_inc(N["new"], 1)
                dve.wait_ge(N["new"], 1)
                dve.wait_ge(N["q_in"], 16)
                v.do(dve.tensor_tensor(flat(T), flat(SD), flat(KB), ALU.mult))
                dve.tensor_reduce(O[:].rearrange("p b h -> p (b h)"), flat3(T), AX.X, ALU.add).then_inc(N["o"], 1)
                dve.wait_ge(N["osq"], 1)
                v.do(dve.tensor_scalar(OS[:], OS[:], 1.0 / P, EPS, ALU.mult, ALU.add))
                rsqrt(v, OS[:], OR1[:], OM[:])
                dve.tensor_scalar(OR[:], K.ps[0:32, 2, 0:P], OR1[:, 0:1], None, ALU.mult).then_inc(N["on"], 1)


def lru(K):
    nc, i = K.nc, K.i
    with ExitStack() as c:
        sb = lambda n_, s, d=F32: c.enter_context(nc.sbuf_tensor("l" + n_, s, d))
        BD = sb("_blocks", [P, 2, H, P])
        A, U, XG = sb("_a", [P, H, TOK]), sb("_u", [P, H, TOK]), sb("_x", [P, H, TOK])
        SM = sb("_sp", [P, 6, H])
        HR = sb("_h_rows", [9, BW])
        N = {x: K.sem("lru_" + x) for x in ("zero", "w_in", "gates", "tr", "ti", "nla", "a", "th", "u", "root",
                                            "h", "hT", "hTe", "out", "lam", "lamu", "xg", "ps")}
        lam = K.par[:, PROW["lru_lambda"]:PROW["lru_lambda"] + H]
        with nc.Block(no_gpsimd_drain=True) as block:
            @block.gpsimd
            def _(pool):
                pool.memset(BD[:], 0.0).then_inc(N["zero"], 1)

            @block.sync
            def _(sp):
                sp.wait_ge(N["zero"], 1)
                for r, name in enumerate(("lru_w_r", "lru_w_i")):
                    w = i[name][0].rearrange("(t a) e f -> a e t f", a=2)
                    for a in range(2):
                        sp.dma_start(BD[64 * a:64 * a + 64, r, :, 64 * a:64 * a + 64], w[a]).then_inc(N["w_in"], 16)
                sp.wait_ge(N["hTe"], 1)
                K.store(sp, K.o["lru_h"][0], HR[0:1])
                K.store(sp, K.o["lru_h_s"][0], HR[1:9])
                sp.wait_ge(K.stored, K.n_stored)

            @block.tensor
            def _(pe):
                pe.wait_ge(N["w_in"], 64)
                for t in range(H):
                    for r in range(2):
                        if t >= 1:
                            pe.wait_ge(N["tr"] if r == 0 else N["ti"], t)
                        for g in range(3):
                            last = pe.matmul(K.ps[:, 3 * r + g, 0:G3], BD[:, r, t], K.OT[:, t, g * G3:(g + 1) * G3],
                                             start=True, stop=True)
                        last.then_inc(N["gates"], 1)
                pe.wait_ge(N["h"], H)
                for t in range(H):
                    last = pe.transpose(K.ps[0:9, 6, t * P:(t + 1) * P], K.OT[:, t, SEQ - 1:TOK], K.ident[:])
                last.then_inc(N["hT"], 1)

            @block.scalar
            def _(act):
                act.wait_ge(N["lam"], 1)
                act.activation(SM[:, 1], SM[:, 1], ACT.Exp).then_inc(N["lamu"], 1)
                for t in range(H):
                    for r, (dst, name, s) in enumerate(((A, "lru_b_r", "tr"), (U, "lru_b_i", "ti"))):
                        act.wait_ge(N["gates"], 2 * t + r + 1)
                        b = PROW[name] + t
                        act.activation(dst[:, t].rearrange("p (a b) -> p a b", a=3),
                                       K.ps[:, 3 * r:3 * r + 3, 0:G3], ACT.Tanh, scale=0.5,
                                       bias=K.hpar[:, b:b + 1]).then_inc(N[s], 1)
                    act.wait_ge(N["nla"], t + 1)
                    act.activation(U[:, t], A[:, t], ACT.Tanh).then_inc(N["th"], 1)
                    act.activation(A[:, t], A[:, t], ACT.Exp, scale=-1.0).then_inc(N["a"], 1)
                for t in range(H):
                    act.wait_ge(N["u"], t + 1)
                    act.activation(U[:, t], U[:, t], ACT.Sqrt).then_inc(N["root"], 1)
                act.wait_ge(N["hT"], 1)
                act.activation(HR[:], K.ps[0:9, 6], ACT.Identity).then_inc(N["hTe"], 1)

            @block.vector
            def _(dve):
                v = K.V(dve)
                v.do(dve.tensor_scalar(SM[:, 0], lam, -1.0, None, ALU.mult))
                dve.tensor_tensor(SM[:, 1], SM[:, 0], lam, ALU.min).then_inc(N["lam"], 1)
                dve.wait_ge(N["lamu"], 1)
                log1p_exp(v, SM[:, 0], SM[:, 1], SM[:, 2], SM[:, 3], SM[:, 4])
                v.do(dve.tensor_scalar(SM[:, 5], SM[:, 4], LRU_C / 2, None, ALU.mult))
                for t in range(H):
                    dve.wait_ge(N["tr"], t + 1)
                    dve.wait_ge(N["ti"], t + 1)
                    v.step(dve.scalar_tensor_tensor(XG[:, t], U[:, t], 1.0, K.OT[:, t], ALU.add, ALU.mult))
                    dve.tensor_scalar(A[:, t], A[:, t], 1.0, SM[:, 5, t:t + 1], ALU.add, ALU.mult).then_inc(N["nla"], 1)
                    dve.wait_ge(N["a"], t + 1)
                    v.do(dve.tensor_tensor(K.OT[:, t], A[:, t], A[:, t], ALU.mult))
                    dve.scalar_tensor_tensor(U[:, t], K.OT[:, t], 1.0, U[:, t], ALU.add, ALU.mult).then_inc(N["u"], 1)
                for t in range(H):
                    dve.wait_ge(N["root"], t + 1)
                    v.do(dve.scalar_tensor_tensor(XG[:, t], U[:, t], 0.5, XG[:, t], ALU.mult, ALU.mult))
                    v.step(dve.tensor_tensor_scan(K.OT[:, t, 0:SEQ], A[:, t, 0:SEQ], XG[:, t, 0:SEQ], 0.0, ALU.mult,
                                                  ALU.add))
                    v.do(dve.tensor_tensor(A[:, t, SEQ:TOK], A[:, t, SEQ:TOK], K.convs[:, 12 + t, 24:32], ALU.mult))
                    dve.tensor_tensor(K.OT[:, t, SEQ:TOK], A[:, t, SEQ:TOK], XG[:, t, SEQ:TOK], ALU.add
                                      ).then_inc(N["h"], 1)


def plain_tiles(K, t0, n, row, DST, tag, x=None, cols=TOK):
    nc = K.nc
    xH, xL = x or (K.hH, K.hL)
    with nc.Block(no_gpsimd_drain=True) as block:
        @block.sync
        def _(sp):
            K.loads(sp, t0 + n + 2)

        @block.gpsimd
        def _(pool):
            K.split_lo(pool, t0 + n + 1)

        @block.scalar
        def _(act):
            for j in range(n):
                t = t0 + j
                K.split_hi(act, t + 2)
                act.wait_ge(K.tile_done, t + 1)
                if row is None:
                    act.activation(DST[:, j], K.ps[:, 3 * (t % 2), 0:cols], ACT.Identity).then_inc(K.evac_act, 1)
                else:
                    act.activation(DST[:, j].rearrange("p (a b) -> p a b", a=3), K.psum(t), ACT.Identity,
                                   bias=K.bias[:, row + j:row + j + 1]).then_inc(K.evac_act, 1)

        @block.tensor
        def _(pe):
            for j in range(n):
                K.project(pe, t0 + j, xH, xL, groups=3 if row is not None else 1, cols=cols)


def to_rows(K, SRC, ROWS, sizes, tag, norm=None, back=None, stores=()):
    nc = K.nc
    nt = len(sizes)
    with ExitStack() as c:
        sb = lambda n_, s, d=F32: c.enter_context(nc.sbuf_tensor(tag + n_, s, d))
        N = {x: K.sem(tag + "_" + x) for x in ("tr", "rows", "normed", "back", "backed", "filled")}
        if norm is not None:
            T = sb("_t", [P, H, P])
            SS, RN, TM = (sb(x, [P, nt, H]) for x in ("_ss", "_rn", "_tm"))
        flat = lambda x: x[:].rearrange("p a h -> p (a h)")
        with nc.Block(no_gpsimd_drain=True) as block:
            @block.tensor
            def _(pe):
                for j, n in enumerate(sizes):
                    if j >= 4:
                        pe.wait_ge(N["rows"], j - 3)
                    for h in range(H):
                        last = pe.transpose(K.ps[0:n, j % 4, h * P:(h + 1) * P], SRC[:, h, j * P:j * P + n], K.ident[:])
                    last.then_inc(N["tr"], 1)
                if back is not None:
                    for j, n in enumerate(sizes):
                        pe.wait_ge(N["normed"], j + 1)
                        if j >= 4:
                            pe.wait_ge(N["backed"], j - 3)
                        for h in range(H):
                            last = pe.transpose(K.ps[:, 4 + j % 4, h * P:h * P + n], ROWS[0:n, j, h], K.ident[0:n, 0:n])
                        last.then_inc(N["back"], 1)

            @block.scalar
            def _(act):
                if norm is not None:
                    act.wait_ge(N["filled"], 1)
                for j, n in enumerate(sizes):
                    act.wait_ge(N["tr"], j + 1)
                    act.activation(ROWS[0:n, j], heads(K.ps[0:n, j % 4]), ACT.Identity).then_inc(N["rows"], 1)
                if back is not None:
                    for j, n in enumerate(sizes):
                        act.wait_ge(N["back"], j + 1)
                        act.activation(back[0][:, :, j * P:j * P + n], heads(K.ps[:, 4 + j % 4])[:, :, 0:n],
                                       ACT.Identity, scale=back[1]).then_inc(N["backed"], 1)

            @block.vector
            def _(dve):
                if norm is None:
                    return
                v = K.V(dve)
                v.step(dve.memset(SS[:], 1.0))
                dve.memset(T[:], 1.0).then_inc(N["filled"], 1)
                v.wait()
                for j, n in enumerate(sizes):
                    dve.wait_ge(N["rows"], j + 1)
                    v.do(dve.tensor_tensor(T[0:n], ROWS[0:n, j], ROWS[0:n, j], ALU.mult))
                    v.do(dve.tensor_reduce(SS[0:n, j], T[0:n], AX.X, ALU.add))
                v.do(dve.tensor_scalar(SS[:], SS[:], 1.0 / P, EPS, ALU.mult, ALU.add))
                rsqrt(v, flat(SS), flat(RN), flat(TM))
                for j, n in enumerate(sizes):
                    v.do(dve.tensor_tensor(ROWS[0:n, j], ROWS[0:n, j],
                                           RN[0:n, j].unsqueeze(2).broadcast_to([n, H, P]), ALU.mult))
                    dve.tensor_tensor(ROWS[0:n, j], ROWS[0:n, j], norm[0:n].unsqueeze(1).broadcast_to([n, H, P]),
                                      ALU.mult).then_inc(N["normed"], 1)

            @block.sync
            def _(sp):
                for j, n in enumerate(sizes):
                    if not stores:
                        break
                    sp.wait_ge(N["rows"] if norm is None else N["normed"], j + 1)
                    K.store(sp, stores[j], ROWS[0:n, j])
                if stores:
                    sp.wait_ge(K.stored, K.n_stored)


def query_norms(K, RQ, tag):
    nc = K.nc
    with ExitStack() as c:
        sb = lambda n_, s, d=F32: c.enter_context(nc.sbuf_tensor(tag + n_, s, d))
        SQ = sb("_sq", [P, 2, SEQ])
        SS, TM = sb("_qss", [P, H, TT8]), sb("_qtm", [P, H, TT8])
        sq, sums = K.sem(tag + "_qsq"), K.sem(tag + "_qsum")
        flat = lambda x: x[:].rearrange("p a h -> p (a h)")
        with nc.Block(no_gpsimd_drain=True) as block:
            @block.scalar
            def _(act):
                for h in range(H):
                    if h >= 2:
                        act.wait_ge(sums, h - 1)
                    act.activation(SQ[:, h % 2], K.OT[:, h, 0:SEQ], ACT.Square).then_inc(sq, 1)

            @block.tensor
            def _(pe):
                for h in range(H):
                    pe.wait_ge(sq, h + 1)
                    for t in range(TT8):
                        q = h * TT8 + t
                        last = pe.matmul(K.ps[:, 7, q:q + 1], SQ[:, h % 2, t * P:(t + 1) * P], K.ones[:],
                                         start=True, stop=True)
                    last.then_inc(sums, 1)

            @block.vector
            def _(dve):
                v = K.V(dve)
                dve.wait_ge(sums, H)
                v.do(dve.tensor_scalar(flat(SS), K.ps[:, 7, 0:H * TT8], 1.0 / P, EPS, ALU.mult, ALU.add))
                rsqrt(v, flat(SS), flat(RQ), flat(TM))
                v.do(dve.tensor_scalar(flat(RQ), flat(RQ), SCALE, None, ALU.mult))


def attend(K, KT, V, RQ, tag, causal):
    nc = K.nc
    its = [(h, t) for h in range(H) for t in range(TT8)]
    nb = [t + 1 if causal else MEM // P for _, t in its]
    W = SEQ if causal else MEM
    with ExitStack() as c:
        sb = lambda n_, s, d=F32: c.enter_context(nc.sbuf_tensor(tag + n_, s, d))
        LG = sb("_logits", [P, 2, W])
        PT = sb("_pT", [P, W // P, P])
        NM, RS = sb("_negmax", [P, 2]), sb("_sum", [P, 2])
        if causal:
            C = sb("_c_bc", [P, 2, SEQ])
            CR = sb("_c_rel", [P, SEQ])
            MK = sb("_mask", [P, P])
        N = {x: K.sem(tag + "_" + x) for x in ("c_in0", "c_in1", "rel", "mask", "s", "lg", "max", "exp", "p", "pT", "pTe",
                                               "o", "oe")}
        with nc.Block(no_gpsimd_drain=True) as block:
            @block.sync
            def _(sp):
                if causal:
                    for h in range(H):
                        if h >= 2:
                            sp.wait_ge(N["rel"], TT8 * (h - 1))
                        sp.dma_start(C[:, h % 2], K.d_rows[1, h:h + 1].broadcast_to([P, SEQ])
                                     ).then_inc(N[f"c_in{h % 2}"], 16)

            @block.gpsimd
            def _(pool):
                if not causal:
                    return
                g = K.G(pool)
                g.do(pool.memset(MK[:], 0.0))
                pool.affine_select(out=MK[:], in_=MK[:], compare_op=ALU.is_ge, fill=NEG, base=0,
                                   pattern=[[-1, P]], channel_multiplier=1).then_inc(N["mask"], 1)
                for n, (h, t) in enumerate(its):
                    pool.wait_ge(N[f"c_in{h % 2}"], 16 * (h // 2 + 1))
                    if n >= 1:
                        pool.wait_ge(N["lg"], n)
                    w = nb[n] * P
                    pool.tensor_scalar(CR[:, 0:w], C[:, h % 2, 0:w], K.TK[:, t, 1, h:h + 1], None, ALU.subtract
                                       ).then_inc(N["rel"], 1)

            @block.tensor
            def _(pe):
                def scores(n):
                    h, t = its[n]
                    if n >= 2:
                        pe.wait_ge(N["lg"], n - 1)
                    w = nb[n] * P
                    for a in range(0, w, 512):
                        last = pe.matmul(K.ps[:, 2 * (n % 2) + a // 512, 0:min(512, w - a)],
                                         K.OT[:, h, t * P:(t + 1) * P], KT[:, h, a:min(a + 512, w)],
                                         start=True, stop=True)
                    last.then_inc(N["s"], 1)

                def turn(n):
                    pe.wait_ge(N["p"], n + 1)
                    if n >= 1:
                        pe.wait_ge(N["pTe"], n)
                    for b in range(nb[n]):
                        last = pe.transpose(K.ps[:, 4 + b // 4, (b % 4) * P:(b % 4 + 1) * P],
                                            LG[:, n % 2, b * P:(b + 1) * P], K.ident[:])
                    last.then_inc(N["pT"], 1)

                def values(n):
                    h, t = its[n]
                    pe.wait_ge(N["pTe"], n + 1)
                    if n >= 2:
                        pe.wait_ge(N["oe"], n - 1)
                    for b in range(nb[n]):
                        last = pe.matmul(K.ps[:, 6 + n % 2, 0:P], V[:, b, h], PT[:, b], start=(b == 0),
                                         stop=(b == nb[n] - 1))
                    last.then_inc(N["o"], 1)

                scores(0)
                for n in range(len(its)):
                    if n + 1 < len(its):
                        scores(n + 1)
                    if n >= 1:
                        values(n - 1)
                    turn(n)
                values(len(its) - 1)

            @block.vector
            def _(dve):
                v = K.V(dve)
                if causal:
                    dve.wait_ge(N["mask"], 1)

                def logits(n):
                    h, t = its[n]
                    w = nb[n] * P
                    dve.wait_ge(N["s"], n + 1)
                    if n >= 2:
                        dve.wait_ge(N["pT"], n - 1)
                    q = 2 * (n % 2)
                    lg = LG[:, n % 2, 0:w]
                    rq = RQ[:, h, t:t + 1]
                    if causal:
                        dve.wait_ge(N["rel"], n + 1)
                        m = min(w, 512)
                        ins = dve.scalar_tensor_tensor(lg[:, 0:m], K.ps[:, q, 0:m], rq, CR[:, 0:m], ALU.mult,
                                                       ALU.subtract)
                        if w > 512:
                            v.step(ins)
                            ins = dve.scalar_tensor_tensor(lg[:, 512:w], K.ps[:, q + 1, 0:w - 512], rq, CR[:, 512:w],
                                                           ALU.mult, ALU.subtract)
                        ins.then_inc(N["lg"], 1)
                        dve.wait_ge(N["lg"], n + 1)
                        v.do(dve.tensor_tensor(lg[:, w - P:w], lg[:, w - P:w], MK[:], ALU.add))
                    else:
                        dve.tensor_scalar(lg, K.ps[:, q, 0:w], rq, None, ALU.mult).then_inc(N["lg"], 1)
                        dve.wait_ge(N["lg"], n + 1)
                    dve.tensor_reduce(NM[:, n % 2:n % 2 + 1], lg, AX.X, ALU.max, negate=True).then_inc(N["max"], 1)

                def normalise(n):
                    w = nb[n] * P
                    dve.wait_ge(N["exp"], n + 1)
                    v.do(dve.reciprocal(RS[:, n % 2:n % 2 + 1], RS[:, n % 2:n % 2 + 1]))
                    dve.tensor_scalar(LG[:, n % 2, 0:w], LG[:, n % 2, 0:w], RS[:, n % 2:n % 2 + 1], None, ALU.mult
                                      ).then_inc(N["p"], 1)

                logits(0)
                for n in range(len(its)):
                    if n + 1 < len(its):
                        logits(n + 1)
                    normalise(n)

            @block.scalar
            def _(act):
                def exps(n):
                    w = nb[n] * P
                    act.wait_ge(N["max"], n + 1)
                    act.activation(LG[:, n % 2, 0:w], LG[:, n % 2, 0:w], ACT.Exp, bias=NM[:, n % 2:n % 2 + 1],
                                   accum_out=RS[:, n % 2:n % 2 + 1]).then_inc(N["exp"], 1)

                def turned(n):
                    act.wait_ge(N["pT"], n + 1)
                    if n >= 1:
                        act.wait_ge(N["o"], n)
                    w = nb[n]
                    a = min(w, 4)
                    ins = act.activation(PT[:, 0:a], heads(K.ps[:, 4])[:, 0:a], ACT.Identity)
                    if w > 4:
                        ins = act.activation(PT[:, 4:w], heads(K.ps[:, 5])[:, 0:w - 4], ACT.Identity)
                    ins.then_inc(N["pTe"], 1)

                def out(n):
                    h, t = its[n]
                    act.wait_ge(N["o"], n + 1)
                    act.activation(K.OT[:, h, t * P:(t + 1) * P], K.ps[:, 6 + n % 2, 0:P], ACT.Identity
                                   ).then_inc(N["oe"], 1)

                exps(0)
                for n in range(len(its)):
                    if n + 1 < len(its):
                        exps(n + 1)
                    turned(n)
                    if n >= 1:
                        out(n - 1)
                out(len(its) - 1)


def attend_decode(K, tag, fox):
    nc, i = K.nc, K.i
    NP = PAGES if fox else MEM // P
    W = NP * P
    R = NB * H
    with ExitStack() as c:
        sb = lambda n_, s, d=F32: c.enter_context(nc.sbuf_tensor(tag + n_, s, d))
        KV = sb("_kv", [P, 2, NP, H, P])
        T = sb("_t", [P, NP, H, P])
        QB = sb("_qb", [P, NB, H, P])
        QR = sb("_q_rows", [NB, H, P])
        QS, QN, QM = sb("_qs", [NB, H]), sb("_qn", [NB, H]), sb("_qm", [NB, H])
        SB = sb("_scores", [P, NP, NB, H])
        LG = sb("_logits", [R, W])
        PC = sb("_p_cols", [P, NP, R])
        NM, RS = sb("_nm", [R, 1]), sb("_rs", [R, 1])
        OA = sb("_oa", [P, R])
        N = {x: K.sem(tag + "_" + x) for x in
             ("q", "qsq", "qr", "q_out", "qb", "k_in0", "k_in1", "used", "sc", "scT", "max", "exp", "p", "pT", "pTe",
              "v_in0", "v_in1", "o", "oa", "pg", "lf_in", "lfT", "lfs", "row_in", "new", "newT", "newv")}
        if fox:
            PG = sb("_pages", [1, R], I32)
            LF = sb("_lf", [P, NP, NB, H])
            CC = sb("_c", [R, W])
            LN, SN = sb("_lf_new", [R, 1]), sb("_s_new", [R, 4])
            Q3, K3, V3 = (sb(x, [R, P]) for x in ("_q3", "_k3", "_v3"))
        w_bc = K.qnw if fox else K.mqnw
        cache = ("cache_fox_k", "cache_fox_v") if fox else ("cache_mem_k", "cache_mem_v")
        with nc.Block(no_gpsimd_drain=True) as block:
            @block.sync
            def _(sp):
                pages = []
                if fox:
                    sp.dma_start(PG[:], i["page_table"].rearrange("b g -> (b g)").unsqueeze(0)).then_inc(N["pg"], 16)
                    sp.wait_ge(N["pg"], 16)

                def load(which, b, count):
                    src = i[cache[which]]
                    s = N[("k_in" if which == 0 else "v_in") + str(b % 2)]
                    if not fox:
                        sp.dma_start(KV[:, b % 2], src[0, b].rearrange("(g k) h d -> k g h d", k=P)).then_inc(s, 16)
                        return
                    for g in range(NP):
                        page = sp.value_load(PG[0:1, b * NP + g:b * NP + g + 1], min_val=0,
                                             max_val=src.shape[1] - 1)
                        sp.dma_start(KV[:, b % 2, g], src[0, bass.ds(page, 1)].rearrange("a k h d -> k (a h) d")
                                     ).then_inc(s, 16)
                        if which == 0:
                            sp.dma_start(LF[:, g, b], i["cache_fox_logf"][0, bass.ds(page, 1)].rearrange(
                                "a k h -> k (a h)")).then_inc(N["lf_in"], 16)

                load(0, 0, 0)
                load(0, 1, 0)
                sp.wait_ge(N["qr"], 1)
                sp.dma_start(K.d_q, QR[:]).then_inc(N["q_out"], 16)
                sp.wait_ge(N["q_out"], 16)
                sp.dma_start(QB[:].rearrange("p b h d -> p (b h d)"),
                             K.d_q.rearrange("b h d -> (b h d)").unsqueeze(0).broadcast_to([P, NB * H * P])
                             ).then_inc(N["qb"], 16)
                if fox:
                    sp.dma_start(Q3[:], K.d_q.rearrange("b h d -> (b h) d")).then_inc(N["row_in"], 16)
                    sp.dma_start(K3[:], K.o["fox_k_s"][0, :, 0].rearrange("b h d -> (b h) d")).then_inc(N["row_in"], 16)
                    sp.dma_start(V3[:], K.o["fox_v_s"][0, :, 0].rearrange("b h d -> (b h) d")).then_inc(N["row_in"], 16)
                    sp.dma_start(LN[:], K.d_lf.rearrange("b (h a) -> (b h) a", a=1)).then_inc(N["row_in"], 16)
                for b in range(2, NB):
                    sp.wait_ge(N["used"], b - 1)
                    load(0, b, 0)
                for b in range(NB):
                    if b < 2:
                        sp.wait_ge(N["used"], NB - 1 + b)
                    else:
                        sp.wait_ge(N["o"], b - 1)
                    load(1, b, 0)

            @block.tensor
            def _(pe):
                for h in range(H):
                    last = pe.transpose(K.ps[0:NB, 0, h * P:(h + 1) * P], K.OT[:, h, SEQ:TOK], K.ident[:])
                last.then_inc(N["q"], 1)
                pe.wait_ge(N["sc"], NB)
                for g in range(NP):
                    last = pe.transpose(K.ps[0:R, 1, g * P:(g + 1) * P], SB[:, g].rearrange("p b h -> p (b h)"),
                                        K.ident[:])
                last.then_inc(N["scT"], 1)
                if fox:
                    pe.wait_ge(N["lf_in"], 16 * R)
                    for g in range(NP):
                        last = pe.transpose(K.ps[0:R, 2, g * P:(g + 1) * P],
                                            LF[:, g].rearrange("p b h -> p (b h)"), K.ident[:])
                    last.then_inc(N["lfT"], 1)
                pe.wait_ge(N["p"], 1)
                for g in range(NP):
                    last = pe.transpose(K.ps[:, 3, g * R:(g + 1) * R], LG[:, g * P:(g + 1) * P], K.ident[0:R, 0:R])
                last.then_inc(N["pT"], 1)
                pe.wait_ge(N["pTe"], 1)
                for b in range(NB):
                    pe.wait_ge(N[f"v_in{b % 2}"], 16 * (NP if fox else 1) * (b // 2 + 1))
                    for h in range(H):
                        r = b * H + h
                        for g in range(NP):
                            last = pe.matmul(K.ps[:, 4, r:r + 1], KV[:, b % 2, g, h], PC[:, g, r:r + 1],
                                             start=(g == 0), stop=(g == NP - 1))
                    last.then_inc(N["o"], 1)
                if fox:
                    pe.wait_ge(N["newv"], 1)
                    pe.matmul(K.ps[:, 5, 0:R], V3[:], K.ident[0:R, 0:R], start=True, stop=True).then_inc(N["newT"], 1)

            @block.scalar
            def _(act):
                act.wait_ge(N["q"], 1)
                act.activation(QR[:], heads(K.ps[0:NB, 0]), ACT.Square).then_inc(N["qsq"], 1)
                act.wait_ge(N["max"], 1)
                act.activation(LG[:], LG[:], ACT.Exp, bias=NM[:], accum_out=RS[:])
                if fox:
                    act.activation(SN[:, 1:2], SN[:, 0:1], ACT.Exp, bias=NM[:]).then_inc(N["exp"], 1)
                else:
                    act.activation(OA[0:1, 0:1], NM[0:1], ACT.Identity).then_inc(N["exp"], 1)
                act.wait_ge(N["pT"], 1)
                act.activation(PC[:].rearrange("p g r -> p (g r)"), K.ps[:, 3, 0:NP * R], ACT.Identity
                               ).then_inc(N["pTe"], 1)
                act.wait_ge(N["o"], NB)
                dst = K.OT[:, :, SEQ:TOK].rearrange("p h b -> p b h")
                src = K.ps[:, 4, 0:R].rearrange("p (b h) -> p b h", b=NB)
                act.activation(OA[:].rearrange("p (b h) -> p b h", b=NB) if fox else dst, src, ACT.Identity
                               ).then_inc(N["oa"], 1)

            @block.vector
            def _(dve):
                v = K.V(dve)
                dve.wait_ge(N["qsq"], 1)
                v.do(dve.tensor_reduce(QS[:], QR[:], AX.X, ALU.add))
                v.do(dve.tensor_scalar(QS[:], QS[:], 1.0 / P, EPS, ALU.mult, ALU.add))
                rsqrt(v, QS[:], QN[:], QM[:])
                v.do(dve.tensor_scalar(QN[:], QN[:], SCALE, None, ALU.mult))
                v.do(dve.tensor_tensor(QR[:], heads(K.ps[0:NB, 0]), QN[:].unsqueeze(2).broadcast_to([NB, H, P]), ALU.mult))
                dve.tensor_tensor(QR[:], QR[:], w_bc[0:NB].unsqueeze(1).broadcast_to([NB, H, P]), ALU.mult
                                  ).then_inc(N["qr"], 1)
                dve.wait_ge(N["qb"], 16)
                for b in range(NB):
                    dve.wait_ge(N[f"k_in{b % 2}"], 16 * (NP if fox else 1) * (b // 2 + 1))
                    if b >= 1:
                        dve.wait_ge(N["sc"], b)
                    q = QB[:, b].rearrange("p h d -> p (h d)").unsqueeze(1).broadcast_to([P, NP, H * P])
                    dve.tensor_tensor(T[:].rearrange("p g h d -> p g (h d)"),
                                      KV[:, b % 2].rearrange("p g h d -> p g (h d)"), q, ALU.mult
                                      ).then_inc(N["used"], 1)
                    dve.wait_ge(N["used"], b + 1)
                    dve.tensor_reduce(SB[:, :, b], T[:], AX.X, ALU.add).then_inc(N["sc"], 1)
                dve.wait_ge(N["scT"], 1)
                if fox:
                    dve.wait_ge(N["row_in"], 64)
                    dve.wait_ge(N["lfT"], 1)
                    v.do(dve.memset(LG[:], 1.0))
                    v.do(dve.tensor_tensor_scan(CC[:], LG[:], K.ps[0:R, 2, 0:W], 0.0, ALU.mult, ALU.add))
                    v.do(dve.tensor_tensor(LN[:], LN[:], CC[:, W - 1:W], ALU.add))
                    v.do(dve.tensor_scalar(CC[:], CC[:], LN[:, 0:1], None, ALU.subtract))
                    v.do(dve.tensor_tensor(LG[:], K.ps[0:R, 1, 0:W], CC[:], ALU.subtract))
                    v.do(dve.tensor_tensor(Q3[:], Q3[:], K3[:], ALU.mult))
                    v.do(dve.tensor_reduce(SN[:, 0:1], Q3[:], AX.X, ALU.add))
                    v.do(dve.tensor_reduce(NM[:], LG[:], AX.X, ALU.max))
                    v.do(dve.tensor_tensor(NM[:], NM[:], SN[:, 0:1], ALU.max))
                    dve.tensor_scalar(NM[:], NM[:], -1.0, None, ALU.mult).then_inc(N["max"], 1)
                else:
                    v.do(dve.tensor_copy(LG[:], K.ps[0:R, 1, 0:W]))
                    dve.tensor_reduce(NM[:], LG[:], AX.X, ALU.max, negate=True).then_inc(N["max"], 1)
                dve.wait_ge(N["exp"], 1)
                if fox:
                    v.do(dve.tensor_tensor(RS[:], RS[:], SN[:, 1:2], ALU.add))
                v.do(dve.reciprocal(RS[:], RS[:]))
                dve.tensor_scalar(LG[:], LG[:], RS[:, 0:1], None, ALU.mult).then_inc(N["p"], 1)
                if fox:
                    v.do(dve.tensor_tensor(SN[:, 2:3], SN[:, 1:2], RS[:], ALU.mult))
                    dve.tensor_scalar(V3[:], V3[:], SN[:, 2:3], None, ALU.mult).then_inc(N["newv"], 1)
                    dve.wait_ge(N["newT"], 1)
                    dve.wait_ge(N["oa"], 1)
                    v.do(dve.tensor_tensor(K.OT[:, :, SEQ:TOK].rearrange("p h b -> p b h"),
                                           OA[:].rearrange("p (b h) -> p b h", b=NB),
                                           K.ps[:, 5, 0:R].rearrange("p (b h) -> p b h", b=NB), ALU.add))


def memory_norm(K, MH, ML):
    nc, i = K.nc, K.i
    with ExitStack() as c:
        sb = lambda n_, s, d=F32: c.enter_context(nc.sbuf_tensor("y" + n_, s, d))
        X = sb("_x", [P, 2, D])
        SQ = sb("_sq", [P, D])
        SS, RS, TM = sb("_ss", [P, 2]), sb("_rs", [P, 2]), sb("_tm", [P, 2])
        x_in, sq, sc = K.sem("mem_in"), K.sem("mem_sq"), K.sem("mem_scaled")
        tr, hi, lo = K.sem("mem_tr"), K.sem("mem_hi"), K.sem("mem_lo")
        with nc.Block(no_gpsimd_drain=True) as block:
            @block.sync
            def _(sp):
                for t in range(2):
                    sp.dma_start(X[:, t], i["mem_prompt"][0, t * P:(t + 1) * P]).then_inc(x_in, 16)

            @block.scalar
            def _(act):
                act.wait_ge(x_in, 32)
                for t in range(2):
                    act.activation(SQ[:], X[:, t], ACT.Square, accum_out=SS[:, t:t + 1]).then_inc(sq, 1)
                    act.wait_ge(sq, t + 1)
                for k in range(KD):
                    act.wait_ge(tr, k + 1)
                    w = K.par[:, PROW["mem_norm_w"] + k:PROW["mem_norm_w"] + k + 1]
                    act.activation(MH[:, k], K.ps[:, k % 4, 0:MEM], ACT.Identity, scale=w).then_inc(hi, 1)

            @block.vector
            def _(dve):
                v = K.V(dve)
                dve.wait_ge(sq, 2)
                v.do(dve.tensor_scalar(SS[:], SS[:], 1.0 / D, EPS, ALU.mult, ALU.add))
                rsqrt(v, SS[:], RS[:], TM[:])
                for t in range(2):
                    dve.tensor_scalar(X[:, t], X[:, t], RS[:, t:t + 1], None, ALU.mult).then_inc(sc, 1)
                for k in range(KD):
                    dve.wait_ge(hi, k + 1)
                    w = K.par[:, PROW["mem_norm_w"] + k:PROW["mem_norm_w"] + k + 1]
                    dve.scalar_tensor_tensor(ML[:, k], K.ps[:, k % 4, 0:MEM], w, MH[:, k].bitcast(F32), ALU.mult,
                                             ALU.subtract).then_inc(lo, 1)

            @block.tensor
            def _(pe):
                pe.wait_ge(sc, 2)
                for k in range(KD):
                    if k >= 4:
                        pe.wait_ge(lo, k - 3)
                    for t in range(2):
                        last = pe.transpose(K.ps[:, k % 4, t * P:(t + 1) * P], X[:, t, k * P:(k + 1) * P], K.ident[:])
                    last.then_inc(tr, 1)


def build(nc, ins, outs):
    with ExitStack() as ctx:
        K = Kernel(nc, ins, outs, ctx)
        dram = lambda name, shape: nc.dram_tensor(name, shape, F32).ap()
        K.d_rows = dram("rows_g_c_beta", (3, H, SEQ))
        K.d_ab = dram("decode_alpha_beta_rows", (2, H, NB))
        K.d_lf = dram("decode_logf", (NB, H))
        K.d_qk = dram("decode_qk", (2, NB, H, P))
        K.d_q = dram("decode_q", (NB, H, P))

        at = {}

        def plan(name, n, label=None):
            at[label or name] = len(K.tiles)
            K.plan_in(name, n)

        def plan_merge(n):
            at[f"merge{n}"] = len(K.tiles)
            wb = ins["w_branch"][0, n]
            for d in range(KD):
                a = OFF["gate"] + n * D + d * P
                K.plan(ins["w_in"][0, :, a:a + P].rearrange("(k p) c -> p k c", p=P), KD, "act")
                K.plan(wb[:, d * P:(d + 1) * P].rearrange("(k p) c -> p k c", p=P), 4, "dve")

        plan("dn_qkv", 12)
        plan("dn_z", 4)
        plan_merge(0)
        plan("lru_x", 4)
        plan("lru_g", 4)
        plan_merge(1)
        plan("fk", 4)
        plan("fv", 4)
        plan("fq", 4)
        plan("fg", 4)
        plan_merge(2)
        at["mem_kv"] = len(K.tiles)
        for e in range(8):
            K.plan(ins["w_mem_kv"][0, :, e * P:(e + 1) * P].rearrange("(k p) c -> p k c", p=P), KD, "act")
        plan("mq", 4)
        plan("mg", 4)
        plan_merge(3)
        at["w_out"] = len(K.tiles)
        for e in range(KD):
            K.plan(ins["w_out"][0, :, e * P:(e + 1) * P].rearrange("(k p) c -> p k c", p=P), KD, "act")

        def branch_end(t_gate, name, n, tag):
            with ExitStack() as c:
                K.brH = c.enter_context(nc.sbuf_tensor(tag + "_brH", [P, H, TOK], F32R))
                K.brL = c.enter_context(nc.sbuf_tensor(tag + "_brL", [P, H, TOK], F32R))
                gate_branch(K, t_gate, name, K.OT, tag)
                merge_branch(K, at[f"merge{n}"], n)
            K.stage_ends()

        setup(K)
        small_columns(K)
        conv_tiles(K, at["dn_qkv"], 12, "dn_conv_w", 0, K.hpar, True,
                   lambda j: K.OT[:, j] if j < H else K.merged[:, j - H], "ca", "dn_conv", "dn_conv_s")
        delta_rule(K)
        delta_decode(K)
        branch_end(at["dn_z"], "dn_z", 0, "ga")
        conv_tiles(K, at["lru_x"], 4, "lru_conv_w", 12, K.par, False, lambda j: K.OT[:, j], "cb", "lru_conv",
                   "lru_conv_s")
        lru(K)
        branch_end(at["lru_g"], "lru_g", 1, "gb")
        sizes = [P] * TT8 + [NB]
        rows = lambda p, s: [outs[p][0, 0, t * P:(t + 1) * P] for t in range(TT8)] + [outs[s][0, :, 0]]
        with ExitStack() as c:
            sb = lambda n_, s: c.enter_context(nc.sbuf_tensor(n_, s, F32))
            KX = sb("fox_kT", [P, H, TOK])
            VR = sb("fox_v_rows", [P, TT8 + 1, H, P])
            RQ = sb("fox_rq", [P, H, TT8])
            with nc.sbuf_tensor("fox_k_rows", [P, TT8 + 1, H, P], F32) as KR:
                plain_tiles(K, at["fk"], 4, BROW["fk"], KX, "fk")
                to_rows(K, KX, KR, sizes, "fkr", norm=K.knw, back=(KX, K.par[:, PROW["fox_qn_w"]:PROW["fox_qn_w"] + 1]),
                        stores=rows("fox_k", "fox_k_s"))
            with nc.sbuf_tensor("fox_vT", [P, H, TOK], F32) as VX:
                plain_tiles(K, at["fv"], 4, BROW["fv"], VX, "fv")
                to_rows(K, VX, VR, sizes, "fvr", stores=rows("fox_v", "fox_v_s"))
            plain_tiles(K, at["fq"], 4, BROW["fq"], K.OT, "fq")
            query_norms(K, RQ, "fq")
            attend(K, KX, VR, RQ, "fa", True)
        attend_decode(K, "fd", True)
        branch_end(at["fg"], "fg", 2, "gc")
        with ExitStack() as c:
            sb = lambda n_, s, d=F32: c.enter_context(nc.sbuf_tensor(n_, s, d))
            KX, VX = sb("mem_kT", [P, H, MEM]), sb("mem_vT", [P, H, MEM])
            VR = sb("mem_v_rows", [P, 2, H, P])
            RQ = sb("mem_rq", [P, H, TT8])
            with ExitStack() as c2:
                MH = c2.enter_context(nc.sbuf_tensor("memH", [P, KD, MEM], F32R))
                ML = c2.enter_context(nc.sbuf_tensor("memL", [P, KD, MEM], F32R))
                KR = c2.enter_context(nc.sbuf_tensor("mem_k_rows", [P, 2, H, P], F32))
                memory_norm(K, MH, ML)
                t = at["mem_kv"]
                plain_tiles(K, t, 4, None, KX, "mk", x=(MH, ML), cols=MEM)
                plain_tiles(K, t + 4, 4, None, VX, "mv", x=(MH, ML), cols=MEM)
                mrows = lambda p: [outs[p][0, 0, t_ * P:(t_ + 1) * P] for t_ in range(2)]
                to_rows(K, KX, KR, [P, P], "mkr", norm=K.mknw, back=(KX, K.par[:, PROW["mem_qn_w"]:PROW["mem_qn_w"] + 1]),
                        stores=mrows("mem_k"))
                to_rows(K, VX, VR, [P, P], "mvr", stores=mrows("mem_v"))
            plain_tiles(K, at["mq"], 4, BROW["mq"], K.OT, "mq")
            query_norms(K, RQ, "mq")
            attend(K, KX, VR, RQ, "ma", False)
        attend_decode(K, "md", False)
        branch_end(at["mg"], "mg", 3, "gd")
        K.OT_space.close()
        output(K, at["w_out"])


INS = ["x_prompt", "x_sample", "cache_fox_k", "cache_fox_v", "cache_fox_logf", "cache_mem_k", "cache_mem_v",
       "state_dn", "state_dn_conv", "state_lru_h", "state_lru_conv", "page_table", "mem_prompt", "norm_w", "w_in",
       "b_in", "dn_conv_w", "dn_A_log", "dn_dt_bias", "dn_onorm_w", "lru_conv_w", "lru_conv_b", "lru_w_r",
       "lru_b_r", "lru_w_i", "lru_b_i", "lru_lambda", "fox_qn_w", "fox_kn_w", "mem_norm_w", "w_mem_kv",
       "mem_qn_w", "mem_kn_w", "w_branch", "w_out"]
OUTS = [("y", (1, SEQ, D)), ("y_s", (NB, 1, D)),
        ("fox_k", (1, 1, SEQ, H, P)), ("fox_v", (1, 1, SEQ, H, P)), ("fox_logf", (1, 1, SEQ, H)),
        ("mem_k", (1, 1, MEM, H, P)), ("mem_v", (1, 1, MEM, H, P)), ("dn_state", (1, 1, H, P, P)),
        ("dn_conv", (1, 1, 3, 1536)), ("lru_h", (1, 1, BW)), ("lru_conv", (1, 1, 3, BW)),
        ("fox_k_s", (1, NB, 1, H, P)), ("fox_v_s", (1, NB, 1, H, P)), ("fox_logf_s", (1, NB, 1, H)),
        ("dn_state_s", (1, NB, H, P, P)), ("dn_conv_s", (1, NB, 3, 1536)), ("lru_h_s", (1, NB, BW)),
        ("lru_conv_s", (1, NB, 3, BW))]


def kernel(**inputs):
    import concourse.bacc as bacc
    import numpy as np
    from concourse.bass_utils import run_bass_kernel_spmd

    nc = bacc.Bacc("TRN2", target_bir_lowering=False, num_devices=1)
    arrays, ins, outs = {}, {}, {}
    for name in INS:
        a = np.ascontiguousarray(inputs[name])
        arrays["in_" + name] = a
        ins[name] = nc.dram_tensor("in_" + name, a.shape, mybir.dt.from_np(a.dtype), kind="ExternalInput").ap()
    for name, shape in OUTS:
        outs[name] = nc.dram_tensor("out_" + name, shape, F32, kind="ExternalOutput").ap()
    build(nc, ins, outs)
    r = run_bass_kernel_spmd(nc, [arrays], core_ids=[0])
    return tuple(r.results[0]["out_" + name] for name, _ in OUTS)
```

```python
from contextlib import ExitStack

import concourse.bass as bass
from concourse import mybir

F32 = mybir.dt.float32
F32R = mybir.dt.float32r
I32 = mybir.dt.int32
I8 = mybir.dt.int8
ALU = mybir.AluOpType
ACT = mybir.ActivationFunctionType
AX = mybir.AxisListType

P = 128
D = 1024
KD = D // P
SEQ = 1024
NB = 8
TOK = SEQ + NB
G3 = TOK // 3
TT8 = SEQ // P
H = 4
BW = 512
CONV = 4
CH = 128
NCH = SEQ // CH
MEM = 256
PAGES = 4
PAGE = 128
PAST = PAGES * PAGE
EPS = 1e-6
LRU_C = 8.0
SCALE = float(P) ** -0.5
NEG = -1e30
RSQRT_SEED = float(0x5F3759DF)

OFF = {}
_o = 0
for _n, _w in (("dn_qkv", 1536), ("dn_z", 512), ("dn_b", 4), ("dn_a", 4), ("lru_x", 512), ("lru_g", 512),
               ("fq", 512), ("fk", 512), ("fv", 512), ("ff", 4), ("fg", 512), ("mq", 512), ("mg", 512),
               ("gate", 4096)):
    OFF[_n] = _o
    _o += _w
BROW = {}
_r = 0
for _n, _w in (("dn_qkv", 12), ("dn_z", 4), ("lru_x", 4), ("lru_g", 4), ("fq", 4), ("fk", 4), ("fv", 4),
               ("fg", 4), ("mq", 4), ("mg", 4), ("gate", 32)):
    BROW[_n] = _r
    _r += _w
NBROW = _r
PROW = {}
_r = 0
for _n, _w in (("dn_conv_w", 48), ("lru_conv_w", 16), ("lru_conv_b", 4), ("lru_b_r", 4), ("lru_b_i", 4),
               ("lru_lambda", 4), ("fox_qn_w", 1), ("mem_qn_w", 1), ("dn_onorm_w", 1), ("norm_w", 8),
               ("mem_norm_w", 8)):
    PROW[_n] = _r
    _r += _w
NPROW = _r


class Steps:

    def __init__(self, eng, sem, state):
        self.eng, self.sem, self.state = eng, sem, state

    def step(self, ins):
        ins.then_inc(self.sem, 1)
        self.state[0] += 1

    def wait(self):
        self.eng.wait_ge(self.sem, self.state[0])

    def do(self, ins):
        self.step(ins)
        self.wait()


def heads(ap):
    return ap.rearrange("p (h d) -> p h d", h=H)


def rsqrt(v, x, y, t):
    eng = v.eng
    yi, yf = y.bitcast(I32), y
    v.do(eng.tensor_scalar(yi, x.bitcast(I32), 1, None, ALU.logical_shift_right))
    v.do(eng.tensor_scalar(yi, yi, -1.0, RSQRT_SEED, ALU.mult, ALU.add))
    for _ in range(3):
        v.do(eng.tensor_tensor(t, yf, yf, ALU.mult))
        v.do(eng.scalar_tensor_tensor(t, t, -0.5, x, ALU.mult, ALU.mult))
        v.do(eng.scalar_tensor_tensor(yf, t, 1.5, yf, ALU.add, ALU.mult))


def log1p_exp(v, z, u, s, s2, acc):
    eng = v.eng
    v.do(eng.tensor_scalar(s, u, 2.0, None, ALU.add))
    v.do(eng.reciprocal(s, s))
    v.do(eng.tensor_tensor(s, s, u, ALU.mult))
    v.do(eng.tensor_tensor(s2, s, s, ALU.mult))
    v.do(eng.tensor_scalar(acc, s2, 1.0 / 17, None, ALU.mult))
    for c in (15, 13, 11, 9, 7, 5, 3):
        v.do(eng.scalar_tensor_tensor(acc, acc, 1.0 / c, s2, ALU.add, ALU.mult))
    v.do(eng.scalar_tensor_tensor(acc, acc, 1.0, s, ALU.add, ALU.mult))
    v.do(eng.tensor_scalar(s, z, 0.0, None, ALU.max))
    v.do(eng.scalar_tensor_tensor(acc, acc, 2.0, s, ALU.mult, ALU.add))


class Kernel:

    def __init__(self, nc, ins, outs, ctx):
        self.nc, self.i, self.o, self.ctx = nc, ins, outs, ctx
        sb = lambda n, s, d=F32: ctx.enter_context(nc.sbuf_tensor(n, s, d))
        sem = lambda n: ctx.enter_context(nc.semaphore(n))
        self.hH, self.hL = sb("hH", [P, KD, TOK], F32R), sb("hL", [P, KD, TOK], F32R)
        self.slots_at = nc.sbuf_base
        self.raw = sb("w_raw", [P, 2, KD, P])
        self.wH, self.wL = sb("wH", [P, 2, KD, P], F32R), sb("wL", [P, 2, KD, P], F32R)
        self.ident = sb("ident", [P, P])
        self.ones = sb("ones", [P, 1])
        self.bias, self.hbias = sb("bias", [P, NBROW]), sb("half_bias", [P, NBROW])
        self.par, self.hpar = sb("par", [P, NPROW]), sb("half_par", [P, NPROW])
        self.TK = sb("token_scalars", [P, TT8, 3, H])
        self.knw, self.mknw = sb("fox_kn_bc", [P, P]), sb("mem_kn_bc", [P, P])
        self.qnw, self.mqnw = sb("fox_qn_bc", [P, P]), sb("mem_qn_bc", [P, P])
        self.alpha = sb("decode_alpha_beta", [P, 2, H, NB])
        self.convs = sb("conv_states", [P, 16, 32])
        self.ps = ctx.enter_context(nc.psum_tensor("ps", [P, 8, 512], F32))
        self.merged = sb("merged", [P, KD, TOK])
        self.OT_space = ExitStack()
        self.OT = self.OT_space.enter_context(nc.sbuf_tensor("branch_in", [P, H, TOK], F32))
        self.w_loaded = [sem("w_loaded0"), sem("w_loaded1")]
        self.w_hi, self.w_lo = sem("w_hi"), sem("w_lo")
        self.tile_done = sem("tile_done")
        self.evac_act, self.evac_dve = sem("evac_act"), sem("evac_dve")
        self.tiles = []
        self.at_load = self.at_hi = self.at_lo = 0
        self.v_sem, self.v_n = sem("vector_step"), [0]
        self.a_sem, self.a_n = sem("scalar_step"), [0]
        self.p_sem, self.p_n = sem("pool_step"), [0]
        self.stored, self.n_stored = sem("stored"), 0
        self.y_out = [sem("y_out0"), sem("y_out1")]
        self.stage = []

    def sem(self, name):
        s = self.nc.alloc_semaphore(name=name)
        self.stage.append(s)
        return s

    def stage_ends(self):
        self.nc.clear_and_free_semaphores(self.stage)
        self.nc.all_engine_barrier()
        self.stage = []

    def borrowed(self, name, slot, shape):
        return self.nc.alloc_sbuf_tensor_at(name, shape, F32, offset=self.slots_at + slot * 2 * KD * P * 4)

    def V(self, eng):
        return Steps(eng, self.v_sem, self.v_n)

    def A(self, eng):
        return Steps(eng, self.a_sem, self.a_n)

    def G(self, eng):
        return Steps(eng, self.p_sem, self.p_n)

    def store(self, eng, dst, src):
        eng.dma_start(dst, src).then_inc(self.stored, 16)
        self.n_stored += 16

    def plan(self, src, nk, evac):
        self.tiles.append((src, nk, evac))

    def plan_in(self, name, n, evac="act"):
        for t in range(n):
            a = OFF[name] + t * P
            self.plan(self.i["w_in"][0, :, a:a + P].rearrange("(k p) c -> p k c", p=P), KD, evac)

    def loads(self, sp, upto):
        for t in range(self.at_load, min(upto, len(self.tiles))):
            src, nk, _ = self.tiles[t]
            if t >= 2:
                sp.wait_ge(self.w_lo, t - 1)
            sp.dma_start(self.raw[:, t % 2, 0:nk], src).then_inc(self.w_loaded[t % 2], 16)
            self.at_load = t + 1

    def split_hi(self, act, upto):
        for t in range(self.at_hi, min(upto, len(self.tiles))):
            nk = self.tiles[t][1]
            act.wait_ge(self.w_loaded[t % 2], 16 * (t // 2 + 1))
            if t >= 2:
                act.wait_ge(self.tile_done, t - 1)
            act.activation(self.wH[:, t % 2, 0:nk], self.raw[:, t % 2, 0:nk], ACT.Identity).then_inc(self.w_hi, 1)
            self.at_hi = t + 1

    def split_lo(self, pool, upto):
        for t in range(self.at_lo, min(upto, len(self.tiles))):
            nk = self.tiles[t][1]
            pool.wait_ge(self.w_hi, t + 1)
            pool.tensor_tensor(self.wL[:, t % 2, 0:nk], self.raw[:, t % 2, 0:nk],
                               self.wH[:, t % 2, 0:nk].bitcast(F32), ALU.subtract).then_inc(self.w_lo, 1)
            self.at_lo = t + 1

    def psum(self, t):
        return self.ps[:, 3 * (t % 2):3 * (t % 2) + 3, 0:G3]

    def emptied(self, t):
        kind = self.tiles[t][2]
        n = sum(1 for x in self.tiles[:t + 1] if x[2] == kind)
        return (self.evac_act if kind == "act" else self.evac_dve), n

    def project(self, pe, t, xH, xL, groups=3, cols=None, meanwhile=None):
        _, nk, _ = self.tiles[t]
        pe.wait_ge(self.w_lo, t + 1)
        if t >= 2:
            pe.wait_ge(*self.emptied(t - 2))
        width = TOK // 3 if groups == 3 else cols
        for k in range(nk):
            for n, (w, x) in enumerate(((self.wH, xH), (self.wH, xL), (self.wL, xH))):
                for g in range(groups):
                    last = pe.matmul(self.ps[:, 3 * (t % 2) + g, 0:width], w[:, t % 2, k],
                                     x[:, k, g * width:(g + 1) * width],
                                     start=(k == 0 and n == 0), stop=(k == nk - 1 and n == 2))
            if k == nk - 1:
                last.then_inc(self.tile_done, 1)
            if meanwhile:
                meanwhile(k)


def setup(K):
    nc, i = K.nc, K.i
    with ExitStack() as c:
        sb = lambda n, s, d=F32: c.enter_context(nc.sbuf_tensor(n, s, d))
        X = sb("x_rows", [P, TT8 + 1, D])
        SQ = sb("x_square", [P, D])
        SS, RS, TM = sb("x_ss", [P, 9]), sb("x_rstd", [P, 9]), sb("x_tm", [P, 9])
        BR, PR = sb("bias_rows", [NBROW, P]), sb("par_rows", [NPROW, P])
        ST = sb("state_rows", [24, 1536])
        SL = sb("lru_state_rows", [32, 512])
        x_in, par_in = K.sem("x_in"), K.sem("par_in")
        made, squared, scaled = K.sem("constants_made"), K.sem("x_squared"), K.sem("x_scaled")
        tabT, tab = K.sem("tables_transposed"), K.sem("tables_ready")
        filled = K.sem("x_ss_filled")
        xT, hi, lo = K.sem("x_transposed"), K.sem("h_hi"), K.sem("h_lo")
        par_dmas = []

        def par(dst, src):
            par_dmas.append((dst, src))

        rows = lambda ap: ap.rearrange("(r p) -> r p", p=P)
        segments = [("dn_qkv", 16), ("lru_x", 20), ("fg", 4), ("mq", 40)]
        b = i["b_in"][0]
        for name, n in segments:
            par(BR[BROW[name]:BROW[name] + n, :], rows(b[OFF[name]:OFF[name] + n * P]))
        par(PR[PROW["dn_conv_w"]:PROW["dn_conv_w"] + 48, :], i["dn_conv_w"][0].rearrange("j (t p) -> (j t) p", p=P))
        par(PR[PROW["lru_conv_w"]:PROW["lru_conv_w"] + 16, :], i["lru_conv_w"][0].rearrange("j (t p) -> (j t) p", p=P))
        for name, n in (("lru_conv_b", 4), ("lru_b_r", 4), ("lru_b_i", 4), ("lru_lambda", 4), ("fox_qn_w", 1),
                        ("mem_qn_w", 1), ("dn_onorm_w", 1), ("norm_w", 8), ("mem_norm_w", 8)):
            par(PR[PROW[name]:PROW[name] + n, :], rows(i[name][0]))
        par(ST[:], i["state_dn_conv"][0].rearrange("b j c -> (b j) c"))
        par(SL[0:24, :], i["state_lru_conv"][0].rearrange("b j c -> (b j) c"))
        par(SL[24:32, :], i["state_lru_h"][0])
        for dst, name in ((K.knw, "fox_kn_w"), (K.mknw, "mem_kn_w"), (K.qnw, "fox_qn_w"), (K.mqnw, "mem_qn_w")):
            par(dst[:], i[name][0:1].broadcast_to([P, P]))

        with nc.Block(no_gpsimd_drain=True) as block:
            @block.sync
            def _(sp):
                for t in range(TT8):
                    sp.dma_start(X[:, t], i["x_prompt"][0, t * P:(t + 1) * P]).then_inc(x_in, 16)
                sp.dma_start(X[0:NB, TT8], i["x_sample"][:, 0]).then_inc(x_in, 16)
                K.loads(sp, 2)
                for src, dst in (("state_dn_conv", "dn_conv_s"), ("state_lru_conv", "lru_conv_s")):
                    K.store(sp, K.o[dst][0, :, 0:2], i[src][0, :, 1:3])

            @block.gpsimd
            def _(pool):
                pool.memset(K.ident[:], 0.0).then_inc(made, 1)
                pool.wait_ge(made, 1)
                pool.affine_select(out=K.ident[:], in_=K.ident[:], compare_op=ALU.not_equal, fill=1.0, base=0,
                                   pattern=[[-1, P]], channel_multiplier=1).then_inc(made, 1)
                pool.memset(K.ones[:], 1.0).then_inc(made, 1)
                K.split_lo(pool, 1)

            @block.scalar
            def _(act):
                for dst, src in par_dmas:
                    act.dma_start(dst, src).then_inc(par_in, 16)
                act.wait_ge(x_in, 16 * 9)
                act.wait_ge(filled, 1)
                a = K.A(act)
                for t in range(9):
                    n = P if t < TT8 else NB
                    act.activation(SQ[0:n], X[0:n, t], ACT.Square, accum_out=SS[0:n, t:t + 1]).then_inc(squared, 1)
                    act.wait_ge(squared, t + 1)
                K.split_hi(act, 1)
                act.wait_ge(tabT, 1)
                a.do(act.activation(K.bias[:], K.ps[:, 6, 0:NBROW], ACT.Identity))
                a.do(act.activation(K.par[:], K.ps[:, 6, 128:128 + NPROW], ACT.Identity))
                act.activation(K.hbias[:], K.bias[:], ACT.Identity, scale=0.5).then_inc(tab, 1)
                act.activation(K.hpar[:], K.par[:], ACT.Identity, scale=0.5).then_inc(tab, 1)
                act.activation(K.convs[:, 0:12, 0:24], K.ps[:, 7, 0:12 * 24].rearrange("p (t r) -> p t r", t=12),
                               ACT.Identity).then_inc(tab, 1)
                act.activation(K.convs[:, 12:16, :], K.ps[:, 7, 288:288 + 128].rearrange("p (t r) -> p t r", t=4),
                               ACT.Identity).then_inc(tab, 1)
                for k in range(KD):
                    q = 3 * (k % 2)
                    act.wait_ge(xT, k + 1)
                    w = K.par[:, PROW["norm_w"] + k:PROW["norm_w"] + k + 1]
                    act.activation(K.hH[:, k, 0:SEQ].rearrange("p (a b) -> p a b", a=2), K.ps[:, q:q + 2, :],
                                   ACT.Identity, scale=w)
                    act.activation(K.hH[:, k, SEQ:TOK], K.ps[:, q + 2, 0:NB], ACT.Identity, scale=w).then_inc(hi, 1)

            @block.vector
            def _(dve):
                v = K.V(dve)
                dve.memset(SS[:], 1.0).then_inc(filled, 1)
                dve.wait_ge(squared, 9)
                v.do(dve.tensor_scalar(SS[:], SS[:], 1.0 / D, EPS, ALU.mult, ALU.add))
                rsqrt(v, SS[:], RS[:], TM[:])
                for t in range(9):
                    n = P if t < TT8 else NB
                    dve.tensor_scalar(X[0:n, t], X[0:n, t], RS[0:n, t:t + 1], None, ALU.mult).then_inc(scaled, 1)
                for k in range(KD):
                    q = 3 * (k % 2)
                    dve.wait_ge(hi, k + 1)
                    w = K.par[:, PROW["norm_w"] + k:PROW["norm_w"] + k + 1]
                    dve.scalar_tensor_tensor(
                        K.hL[:, k, 0:SEQ].rearrange("p (a b) -> p a b", a=2), K.ps[:, q:q + 2, :], w,
                        K.hH[:, k, 0:SEQ].bitcast(F32).rearrange("p (a b) -> p a b", a=2), ALU.mult, ALU.subtract)
                    dve.scalar_tensor_tensor(K.hL[:, k, SEQ:TOK], K.ps[:, q + 2, 0:NB], w,
                                             K.hH[:, k, SEQ:TOK].bitcast(F32), ALU.mult,
                                             ALU.subtract).then_inc(lo, 1)

            @block.tensor
            def _(pe):
                pe.wait_ge(made, 3)
                pe.wait_ge(par_in, 16 * len(par_dmas))
                pe.transpose(K.ps[:, 6, 0:NBROW], BR[:], K.ident[0:NBROW, 0:NBROW])
                pe.transpose(K.ps[:, 6, 128:128 + NPROW], PR[:], K.ident[0:NPROW, 0:NPROW])
                for t in range(12):
                    pe.transpose(K.ps[:, 7, 24 * t:24 * t + 24], ST[:, t * P:(t + 1) * P], K.ident[0:24, 0:24])
                for t in range(4):
                    last = pe.transpose(K.ps[:, 7, 288 + 32 * t:320 + 32 * t], SL[:, t * P:(t + 1) * P],
                                        K.ident[0:32, 0:32])
                last.then_inc(tabT, 1)
                pe.wait_ge(scaled, 9)
                for k in range(KD):
                    q = 3 * (k % 2)
                    if k >= 2:
                        pe.wait_ge(lo, k - 1)
                    for t in range(TT8):
                        pe.transpose(K.ps[:, q + t // 4, (t % 4) * P:(t % 4 + 1) * P], X[:, t, k * P:(k + 1) * P],
                                     K.ident[:])
                    pe.transpose(K.ps[:, q + 2, 0:NB], X[0:NB, TT8, k * P:(k + 1) * P],
                                 K.ident[0:NB, 0:NB]).then_inc(xT, 1)


def small_columns(K):
    nc, i = K.nc, K.i
    DNA, FF, DNB = 0, 32, 64
    M = 96
    with ExitStack() as c:
        sb = lambda n, s, d=F32: c.enter_context(nc.sbuf_tensor(n, s, d))
        W = sb("sw", [P, KD, M])
        WH, WL = sb("swH", [P, KD, M], F32R), sb("swL", [P, KD, M], F32R)
        col = sb("sw_cols", [M, 8])
        Z, T1, U, S, S2, SP = (sb(n, [M, TOK]) for n in ("sz", "st1", "su", "ss", "ss2", "ssp"))
        SC, MK = sb("s_scan", [M, SEQ]), sb("s_mask", [M, SEQ])
        EX = sb("s_exp", [M, NB])
        VT = sb("s_value_rows", [P, TT8 + 1, M])
        loaded, prep, split = K.sem("sw_loaded"), K.sem("sw_prepared"), K.sem("sw_split")
        done, z, t1, u = K.sem("sw_done"), K.sem("sz_ready"), K.sem("st1_ready"), K.sem("su_ready")
        val, beta, tr, out = K.sem("s_values"), K.sem("s_beta"), K.sem("s_transposed"), K.sem("s_out")
        K.rows_out = K.sem("rows_out")
        with nc.Block(no_gpsimd_drain=True) as block:
            @block.gpsimd
            def _(pool):
                g = K.G(pool)
                pool.memset(W[:], 0.0)
                pool.memset(col[:], 0.0)
                pool.memset(MK[:], 1.0).then_inc(prep, 1)
                pool.wait_ge(prep, 1)
                pool.memset(MK[0:32].rearrange("p (a b) -> p a b", b=CH)[:, :, 0:1], 0.0)
                pool.memset(col[0:32, 3:4], 1.0)
                pool.memset(col[32:64, 3:4], -1.0)
                pool.memset(col[64:96, 3:4], -1.0).then_inc(prep, 1)

            @block.sync
            def _(sp):
                sp.wait_ge(prep, 2)
                for name, r in (("dn_a", DNA), ("ff", FF), ("dn_b", DNB)):
                    a = OFF[name]
                    sp.dma_start(W[:, :, r:r + 4], i["w_in"][0, :, a:a + 4].rearrange("(k p) c -> p k c", p=P)
                                 ).then_inc(loaded, 16)
                    sp.dma_start(col[r:r + 4, 0:1], i["b_in"][0, a:a + 4].rearrange("(c a) -> c a", a=1)
                                 ).then_inc(loaded, 16)
                sp.dma_start(col[0:4, 1:2], i["dn_dt_bias"][0].rearrange("(c a) -> c a", a=1)).then_inc(loaded, 16)
                sp.dma_start(col[0:4, 2:3], i["dn_A_log"][0].rearrange("(c a) -> c a", a=1)).then_inc(loaded, 16)
                sp.wait_ge(out, 1)
                for t in range(TT8):
                    K.store(sp, K.o["fox_logf"][0, 0, t * P:(t + 1) * P], VT[:, t, FF:FF + 4])
                K.store(sp, K.o["fox_logf_s"][0, :, 0], VT[0:NB, TT8, FF:FF + 4])
                sp.dma_start(K.d_rows[0], SC[DNA:DNA + 4]).then_inc(K.rows_out, 16)
                sp.dma_start(K.d_rows[1], SC[FF:FF + 4]).then_inc(K.rows_out, 16)
                sp.dma_start(K.d_rows[2], SC[DNB:DNB + 4]).then_inc(K.rows_out, 16)
                sp.dma_start(K.d_ab[0], EX[DNA:DNA + 4]).then_inc(K.rows_out, 16)
                sp.dma_start(K.d_ab[1], EX[DNB:DNB + 4]).then_inc(K.rows_out, 16)
                sp.dma_start(K.d_lf, VT[0:NB, TT8, FF:FF + 4]).then_inc(K.rows_out, 16)
                sp.wait_ge(K.rows_out, 96)
                sp.dma_start(K.alpha[:].rearrange("p a h b -> p (a h b)"),
                             K.d_ab.rearrange("a h b -> (a h b)").unsqueeze(0).broadcast_to([P, 64])
                             ).then_inc(K.rows_out, 16)
                sp.wait_ge(K.rows_out, 112)
                sp.wait_ge(K.stored, K.n_stored)
                K.loads(sp, 2)

            @block.scalar
            def _(act):
                a = K.A(act)
                act.wait_ge(loaded, 16 * 8)
                a.do(act.activation(WH[:], W[:], ACT.Identity))
                act.activation(col[:, 5:6], col[:, 2:3], ACT.Exp).then_inc(split, 1)
                act.wait_ge(done, 1)
                act.wait_ge(split, 3)
                act.activation(Z[:].rearrange("p (a b) -> p a b", a=3), K.ps[0:M, 0:3, 0:G3], ACT.Identity,
                               scale=col[:, 3:4], bias=col[:, 4:5]).then_inc(z, 1)
                act.wait_ge(t1, 1)
                act.activation(U[:], T1[:], ACT.Exp).then_inc(u, 1)
                act.wait_ge(val, 2)
                act.activation(SC[DNB:DNB + 32], SP[DNB:DNB + 32, 0:SEQ], ACT.Exp)
                act.activation(EX[:], SP[:, SEQ:TOK], ACT.Exp).then_inc(beta, 1)
                act.wait_ge(tr, 1)
                for t in range(TT8):
                    act.activation(K.TK[:, t], K.ps[:, t // 4, (t % 4) * M:(t % 4 + 1) * M].rearrange(
                        "p (g m) -> p g m", g=3)[:, :, 0:H], ACT.Identity)
                act.activation(VT[:, 0:TT8].rearrange("p (a b) m -> p a b m", a=2),
                               K.ps[:, 2:4, 0:4 * M].rearrange("p a (b m) -> p a b m", m=M), ACT.Identity)
                act.activation(VT[0:NB, TT8], K.ps[0:NB, 4, 0:M], ACT.Identity).then_inc(out, 1)

            @block.vector
            def _(dve):
                v = K.V(dve)
                dve.wait_ge(split, 1)
                dve.tensor_tensor(WL[:], W[:], WH[:].bitcast(F32), ALU.subtract).then_inc(split, 1)
                v.do(dve.scalar_tensor_tensor(col[:, 4:5], col[:, 0:1], col[:, 3:4], col[:, 1:2], ALU.mult, ALU.add))
                dve.tensor_scalar(col[:, 5:6], col[:, 5:6], -1.0, None, ALU.mult).then_inc(split, 1)
                dve.wait_ge(split, 3)
                dve.wait_ge(z, 1)
                v.do(dve.tensor_scalar(T1[:], Z[:], -1.0, None, ALU.mult))
                dve.tensor_tensor(T1[:], T1[:], Z[:], ALU.min).then_inc(t1, 1)
                dve.wait_ge(u, 1)
                log1p_exp(v, Z[:], U[:], S[:], S2[:], SP[:])
                dve.tensor_scalar(SP[:], SP[:], col[:, 5:6], None, ALU.mult).then_inc(val, 1)
                dve.wait_ge(val, 1)
                dve.tensor_tensor_scan(SC[:], MK[:], SP[:, 0:SEQ], 0.0, ALU.mult, ALU.add).then_inc(val, 1)

            @block.tensor
            def _(pe):
                pe.wait_ge(split, 2)
                for k in range(KD):
                    for n, (w, x) in enumerate(((WH, K.hH), (WH, K.hL), (WL, K.hH))):
                        for g in range(3):
                            last = pe.matmul(K.ps[0:M, g, 0:G3], w[:, k], x[:, k, g * G3:(g + 1) * G3],
                                             start=(k == 0 and n == 0), stop=(k == KD - 1 and n == 2))
                last.then_inc(done, 1)
                pe.wait_ge(beta, 1)
                for t in range(TT8):
                    pe.transpose(K.ps[:, t // 4, (t % 4) * M:(t % 4 + 1) * M], SC[:, t * P:(t + 1) * P],
                                 K.ident[0:M, 0:M])
                    pe.transpose(K.ps[:, 2 + t // 4, (t % 4) * M:(t % 4 + 1) * M], SP[:, t * P:(t + 1) * P],
                                 K.ident[0:M, 0:M])
                pe.transpose(K.ps[0:NB, 4, 0:M], SP[:, SEQ:TOK], K.ident[0:M, 0:M]).then_inc(tr, 1)


def conv_tiles(K, t0, n, name, state0, par, silu, OUT, tag, prompt_out, sample_out):
    nc = K.nc
    PAD = CONV - 1
    taps = PROW[name]
    with ExitStack() as c:
        sb = lambda n_, s, d=F32: c.enter_context(nc.sbuf_tensor(tag + n_, s, d))
        XI = sb("_in", [P, 2, PAD + TOK])
        TH = sb("_th", [P, 2, TOK]) if silu else None
        XL = sb("_last", [P, n, PAD + NB])
        XR = sb("_last_rows", [PAD + NB, n * P])
        padded, conv, th, fin = (K.sem(tag + x) for x in ("_padded", "_conv", "_tanh", "_silu"))
        last_cols, last_tr, last_ev = (K.sem(tag + x) for x in ("_lastc", "_lastt", "_laste"))

        def tap(j, t):
            return par[:, taps + j * n + t:taps + j * n + t + 1]

        with nc.Block(no_gpsimd_drain=True) as block:
            @block.sync
            def _(sp):
                K.loads(sp, t0 + n + 2)
                sp.wait_ge(last_ev, 1)
                K.store(sp, K.o[prompt_out][0, 0], XR[0:PAD])
                K.store(sp, K.o[sample_out][0, :, 2], XR[PAD:PAD + NB])
                sp.wait_ge(K.stored, K.n_stored)

            @block.gpsimd
            def _(pool):
                pool.memset(XI[:, :, 0:PAD], 0.0).then_inc(padded, 1)
                K.split_lo(pool, t0 + n + 1)

            @block.scalar
            def _(act):
                for j in range(n + 1):
                    if j < n:
                        t = t0 + j
                        K.split_hi(act, t + 2)
                        act.wait_ge(K.tile_done, t + 1)
                        if j >= 2:
                            act.wait_ge(conv, j - 1)
                        b = BROW[CONV_OF[name]] + j
                        act.activation(XI[:, j % 2, PAD:].rearrange("p (a b) -> p a b", a=3), K.psum(t), ACT.Identity,
                                       bias=K.bias[:, b:b + 1]).then_inc(K.evac_act, 1)
                    if silu and j >= 1:
                        act.wait_ge(conv, j)
                        if j >= 3:
                            act.wait_ge(fin, j - 2)
                        act.activation(TH[:, (j - 1) % 2], OUT(j - 1), ACT.Tanh).then_inc(th, 1)
                act.wait_ge(last_tr, 1)
                act.activation(XR[:].rearrange("p (a b) -> p a b", b=512),
                               K.ps[0:PAD + NB, 0:n // 4, :], ACT.Identity).then_inc(last_ev, 1)

            @block.vector
            def _(dve):
                v = K.V(dve)
                dve.wait_ge(padded, 1)
                for j in range(n + 1):
                    if j < n:
                        dve.wait_ge(*K.emptied(t0 + j))
                        x, y = XI[:, j % 2], OUT(j)[:, 0:SEQ]
                        xs, ys = XI[:, j % 2, PAD + SEQ:], OUT(j)[:, SEQ:TOK]
                        st = K.convs[:, state0 + j, 0:24].rearrange("p (b j) -> p j b", j=PAD)
                        if silu:
                            v.step(dve.tensor_scalar(y, x[:, PAD:PAD + SEQ], tap(3, j), None, ALU.mult))
                            v.step(dve.tensor_scalar(ys, xs, tap(3, j), None, ALU.mult))
                        else:
                            cb = K.par[:, PROW["lru_conv_b"] + j:PROW["lru_conv_b"] + j + 1]
                            v.step(dve.tensor_scalar(y, x[:, PAD:PAD + SEQ], tap(3, j), cb, ALU.mult, ALU.add))
                            v.step(dve.tensor_scalar(ys, xs, tap(3, j), cb, ALU.mult, ALU.add))
                        v.step(dve.tensor_copy(XL[:, j], x[:, SEQ:SEQ + PAD + NB]))
                        for k in range(PAD):
                            v.wait()
                            v.step(dve.scalar_tensor_tensor(y, x[:, k:k + SEQ], tap(k, j), y, ALU.mult, ALU.add))
                            ins = dve.scalar_tensor_tensor(ys, st[:, k], tap(k, j), ys, ALU.mult, ALU.add)
                            if k == PAD - 1:
                                ins.then_inc(conv, 1)
                            else:
                                v.step(ins)
                    if silu and j >= 1:
                        dve.wait_ge(th, j)
                        dve.scalar_tensor_tensor(OUT(j - 1), TH[:, (j - 1) % 2], 1.0, OUT(j - 1), ALU.add,
                                                 ALU.mult).then_inc(fin, 1)
                if not silu:
                    dve.wait_ge(conv, n)

            @block.tensor
            def _(pe):
                for j in range(n):
                    K.project(pe, t0 + j, K.hH, K.hL)
                pe.wait_ge(conv, n)
                pe.wait_ge(*K.emptied(t0 + n - 1))
                for j in range(n):
                    last = pe.transpose(K.ps[0:PAD + NB, j // 4, (j % 4) * P:(j % 4 + 1) * P], XL[:, j], K.ident[:])
                last.then_inc(last_tr, 1)


CONV_OF = {"dn_conv_w": "dn_qkv", "lru_conv_w": "lru_x"}


def gate_branch(K, t0, name, OT, tag):
    nc = K.nc
    with ExitStack() as c:
        sb = lambda n_, s, d=F32: c.enter_context(nc.sbuf_tensor(tag + n_, s, d))
        G, TH = sb("_gx", [P, 2, TOK]), sb("_gth", [P, 2, TOK])
        th, prod, hi = K.sem(tag + "_gth"), K.sem(tag + "_gprod"), K.sem(tag + "_ghi")
        with nc.Block(no_gpsimd_drain=True) as block:
            @block.sync
            def _(sp):
                K.loads(sp, t0 + 4 + 2)

            @block.gpsimd
            def _(pool):
                K.split_lo(pool, t0 + 4 + 1)

            @block.scalar
            def _(act):
                for j in range(5):
                    if j < 4:
                        t = t0 + j
                        K.split_hi(act, t + 2)
                        act.wait_ge(K.tile_done, t + 1)
                        if j >= 2:
                            act.wait_ge(prod, j - 1)
                        b = BROW[name] + j
                        act.activation(G[:, j % 2].rearrange("p (a b) -> p a b", a=3), K.psum(t), ACT.Identity,
                                       scale=0.5, bias=K.hbias[:, b:b + 1]).then_inc(K.evac_act, 1)
                        act.wait_ge(*K.emptied(t))
                        act.activation(TH[:, j % 2], G[:, j % 2], ACT.Tanh).then_inc(th, 1)
                    if j >= 1:
                        act.wait_ge(prod, j)
                        act.activation(K.brH[:, j - 1], OT[:, j - 1], ACT.Identity).then_inc(hi, 1)

            @block.vector
            def _(dve):
                v = K.V(dve)
                for j in range(5):
                    if j < 4:
                        dve.wait_ge(th, j + 1)
                        v.do(dve.scalar_tensor_tensor(G[:, j % 2], TH[:, j % 2], 1.0, G[:, j % 2], ALU.add, ALU.mult))
                        dve.tensor_tensor(OT[:, j], G[:, j % 2], OT[:, j], ALU.mult).then_inc(prod, 1)
                    if j >= 1:
                        dve.wait_ge(hi, j)
                        dve.wait_ge(prod, j)
                        v.step(dve.tensor_tensor(K.brL[:, j - 1], OT[:, j - 1], K.brH[:, j - 1].bitcast(F32),
                                                 ALU.subtract))

            @block.tensor
            def _(pe):
                for j in range(4):
                    K.project(pe, t0 + j, K.hH, K.hL)


def merge_branch(K, t0, n):
    nc = K.nc
    with ExitStack() as c:
        sb = lambda n_, s, d=F32: c.enter_context(nc.sbuf_tensor(f"m{n}" + n_, s, d))
        TH, TM = sb("_th", [P, 2, TOK]), sb("_tm", [P, 2, TOK])
        with nc.Block(no_gpsimd_drain=True) as block:
            @block.sync
            def _(sp):
                K.loads(sp, t0 + 16 + 2)

            @block.gpsimd
            def _(pool):
                K.split_lo(pool, t0 + (16 if n == 3 else 17))

            @block.scalar
            def _(act):
                for d in range(KD):
                    t = t0 + 2 * d
                    K.split_hi(act, t + 2)
                    act.wait_ge(K.tile_done, t + 1)
                    if d >= 2:
                        act.wait_ge(*K.emptied(t - 3))
                    b = BROW["gate"] + KD * n + d
                    act.activation(TH[:, d % 2].rearrange("p (a b) -> p a b", a=3), K.psum(t), ACT.Tanh,
                                   scale=0.5, bias=K.hbias[:, b:b + 1]).then_inc(K.evac_act, 1)
                    K.split_hi(act, min(t + 3, t0 + 16 if n == 3 else t + 3))

            @block.vector
            def _(dve):
                v = K.V(dve)
                for d in range(KD):
                    t = t0 + 2 * d
                    dve.wait_ge(*K.emptied(t))
                    dve.wait_ge(K.tile_done, t + 2)
                    o = K.merged[:, d] if n == 0 else TM[:, d % 2]
                    dve.scalar_tensor_tensor(o.rearrange("p (a b) -> p a b", a=3),
                                             TH[:, d % 2].rearrange("p (a b) -> p a b", a=3), 1.0, K.psum(t + 1),
                                             ALU.add, ALU.mult).then_inc(K.evac_dve, 1)
                    if n:
                        dve.wait_ge(*K.emptied(t + 1))
                        v.step(dve.tensor_tensor(K.merged[:, d], K.merged[:, d], o, ALU.add))

            @block.tensor
            def _(pe):
                for d in range(KD):
                    K.project(pe, t0 + 2 * d, K.hH, K.hL)
                    K.project(pe, t0 + 2 * d + 1, K.brH, K.brL)


def output(K, t0):
    nc, i = K.nc, K.i
    NE = D // P
    with ExitStack() as c:
        sb = lambda n_, s, d=F32: c.enter_context(nc.sbuf_tensor("o" + n_, s, d))
        WH, WL = sb("_wH", [P, KD, D], F32R), sb("_wL", [P, KD, D], F32R)
        X = sb("_x", [P, 2, D])
        x_in = [K.sem("ox_in0"), K.sem("ox_in1")]
        y_out = K.y_out
        hi, lo, done, y = K.sem("m_hi"), K.sem("m_lo"), K.sem("o_done"), K.sem("y_ready")
        with nc.Block(no_gpsimd_drain=True) as block:
            @block.sync
            def _(sp):
                K.loads(sp, len(K.tiles))
                for t in range(TT8 + 1):
                    if t >= 2:
                        sp.wait_ge(y_out[t % 2], 16 * (t // 2))
                    if t < TT8:
                        sp.dma_start(X[:, t % 2], i["x_prompt"][0, t * P:(t + 1) * P]).then_inc(x_in[t % 2], 16)
                    else:
                        sp.dma_start(X[0:NB, t % 2], i["x_sample"][:, 0]).then_inc(x_in[t % 2], 16)
                    if t >= 1:
                        s = t - 1
                        sp.wait_ge(y, s + 1)
                        sp.dma_start(K.o["y"][0, s * P:(s + 1) * P], X[:, s % 2]).then_inc(y_out[s % 2], 16)
                sp.wait_ge(y, TT8 + 1)
                sp.dma_start(K.o["y_s"][:, 0], X[0:NB, TT8 % 2]).then_inc(y_out[TT8 % 2], 16)
                sp.wait_ge(y_out[0], 16 * 5)
                sp.wait_ge(y_out[1], 16 * 4)
                sp.wait_ge(K.stored, K.n_stored)

            @block.gpsimd
            def _(pool):
                for e in range(NE):
                    t = t0 + e
                    pool.wait_ge(K.w_hi, t + 1)
                    pool.tensor_tensor(WL[:, :, e * P:(e + 1) * P], K.raw[:, t % 2],
                                       WH[:, :, e * P:(e + 1) * P].bitcast(F32), ALU.subtract).then_inc(K.w_lo, 1)

            @block.scalar
            def _(act):
                for k in range(KD):
                    act.activation(K.hH[:, k], K.merged[:, k], ACT.Identity, scale=0.5).then_inc(hi, 1)
                    e, t = k, t0 + k
                    act.wait_ge(K.w_loaded[t % 2], 16 * (t // 2 + 1))
                    act.activation(WH[:, :, e * P:(e + 1) * P], K.raw[:, t % 2], ACT.Identity).then_inc(K.w_hi, 1)

            @block.vector
            def _(dve):
                for k in range(KD):
                    dve.wait_ge(hi, k + 1)
                    dve.scalar_tensor_tensor(K.hL[:, k], K.merged[:, k], 0.5, K.hH[:, k].bitcast(F32), ALU.mult,
                                             ALU.subtract).then_inc(lo, 1)
                for t in range(TT8 + 1):
                    n = P if t < TT8 else NB
                    dve.wait_ge(x_in[t % 2], 16 * (t // 2 + 1))
                    dve.wait_ge(done, t + 1)
                    q = 2 * (t % 4)
                    dve.tensor_tensor(X[0:n, t % 2].rearrange("p (a b) -> p a b", a=2), K.ps[0:n, q:q + 2, :],
                                      X[0:n, t % 2].rearrange("p (a b) -> p a b", a=2), ALU.add).then_inc(y, 1)

            @block.tensor
            def _(pe):
                pe.wait_ge(lo, KD)
                pe.wait_ge(K.w_lo, t0 + NE)
                for t in range(TT8 + 1):
                    n = P if t < TT8 else NB
                    if t >= 4:
                        pe.wait_ge(y, t - 3)
                    q = 2 * (t % 4)
                    for k in range(KD):
                        for m, (x, w) in enumerate(((K.hH, WH), (K.hH, WL), (K.hL, WH))):
                            for e in range(2):
                                last = pe.matmul(K.ps[0:n, q + e, :], x[:, k, t * P:t * P + n],
                                                 w[:, k, 512 * e:512 * (e + 1)], start=(k == 0 and m == 0),
                                                 stop=(k == KD - 1 and m == 2))
                    last.then_inc(done, 1)


def level_masks(K, pool, LO, UP, made):
    n = 0
    for l in range(7):
        s = 1 << l
        for M in (LO, UP):
            pool.memset(M[:, l], 0).then_inc(made, 1)
            n += 1
            pool.wait_ge(made, n)
            lower = M is LO
            v = M[:, l].rearrange("p (b r) -> p b r", r=2 * s)
            v = v[:, :, 0:s] if lower else v[:, :, s:2 * s]
            pool.memset(v, 1).then_inc(made, 1)
            n += 1
            for base, mul in (((-s, 1), (2 * s - 1, -1)) if lower else ((0, 1), (s - 1, -1))):
                pool.wait_ge(made, n)
                pool.affine_select(out=v, in_=v, compare_op=ALU.is_ge, fill=0, base=base,
                                   pattern=[[-2 * s * mul, P // (2 * s)], [0, s]], channel_multiplier=mul
                                   ).then_inc(made, 1)
                n += 1
    return n


def delta_rule(K):
    nc = K.nc
    with ExitStack() as c:
        sb = lambda n_, s, d=F32: c.enter_context(nc.sbuf_tensor("d" + n_, s, d))
        hs = lambda n_: sb(n_, [P, H, P])
        two = lambda n_: [sb(n_ + str(q), [P, H, P]) for q in range(2)]
        LO, UP = sb("_lo", [P, 7, P], I8), sb("_up", [P, 7, P], I8)
        NEGM, STR = sb("_negm", [P, P]), sb("_strict", [P, P])
        SS, RN, TM = sb("_ss", [P, 2 * H]), sb("_rn", [P, 2 * H]), sb("_tm", [P, 2 * H])
        GC = sb("_gc", [P, 2, H, P])
        SC = sb("_sc", [P, 4, H])
        GE = sb("_ge", [P, 2, H])
        KN, QN, KT, QT, DT, W = hs("_kn"), hs("_qn"), hs("_kT"), hs("_qT"), hs("_dT"), hs("_w")
        VB, KBG, KD_, QG, QKT = two("_vb"), two("_kbg"), two("_kdec"), two("_qgT"), two("_qkT")
        X, Y, NU = two("_X"), two("_Y"), two("_NU")
        M1s = sb("_M1", [P, 2, H, P])
        M1 = [M1s[:, q] for q in range(2)]
        SQ = M1s[:].rearrange("p a h d -> p (a h) d")
        NWT, U, STG = KN, QN, DT
        ST = hs("_state")
        OS, OR, OM = sb("_os", [P, H]), sb("_or", [P, H]), sb("_om", [P, H])
        qkv = lambda r, h, cols: K.OT[:, h, cols] if r == 0 else K.merged[:, (r - 1) * H + h, cols]
        OT = K.OT
        made = K.sem("dn_masks")
        S = {n_: K.sem("dn_" + n_) for n_ in
             ("rows_in", "tok", "square", "scaled", "back", "backed", "gram", "nu", "diff", "decay", "w", "pool",
              "unit", "first", "firsted", "m1", "m1e", "dxy", "upd", "wT", "wTe", "u", "ue", "o", "osq", "on",
              "oT", "oTe", "ds", "state", "stg", "ge", "fin", "fine", "kd")}
        B = [K.ps[:, b].rearrange("p (h d) -> p h d", h=H) for b in range(8)]
        tokv = lambda ch, r: K.TK[:, ch, r]
        bc = lambda ap: ap.unsqueeze(2).broadcast_to([P, H, P])
        mb = lambda ap: ap.unsqueeze(1).broadcast_to([P, H, P])

        with nc.Block(no_gpsimd_drain=True) as block:
            @block.sync
            def _(sp):
                for ch in range(NCH):
                    if ch >= 1:
                        sp.wait_ge(S["pool"], ch)
                        sp.wait_ge(S["ge"], ch)
                    for q, r in ((0, 0), (1, 2)):
                        sp.dma_start(GC[:, q], K.d_rows[r, :, ch * CH:(ch + 1) * CH].unsqueeze(0).broadcast_to(
                            [P, H, CH])).then_inc(S["rows_in"], 16)
                sp.wait_ge(S["fine"], 1)
                K.store(sp, K.o["dn_state"][0, 0].rearrange("h v k -> v h k"), KN[:])
                sp.wait_ge(K.stored, K.n_stored)

            @block.gpsimd
            def _(pool):
                g = K.G(pool)
                level_masks(K, pool, LO, UP, made)
                g.step(pool.memset(NEGM[:], 0.0))
                g.step(pool.memset(STR[:], -1.0))
                g.do(pool.memset(ST[:], 0.0))
                g.step(pool.affine_select(out=NEGM[:], in_=NEGM[:], compare_op=ALU.is_ge, fill=NEG, base=0,
                                          pattern=[[1, P]], channel_multiplier=-1))
                g.do(pool.affine_select(out=STR[:], in_=STR[:], compare_op=ALU.is_gt, fill=0.0, base=0,
                                        pattern=[[1, P]], channel_multiplier=-1))
                pool.sem_inc(made, 1)
                for ch in range(NCH):
                    q = ch % 2
                    pool.wait_ge(S["rows_in"], 32 * (ch + 1))
                    if ch >= 1 and q == 0:
                        pool.wait_ge(S["state"], ch)
                    if q == 1:
                        pool.wait_ge(S["nu"], ch)
                    g.do(pool.tensor_tensor(DT[:], GC[:, 0], bc(tokv(ch, 0)), ALU.subtract))
                    pool.tensor_tensor(DT[:], DT[:], mb(NEGM[:]), ALU.add).then_inc(S["diff"], 1)
                    g.do(pool.tensor_tensor(W[:], GC[:, 1], mb(STR[:]), ALU.mult))
                    pool.wait_ge(S["decay"], ch + 1)
                    pool.tensor_tensor(W[:], W[:], DT[:], ALU.mult).then_inc(S["w"], 1)
                    pool.wait_ge(S["scaled"], ch + 1)
                    pool.wait_ge(S["kd"], ch + 1)
                    g.step(pool.tensor_tensor(KBG[q][:], KN[:], bc(SC[:, 0]), ALU.mult))
                    g.step(pool.tensor_tensor(KD_[q][:], KN[:], bc(SC[:, 1]), ALU.mult))
                    pool.wait_ge(S["backed"], ch + 1)
                    g.wait()
                    pool.tensor_tensor(QG[q][:], QT[:], GC[:, 0], ALU.mult).then_inc(S["pool"], 1)

            @block.scalar
            def _(act):
                a = K.A(act)

                def pre(ch):
                    q = ch % 2
                    act.wait_ge(S["diff"], ch + 1)
                    act.activation(DT[:], DT[:], ACT.Exp).then_inc(S["decay"], 1)
                    a.step(act.activation(SC[:, 2], tokv(ch, 0), ACT.Exp))
                    for h in range(H):
                        a.step(act.activation(SC[:, 1, h:h + 1], K.TK[:, ch, 0, h:h + 1], ACT.Exp, scale=-1.0,
                                              bias=GC[:, 0, h, CH - 1:CH]))
                    act.activation(GE[:, q], GC[:, 0, :, CH - 1:CH].rearrange("p h a -> p (h a)"), ACT.Exp
                                   ).then_inc(S["ge"], 1)
                    a.wait()
                    act.wait_ge(S["ge"], ch + 1)
                    act.activation(GC[:, 0], GC[:, 0], ACT.Exp).then_inc(S["unit"], 1)
                    act.wait_ge(S["tok"], ch + 1)
                    act.activation(M1s[:].rearrange("p a h d -> p a (h d)"), K.ps[:, 0:2], ACT.Square
                                   ).then_inc(S["square"], 1)
                    act.wait_ge(S["back"], ch + 1)
                    act.activation(KT[:], B[3], ACT.Identity)
                    act.activation(QT[:], B[4], ACT.Identity).then_inc(S["backed"], 1)
                    act.activation(X[q][:], mb(K.ident[:]), ACT.Identity)
                    act.activation(Y[q][:], mb(K.ident[:]), ACT.Identity).then_inc(S["first"], 1)

                for c0 in range(0, NCH, 2):
                    pre(c0)
                    pre(c0 + 1)
                    for l in range(6):
                        for q in range(2):
                            n = (c0 // 2 * 6 + l) * 2 + q + 1
                            act.wait_ge(S["m1"], n)
                            act.activation(M1[q], B[q], ACT.Identity).then_inc(S["m1e"], 1)
                    for ch in (c0, c0 + 1):
                        act.wait_ge(S["wT"], ch + 1)
                        act.activation(NWT[:], B[0], ACT.Identity, scale=-1.0).then_inc(S["wTe"], 1)
                        act.wait_ge(S["u"], ch + 1)
                        act.activation(U[:], B[1], ACT.Identity).then_inc(S["ue"], 1)
                        act.wait_ge(S["o"], ch + 1)
                        act.activation(M1[ch % 2], B[2], ACT.Square).then_inc(S["osq"], 1)
                        act.wait_ge(S["oT"], ch + 1)
                        act.activation(OT[:, :, ch * CH:(ch + 1) * CH], B[4], ACT.Identity,
                                       scale=K.par[:, PROW["dn_onorm_w"]:PROW["dn_onorm_w"] + 1]).then_inc(S["oTe"], 1)
                act.wait_ge(S["fin"], 1)
                act.activation(KN[:], B[5], ACT.Identity).then_inc(S["fine"], 1)

            @block.vector
            def _(dve):
                v = K.V(dve)
                dve.wait_ge(made, 57)

                def pre(ch):
                    q = ch % 2
                    dve.wait_ge(S["square"], ch + 1)
                    v.do(dve.tensor_reduce(SS[:], SQ, AX.X, ALU.add))
                    v.do(dve.tensor_scalar(SS[:], SS[:], EPS, None, ALU.add))
                    rsqrt(v, SS[:], RN[:], TM[:])
                    v.do(dve.tensor_scalar(RN[:, 0:H], RN[:, 0:H], SCALE, None, ALU.mult))
                    if ch >= 1:
                        dve.wait_ge(S["pool"], ch)
                    v.step(dve.tensor_tensor(QN[:], B[0], bc(RN[:, 0:H]), ALU.mult))
                    v.step(dve.tensor_tensor(KN[:], B[1], bc(RN[:, H:2 * H]), ALU.mult))
                    dve.tensor_tensor(VB[q][:], B[2], bc(tokv(ch, 2)), ALU.mult).then_inc(S["scaled"], 1)
                    dve.wait_ge(S["unit"], ch + 1)
                    dve.tensor_tensor(SC[:, 0], SC[:, 2], tokv(ch, 2), ALU.mult).then_inc(S["kd"], 1)
                    dve.wait_ge(S["gram"], ch + 1)
                    dve.wait_ge(S["w"], ch + 1)
                    v.step(dve.tensor_tensor(NU[q][:], B[5], W[:], ALU.mult))
                    dve.tensor_tensor(QKT[q][:], B[6], DT[:], ALU.mult).then_inc(S["nu"], 1)

                for c0 in range(0, NCH, 2):
                    pre(c0)
                    pre(c0 + 1)
                    for q in range(2):
                        ch = c0 + q
                        dve.wait_ge(S["firsted"], ch + 1)
                        dve.wait_ge(S["first"], ch + 1)
                        dve.wait_ge(S["nu"], ch + 1)
                        v.step(dve.copy_predicated(X[q][:], mb(LO[:, 0]), B[q]))
                        dve.copy_predicated(Y[q][:], mb(UP[:, 0]), NU[q][:]).then_inc(S["upd"], 1)
                    for l in range(1, 7):
                        for q in range(2):
                            n = (c0 // 2 * 6 + l - 1) * 2 + q + 1
                            dve.wait_ge(S["dxy"], n)
                            if l < 6:
                                v.step(dve.copy_predicated(X[q][:], mb(LO[:, l]), B[2 + q]))
                            dve.copy_predicated(Y[q][:], mb(UP[:, l]), B[4 + q]).then_inc(S["upd"], 1)
                    for q in range(2):
                        ch = c0 + q
                        if ch >= 1:
                            dve.wait_ge(S["state"], ch)
                        v.step(dve.tensor_tensor(STG[:], ST[:], bc(GE[:, q]), ALU.mult))
                        dve.wait_ge(S["osq"], ch + 1)
                        v.do(dve.tensor_reduce(OS[:], M1[q], AX.X, ALU.add))
                        v.do(dve.tensor_scalar(OS[:], OS[:], 1.0 / P, EPS, ALU.mult, ALU.add))
                        rsqrt(v, OS[:], OR[:], OM[:])
                        dve.tensor_tensor(M1[q], B[2], bc(OR[:]), ALU.mult).then_inc(S["on"], 1)
                        dve.wait_ge(S["ds"], ch + 1)
                        dve.tensor_tensor(ST[:], STG[:], B[3], ALU.add).then_inc(S["state"], 1)

            @block.tensor
            def _(pe):
                def pre(ch):
                    q = ch % 2
                    cols = slice(ch * CH, (ch + 1) * CH)
                    if ch >= 1:
                        pe.wait_ge(S["nu"], ch)
                        pe.wait_ge(S["scaled"], ch)
                        if ch - q:
                            pe.wait_ge(S["oTe"], ch - q)
                            pe.wait_ge(S["state"], ch - q)
                            pe.wait_ge(S["on"], ch - q)
                    for r in range(3):
                        for h in range(H):
                            last = pe.transpose(B[r][:, h], qkv(r, h, cols), K.ident[:])
                    last.then_inc(S["tok"], 1)
                    pe.wait_ge(S["scaled"], ch + 1)
                    if ch >= 1:
                        pe.wait_ge(S["backed"], ch)
                    for r, src in ((3, KN), (4, QN)):
                        for h in range(H):
                            last = pe.transpose(B[r][:, h], src[:, h], K.ident[:])
                    last.then_inc(S["back"], 1)
                    pe.wait_ge(S["backed"], ch + 1)
                    for r, src in ((5, KT), (6, QT)):
                        for h in range(H):
                            last = pe.matmul(B[r][:, h], KT[:, h], src[:, h], start=True, stop=True)
                    last.then_inc(S["gram"], 1)

                for c0 in range(0, NCH, 2):
                    pre(c0)
                    pre(c0 + 1)
                    for q in range(2):
                        ch = c0 + q
                        pe.wait_ge(S["nu"], ch + 1)
                        pe.wait_ge(S["scaled"], c0 + 2)
                        for h in range(H):
                            last = pe.matmul(B[q][:, h], NU[q][:, h], K.ident[:], start=True, stop=True)
                        last.then_inc(S["firsted"], 1)
                    for l in range(1, 7):
                        for q in range(2):
                            n = (c0 // 2 * 6 + l - 1) * 2 + q
                            pe.wait_ge(S["upd"], c0 // 2 * 14 + (l - 1) * 2 + q + 1)
                            for h in range(H):
                                last = pe.matmul(B[q][:, h], NU[q][:, h], X[q][:, h], start=True, stop=True)
                            last.then_inc(S["m1"], 1)
                        for q in range(2):
                            n = (c0 // 2 * 6 + l - 1) * 2 + q
                            pe.wait_ge(S["m1e"], n + 1)
                            for h in range(H):
                                if l < 6:
                                    pe.matmul(B[2 + q][:, h], Y[q][:, h], M1[q][:, h], start=True, stop=True)
                                last = pe.matmul(B[4 + q][:, h], M1[q][:, h], Y[q][:, h], start=True, stop=True)
                            last.then_inc(S["dxy"], 1)
                    for q in range(2):
                        ch = c0 + q
                        pe.wait_ge(S["upd"], c0 // 2 * 14 + 14)
                        pe.wait_ge(S["pool"], c0 + 2)
                        if q:
                            pe.wait_ge(S["wTe"], ch)
                        for h in range(H):
                            last = pe.matmul(B[0][:, h], KBG[q][:, h], Y[q][:, h], start=True, stop=True)
                        last.then_inc(S["wT"], 1)
                        pe.wait_ge(S["wTe"], ch + 1)
                        if ch:
                            pe.wait_ge(S["state"], ch)
                        for h in range(H):
                            pe.matmul(B[1][:, h], Y[q][:, h], VB[q][:, h], start=True, stop=False)
                            last = pe.matmul(B[1][:, h], NWT[:, h], ST[:, h], start=False, stop=True)
                        last.then_inc(S["u"], 1)
                        pe.wait_ge(S["ue"], ch + 1)
                        for h in range(H):
                            pe.matmul(B[2][:, h], QG[q][:, h], ST[:, h], start=True, stop=False)
                            last = pe.matmul(B[2][:, h], QKT[q][:, h], U[:, h], start=False, stop=True)
                        last.then_inc(S["o"], 1)
                        for h in range(H):
                            last = pe.matmul(B[3][:, h], KD_[q][:, h], U[:, h], start=True, stop=True)
                        last.then_inc(S["ds"], 1)
                        pe.wait_ge(S["on"], ch + 1)
                        if q:
                            pe.wait_ge(S["oTe"], ch)
                        for h in range(H):
                            last = pe.transpose(B[4][:, h], M1[q][:, h], K.ident[:])
                        last.then_inc(S["oT"], 1)
                pe.wait_ge(S["state"], NCH)
                for h in range(H):
                    last = pe.transpose(B[5][:, h], ST[:, h], K.ident[:])
                last.then_inc(S["fin"], 1)


def delta_decode(K):
    nc, i = K.nc, K.i
    S4 = [P, NB, H, P]
    with ExitStack() as c:
        sb = lambda n_, s, d=F32: c.enter_context(nc.sbuf_tensor("e" + n_, s, d))
        SD, KB, T = sb("_state", S4), sb("_row", S4), sb("_prod", S4)
        R = sb("_rows", [NB, 2, H, P])
        SS, RN, TM = sb("_ss", [NB, 2, H]), sb("_rn", [NB, 2, H]), sb("_tm", [NB, 2, H])
        SK, UU, O = sb("_sk", [P, NB, H]), sb("_u", [P, NB, H]), sb("_o", [P, NB, H])
        OR, OQ = sb("_or", [32, P]), sb("_oq", [32, P])
        OS, OR1, OM = sb("_os", [32, 1]), sb("_or1", [32, 1]), sb("_om", [32, 1])
        N = {x: K.sem("de_" + x) for x in ("s_in", "k_in", "q_in", "tr", "sq", "rows", "rows_out", "k_used",
                                           "new", "o", "oT", "osq", "on", "ob")}
        with nc.Block(no_gpsimd_drain=True) as block:
            @block.sync
            def _(sp):
                for b in range(NB):
                    sp.dma_start(SD[:, b], i["state_dn"][0, b].rearrange("h v k -> v h k")).then_inc(N["s_in"], 16)
                sp.wait_ge(N["rows"], 1)
                sp.dma_start(K.d_qk.rearrange("r b h d -> b r h d"), R[:]).then_inc(N["rows_out"], 16)
                sp.wait_ge(N["rows_out"], 16)
                row = lambda r: K.d_qk[r].rearrange("b h d -> (b h d)").unsqueeze(0).broadcast_to([P, NB * H * P])
                sp.dma_start(KB[:].rearrange("p b h d -> p (b h d)"), row(1)).then_inc(N["k_in"], 16)
                sp.wait_ge(N["k_used"], 1)
                sp.dma_start(KB[:].rearrange("p b h d -> p (b h d)"), row(0)).then_inc(N["q_in"], 16)
                sp.wait_ge(N["new"], 1)
                for b in range(NB):
                    K.store(sp, K.o["dn_state_s"][0, b].rearrange("h v k -> v h k"), SD[:, b])
                sp.wait_ge(K.stored, K.n_stored)

            @block.tensor
            def _(pe):
                for r in range(2):
                    for h in range(H):
                        x = K.OT if r == 0 else K.merged
                        last = pe.transpose(K.ps[0:NB, r, h * P:(h + 1) * P], x[:, h, SEQ:TOK], K.ident[:])
                last.then_inc(N["tr"], 1)
                pe.wait_ge(N["o"], 1)
                pe.transpose(K.ps[0:32, 2, 0:P], O[:].rearrange("p b h -> p (b h)"), K.ident[:]).then_inc(N["oT"], 1)
                pe.wait_ge(N["on"], 1)
                pe.transpose(K.ps[:, 3, 0:32], OR[:], K.ident[0:32, 0:32]).then_inc(N["ob"], 1)

            @block.scalar
            def _(act):
                act.wait_ge(N["tr"], 1)
                act.activation(R[:].rearrange("b r h d -> b r (h d)"), K.ps[0:NB, 0:2], ACT.Square).then_inc(N["sq"], 1)
                act.wait_ge(N["oT"], 1)
                act.activation(OQ[:], K.ps[0:32, 2, 0:P], ACT.Square, accum_out=OS[:]).then_inc(N["osq"], 1)
                act.wait_ge(N["ob"], 1)
                act.activation(K.OT[:, :, SEQ:TOK].rearrange("p h b -> p b h"),
                               K.ps[:, 3, 0:32].rearrange("p (b h) -> p b h", b=NB), ACT.Identity,
                               scale=K.par[:, PROW["dn_onorm_w"]:PROW["dn_onorm_w"] + 1])

            @block.vector
            def _(dve):
                v = K.V(dve)
                last = lambda ap: ap.unsqueeze(3).broadcast_to(S4)
                al, be = (K.alpha[:, q].rearrange("p h b -> p b h") for q in range(2))
                dve.wait_ge(N["sq"], 1)
                v.do(dve.tensor_reduce(SS[:], R[:], AX.X, ALU.add))
                v.do(dve.tensor_scalar(SS[:], SS[:], EPS, None, ALU.add))
                rsqrt(v, SS[:].rearrange("b r h -> b (r h)"), RN[:].rearrange("b r h -> b (r h)"),
                      TM[:].rearrange("b r h -> b (r h)"))
                v.do(dve.tensor_scalar(RN[:, 0], RN[:, 0], SCALE, None, ALU.mult))
                for r in range(2):
                    ins = dve.tensor_tensor(R[:, r], heads(K.ps[0:NB, r]),
                                            RN[:, r].unsqueeze(2).broadcast_to([NB, H, P]), ALU.mult)
                ins.then_inc(N["rows"], 1)
                dve.wait_ge(N["s_in"], 16 * NB)
                dve.wait_ge(N["k_in"], 16)
                flat = lambda x: x[:].rearrange("p b h d -> p (b h d)")
                flat3 = lambda x: x[:].rearrange("p b h d -> p (b h) d")
                v.do(dve.tensor_tensor(flat(T), flat(SD), flat(KB), ALU.mult))
                v.do(dve.tensor_reduce(SK[:].rearrange("p b h -> p (b h)"), flat3(T), AX.X, ALU.add))
                v.do(dve.tensor_tensor(SK[:], SK[:], al, ALU.mult))
                v.do(dve.tensor_tensor(UU[:], K.merged[:, H:2 * H, SEQ:TOK].rearrange("p h b -> p b h"), SK[:],
                                       ALU.subtract))
                v.do(dve.tensor_tensor(UU[:], UU[:], be, ALU.mult))
                for b in range(NB):
                    for h in range(H):
                        v.step(dve.tensor_scalar(SD[:, b, h], SD[:, b, h], K.alpha[:, 0, h, b:b + 1], None, ALU.mult))
                        ins = dve.tensor_scalar(T[:, b, h], KB[:, b, h], UU[:, b, h:h + 1], None, ALU.mult)
                        if (b, h) != (NB - 1, H - 1):
                            v.step(ins)
                ins.then_inc(N["k_used"], 1)
                dve.wait_ge(N["k_used"], 1)
                dve.tensor_tensor(flat(SD), flat(SD), flat(T), ALU.add).then_inc(N["new"], 1)
                dve.wait_ge(N["new"], 1)
                dve.wait_ge(N["q_in"], 16)
                v.do(dve.tensor_tensor(flat(T), flat(SD), flat(KB), ALU.mult))
                dve.tensor_reduce(O[:].rearrange("p b h -> p (b h)"), flat3(T), AX.X, ALU.add).then_inc(N["o"], 1)
                dve.wait_ge(N["osq"], 1)
                v.do(dve.tensor_scalar(OS[:], OS[:], 1.0 / P, EPS, ALU.mult, ALU.add))
                rsqrt(v, OS[:], OR1[:], OM[:])
                dve.tensor_scalar(OR[:], K.ps[0:32, 2, 0:P], OR1[:, 0:1], None, ALU.mult).then_inc(N["on"], 1)


def lru(K):
    nc, i = K.nc, K.i
    with ExitStack() as c:
        sb = lambda n_, s, d=F32: c.enter_context(nc.sbuf_tensor("l" + n_, s, d))
        BD = sb("_blocks", [P, 2, H, P])
        A, U, XG = sb("_a", [P, H, TOK]), sb("_u", [P, H, TOK]), sb("_x", [P, H, TOK])
        SM = sb("_sp", [P, 6, H])
        HR = sb("_h_rows", [9, BW])
        N = {x: K.sem("lru_" + x) for x in ("zero", "w_in", "gates", "tr", "ti", "nla", "a", "th", "u", "root",
                                            "h", "hT", "hTe", "out", "lam", "lamu", "xg", "ps")}
        lam = K.par[:, PROW["lru_lambda"]:PROW["lru_lambda"] + H]
        with nc.Block(no_gpsimd_drain=True) as block:
            @block.gpsimd
            def _(pool):
                pool.memset(BD[:], 0.0).then_inc(N["zero"], 1)

            @block.sync
            def _(sp):
                sp.wait_ge(N["zero"], 1)
                for r, name in enumerate(("lru_w_r", "lru_w_i")):
                    w = i[name][0].rearrange("(t a) e f -> a e t f", a=2)
                    for a in range(2):
                        sp.dma_start(BD[64 * a:64 * a + 64, r, :, 64 * a:64 * a + 64], w[a]).then_inc(N["w_in"], 16)
                sp.wait_ge(N["hTe"], 1)
                K.store(sp, K.o["lru_h"][0], HR[0:1])
                K.store(sp, K.o["lru_h_s"][0], HR[1:9])
                sp.wait_ge(K.stored, K.n_stored)

            @block.tensor
            def _(pe):
                pe.wait_ge(N["w_in"], 64)
                for t in range(H):
                    for r in range(2):
                        if t >= 1:
                            pe.wait_ge(N["tr"] if r == 0 else N["ti"], t)
                        for g in range(3):
                            last = pe.matmul(K.ps[:, 3 * r + g, 0:G3], BD[:, r, t], K.OT[:, t, g * G3:(g + 1) * G3],
                                             start=True, stop=True)
                        last.then_inc(N["gates"], 1)
                pe.wait_ge(N["h"], H)
                for t in range(H):
                    last = pe.transpose(K.ps[0:9, 6, t * P:(t + 1) * P], K.OT[:, t, SEQ - 1:TOK], K.ident[:])
                last.then_inc(N["hT"], 1)

            @block.scalar
            def _(act):
                act.wait_ge(N["lam"], 1)
                act.activation(SM[:, 1], SM[:, 1], ACT.Exp).then_inc(N["lamu"], 1)
                for t in range(H):
                    for r, (dst, name, s) in enumerate(((A, "lru_b_r", "tr"), (U, "lru_b_i", "ti"))):
                        act.wait_ge(N["gates"], 2 * t + r + 1)
                        b = PROW[name] + t
                        act.activation(dst[:, t].rearrange("p (a b) -> p a b", a=3),
                                       K.ps[:, 3 * r:3 * r + 3, 0:G3], ACT.Tanh, scale=0.5,
                                       bias=K.hpar[:, b:b + 1]).then_inc(N[s], 1)
                    act.wait_ge(N["nla"], t + 1)
                    act.activation(U[:, t], A[:, t], ACT.Tanh).then_inc(N["th"], 1)
                    act.activation(A[:, t], A[:, t], ACT.Exp, scale=-1.0).then_inc(N["a"], 1)
                for t in range(H):
                    act.wait_ge(N["u"], t + 1)
                    act.activation(U[:, t], U[:, t], ACT.Sqrt).then_inc(N["root"], 1)
                act.wait_ge(N["hT"], 1)
                act.activation(HR[:], K.ps[0:9, 6], ACT.Identity).then_inc(N["hTe"], 1)

            @block.vector
            def _(dve):
                v = K.V(dve)
                v.do(dve.tensor_scalar(SM[:, 0], lam, -1.0, None, ALU.mult))
                dve.tensor_tensor(SM[:, 1], SM[:, 0], lam, ALU.min).then_inc(N["lam"], 1)
                dve.wait_ge(N["lamu"], 1)
                log1p_exp(v, SM[:, 0], SM[:, 1], SM[:, 2], SM[:, 3], SM[:, 4])
                v.do(dve.tensor_scalar(SM[:, 5], SM[:, 4], LRU_C / 2, None, ALU.mult))
                for t in range(H):
                    dve.wait_ge(N["tr"], t + 1)
                    dve.wait_ge(N["ti"], t + 1)
                    v.step(dve.scalar_tensor_tensor(XG[:, t], U[:, t], 1.0, K.OT[:, t], ALU.add, ALU.mult))
                    dve.tensor_scalar(A[:, t], A[:, t], 1.0, SM[:, 5, t:t + 1], ALU.add, ALU.mult).then_inc(N["nla"], 1)
                    dve.wait_ge(N["a"], t + 1)
                    v.do(dve.tensor_tensor(K.OT[:, t], A[:, t], A[:, t], ALU.mult))
                    dve.scalar_tensor_tensor(U[:, t], K.OT[:, t], 1.0, U[:, t], ALU.add, ALU.mult).then_inc(N["u"], 1)
                for t in range(H):
                    dve.wait_ge(N["root"], t + 1)
                    v.do(dve.scalar_tensor_tensor(XG[:, t], U[:, t], 0.5, XG[:, t], ALU.mult, ALU.mult))
                    v.step(dve.tensor_tensor_scan(K.OT[:, t, 0:SEQ], A[:, t, 0:SEQ], XG[:, t, 0:SEQ], 0.0, ALU.mult,
                                                  ALU.add))
                    v.do(dve.tensor_tensor(A[:, t, SEQ:TOK], A[:, t, SEQ:TOK], K.convs[:, 12 + t, 24:32], ALU.mult))
                    dve.tensor_tensor(K.OT[:, t, SEQ:TOK], A[:, t, SEQ:TOK], XG[:, t, SEQ:TOK], ALU.add
                                      ).then_inc(N["h"], 1)


class RowTurns:

    BANK = 6

    def __init__(self, K, tag):
        self.K, self.tag = K, tag
        self.turned, self.moved = K.sem(tag + "_turned"), K.sem(tag + "_turn_moved")
        self.normed = K.sem(tag + "_normed")
        self.turns = []
        self.norm = None

    def out(self, tile, src, dst, n):
        self.turns.append((tile, "out", src, dst, n, len(self.turns)))
        return len(self.turns)

    def back(self, tile, src, dst, n, w, nth):
        self.turns.append((tile, "back", src, (dst, w, nth), n, len(self.turns)))

    def of(self, tile):
        return [x for x in self.turns if x[0] == tile]

    def pe(self, pe, turn):
        K = self.K
        _, kind, src, dst, n, m = turn
        if m:
            pe.wait_ge(self.moved, m)
        if kind == "back":
            pe.wait_ge(self.normed, dst[2])
        for h in range(H):
            if kind == "out":
                last = pe.transpose(K.ps[0:n, self.BANK, h * P:(h + 1) * P], src[:, h], K.ident[:])
            else:
                last = pe.transpose(K.ps[:, self.BANK, h * P:h * P + n], src[:, h], K.ident[0:n, 0:n])
        last.then_inc(self.turned, 1)

    def act(self, act, turn):
        K = self.K
        _, kind, src, dst, n, m = turn
        act.wait_ge(self.turned, m + 1)
        if kind == "out":
            act.activation(dst, heads(K.ps[0:n, self.BANK]), ACT.Identity).then_inc(self.moved, 1)
        else:
            act.activation(dst[0], heads(K.ps[:, self.BANK])[:, :, 0:n], ACT.Identity, scale=dst[1]
                           ).then_inc(self.moved, 1)


def project_tiles(K, t0, n, row, DST, tag, x=None, cols=TOK, turns=None, rows=None, stores=(), RQ=None,
                  preload=True):
    nc = K.nc
    xH, xL = x or (K.hH, K.hL)
    end = t0 + n
    of = lambda tile: turns.of(tile) if turns else []
    with ExitStack() as c:
        sb = lambda n_, s, d=F32: c.enter_context(nc.sbuf_tensor(tag + n_, s, d))
        if RQ is not None:
            SQ = sb("_sq", [P, 2, SEQ])
            QS, QM = sb("_qss", [P, H, TT8]), sb("_qtm", [P, H, TT8])
            sq, sums = K.sem(tag + "_qsq"), K.sem(tag + "_qsum")
        if rows is not None:
            row_list, sizes, norm, after = rows
            nt = len(sizes)
            T = sb("_t", [P, H, P])
            SS, RN, TM = (sb(x_, [P, nt, H]) for x_ in ("_ss", "_rn", "_tm"))
        flat = lambda x_: x_[:].rearrange("p a h -> p (a h)")
        with nc.Block(no_gpsimd_drain=True) as block:
            @block.sync
            def _(sp):
                K.loads(sp, end + 2 if preload else end)
                for (sem, count), dst, src in stores:
                    sp.wait_ge(sem, count)
                    K.store(sp, dst, src)
                if stores:
                    sp.wait_ge(K.stored, K.n_stored)

            @block.gpsimd
            def _(pool):
                K.split_lo(pool, end + 1 if preload else end)

            @block.scalar
            def _(act):
                for j in range(n):
                    t = t0 + j
                    K.split_hi(act, t + 2 if preload else min(t + 2, end))
                    for turn in of(j):
                        turns.act(act, turn)
                    act.wait_ge(K.tile_done, t + 1)
                    if row is None:
                        act.activation(DST[:, j], K.ps[:, 3 * (t % 2), 0:cols], ACT.Identity).then_inc(K.evac_act, 1)
                    else:
                        act.activation(DST[:, j].rearrange("p (a b) -> p a b", a=3), K.psum(t), ACT.Identity,
                                       bias=K.bias[:, row + j:row + j + 1]).then_inc(K.evac_act, 1)
                    if RQ is not None:
                        act.wait_ge(*K.emptied(t))
                        if j >= 2:
                            act.wait_ge(sums, j - 1)
                        act.activation(SQ[:, j % 2], DST[:, j, 0:SEQ], ACT.Square).then_inc(sq, 1)

            @block.tensor
            def _(pe):
                def norms(j):
                    pe.wait_ge(sq, j + 1)
                    for t in range(TT8):
                        q = j * TT8 + t
                        last = pe.matmul(K.ps[:, 7, q:q + 1], SQ[:, j % 2, t * P:(t + 1) * P], K.ones[:],
                                         start=True, stop=True)
                    last.then_inc(sums, 1)

                for j in range(n):
                    todo = of(j)

                    def meanwhile(k, todo=todo):
                        if k < len(todo):
                            turns.pe(pe, todo[k])

                    K.project(pe, t0 + j, xH, xL, groups=3 if row is not None else 1, cols=cols, meanwhile=meanwhile)
                    if RQ is not None and j >= 1:
                        norms(j - 1)
                if RQ is not None:
                    norms(n - 1)

            @block.vector
            def _(dve):
                v = K.V(dve)
                if rows is not None:
                    v.step(dve.memset(SS[:], 1.0))
                    v.do(dve.memset(T[:], 1.0))
                    for j, m in enumerate(sizes):
                        dve.wait_ge(turns.moved, after[j])
                        v.do(dve.tensor_tensor(T[0:m], row_list[j], row_list[j], ALU.mult))
                        v.do(dve.tensor_reduce(SS[0:m, j], T[0:m], AX.X, ALU.add))
                    v.do(dve.tensor_scalar(SS[:], SS[:], 1.0 / P, EPS, ALU.mult, ALU.add))
                    rsqrt(v, flat(SS), flat(RN), flat(TM))
                    for j, m in enumerate(sizes):
                        v.do(dve.tensor_tensor(row_list[j], row_list[j],
                                               RN[0:m, j].unsqueeze(2).broadcast_to([m, H, P]), ALU.mult))
                        dve.tensor_tensor(row_list[j], row_list[j], norm[0:m].unsqueeze(1).broadcast_to([m, H, P]),
                                          ALU.mult).then_inc(turns.normed, 1)
                if RQ is not None:
                    dve.wait_ge(sums, H)
                    v.do(dve.tensor_scalar(flat(QS), K.ps[:, 7, 0:H * TT8], 1.0 / P, EPS, ALU.mult, ALU.add))
                    rsqrt(v, flat(QS), flat(RQ), flat(QM))
                    v.do(dve.tensor_scalar(flat(RQ), flat(RQ), SCALE, None, ALU.mult))


def attend(K, KT, V, RQ, tag, fox):
    nc, i = K.nc, K.i
    its = [(h, t) for h in range(H) for t in range(TT8)]
    nb = [t + 1 if fox else MEM // P for _, t in its]
    UB = 4 if fox else MEM // P
    units = [(n, b, min(UB, nb[n] - b)) for n in range(len(its)) for b in range(0, nb[n], UB)]
    of_tile = [[u for u, x in enumerate(units) if x[0] == n] for n in range(len(its))]
    halves = [(n, a, min(512, nb[n] * P - a)) for n in range(len(its)) for a in range(0, nb[n] * P, 512)]
    half_of = [[x for x in range(len(halves)) if halves[x][0] == n] for n in range(len(its))]
    W = SEQ if fox else MEM
    NP = PAGES if fox else MEM // P
    PW = NP * P
    R = NB * H
    KEYS = lambda b: 1 + 3 * b // 2
    LOGF, MAX, EXP, TURN, VALUES, TAKE, NEW, LAST = 13, 14, 15, 16, (lambda b: 17 + 3 * b // 2), 28, 29, 30
    keys_at = {KEYS(b): b for b in range(NB)}
    values_at = {VALUES(b): b for b in range(NB)}
    with ExitStack() as c:
        sb = lambda n_, s, d=F32: c.enter_context(nc.sbuf_tensor(tag + n_, s, d))
        LG = sb("_logits", [P, 4, W])
        PT = sb("_pT", [P, 2, UB, P])
        OQ = sb("_o_rows", [P, 2, P])
        NM, RS = sb("_negmax", [P, 4]), sb("_sum", [P, 4])
        if fox:
            C = K.borrowed(tag + "_c_bc", 2, [P, 2, SEQ])
            MK = sb("_mask", [P, P])
        N = {x: K.sem(tag + "_" + x) for x in ("c_in0", "c_in1", "rel", "mask", "s", "lg", "max", "exp", "rs", "pT",
                                               "pTe", "v", "od", "b", "oe")}
        KV = [K.borrowed(f"{tag}_kv{q}", q, [P, NP, H, P])[:] for q in range(2)]
        QB = sb("_qb", [P, 2, H * P])
        QS, QN, QM = sb("_qs", [NB, H]), sb("_qn", [NB, H]), sb("_qm", [NB, H])
        SB = sb("_scores", [P, NP, NB, H])
        DLG = sb("_d_logits", [R, max(PW, H * P)])
        QR = DLG[0:NB, 0:H * P].rearrange("p (h d) -> p h d", h=H)
        DL = DLG[:, 0:PW]
        PC = sb("_p_cols", [P, NP, R])
        DM, DS = sb("_dm", [R, 1]), sb("_ds", [R, 1])
        OA = sb("_oa", [P, R])
        M = {x: K.sem(tag + "_d_" + x) for x in
             ("q", "qsq", "qr", "q_out", "qb0", "qb1", "k_in0", "k_in1", "used", "sc", "scT", "max", "exp", "p", "pT",
              "pTe", "v_in0", "v_in1", "o", "oa", "pg", "lf_in", "lfT", "lfs", "row_in", "newT", "newv")}
        if fox:
            PG = sb("_pages", [1, R], I32)
            LF = sb("_lf", [P, NP, NB, H])
            CC = QB[0:R, 0]
            LN, SN = sb("_lf_new", [R, 1]), sb("_s_new", [R, 4])
            Q3, K3, V3 = (sb(x, [R, P]) for x in ("_q3", "_k3", "_v3"))
        w_bc = K.qnw if fox else K.mqnw
        cache = ("cache_fox_k", "cache_fox_v") if fox else ("cache_mem_k", "cache_mem_v")
        per_load = 16 * (NP if fox else 1)
        BANK = K.ps[:, 7]
        with nc.Block(no_gpsimd_drain=True) as block:
            @block.sync
            def _(sp):
                def load_c(h):
                    if fox:
                        if h >= 2:
                            sp.wait_ge(N["rel"], TT8 * (h - 1))
                        sp.dma_start(C[:, h % 2], K.d_rows[1, h:h + 1].broadcast_to([P, SEQ])
                                     ).then_inc(N[f"c_in{h % 2}"], 16)

                def load(which, b, after, count):
                    src = i[cache[which]]
                    s = M[("k_in" if which == 0 else "v_in") + str(b % 2)]
                    pages = [sp.value_load(PG[0:1, b * NP + g:b * NP + g + 1], min_val=0, max_val=src.shape[1] - 1)
                             for g in range(NP)] if fox else None
                    if count:
                        sp.wait_ge(after, count)
                    if not fox:
                        sp.dma_start(KV[b % 2], src[0, b].rearrange("(g k) h d -> k g h d", k=P)).then_inc(s, 16)
                        return
                    for g in range(NP):
                        page = pages[g]
                        sp.dma_start(KV[b % 2][:, g], src[0, bass.ds(page, 1)].rearrange("a k h d -> k (a h) d")
                                     ).then_inc(s, 16)
                        if which == 0:
                            sp.dma_start(LF[:, g, b], i["cache_fox_logf"][0, bass.ds(page, 1)].rearrange(
                                "a k h -> k (a h)")).then_inc(M["lf_in"], 16)

                def load_q(b):
                    sp.dma_start(QB[:, b % 2], K.d_q[b:b + 1].rearrange("b h d -> b (h d)").broadcast_to([P, H * P])
                                 ).then_inc(M[f"qb{b % 2}"], 16)

                load_c(0)
                load_c(1)
                if fox:
                    sp.dma_start(PG[:], i["page_table"].rearrange("b g -> (b g)").unsqueeze(0)).then_inc(M["pg"], 16)
                    sp.wait_ge(M["pg"], 16)
                load(0, 0, None, 0)
                load(0, 1, None, 0)
                sp.wait_ge(M["qr"], 1)
                sp.dma_start(K.d_q, QR).then_inc(M["q_out"], 16)
                sp.wait_ge(M["q_out"], 16)
                load_q(0)
                load_q(1)
                if fox:
                    sp.dma_start(Q3[:], K.d_q.rearrange("b h d -> (b h) d")).then_inc(M["row_in"], 16)
                    sp.dma_start(K3[:], K.o["fox_k_s"][0, :, 0].rearrange("b h d -> (b h) d")).then_inc(M["row_in"], 16)
                    sp.dma_start(V3[:], K.o["fox_v_s"][0, :, 0].rearrange("b h d -> (b h) d")).then_inc(M["row_in"], 16)
                    sp.dma_start(LN[:], K.d_lf.rearrange("b (h a) -> (b h) a", a=1)).then_inc(M["row_in"], 16)
                for b in range(2, NB):
                    load(0, b, M["sc"], b - 1)
                    load_q(b)
                    if b == 5:
                        load_c(2)
                for b in range(NB):
                    if b < 2:
                        load(1, b, M["sc"], NB - 1 + b)
                    else:
                        load(1, b, M["o"], b - 1)
                    if b == 1:
                        load_c(3)

            @block.gpsimd
            def _(pool):
                if not fox:
                    return
                g = K.G(pool)
                g.do(pool.memset(MK[:], 0.0))
                pool.affine_select(out=MK[:], in_=MK[:], compare_op=ALU.is_ge, fill=NEG, base=0,
                                   pattern=[[-1, P]], channel_multiplier=1).then_inc(N["mask"], 1)
                for n, (h, t) in enumerate(its):
                    pool.wait_ge(N[f"c_in{h % 2}"], 16 * (h // 2 + 1))
                    if n >= 4:
                        pool.wait_ge(N["pT"], of_tile[n - 4][-1] + 1)
                    w = nb[n] * P
                    pool.tensor_scalar(LG[:, n % 4, 0:w], C[:, h % 2, 0:w], K.TK[:, t, 1, h:h + 1], None, ALU.subtract
                                       ).then_inc(N["rel"], 1)

            @block.tensor
            def _(pe):
                def scores(n):
                    h, t = its[n]
                    for x in half_of[n]:
                        _, a, w = halves[x]
                        if x >= 3:
                            pe.wait_ge(N["lg"], x - 2)
                        pe.matmul(K.ps[:, x % 3, 0:w], K.OT[:, h, t * P:(t + 1) * P], KT[:, h, a:a + w],
                                  start=True, stop=True).then_inc(N["s"], 1)

                def turn(u):
                    n, b0, k = units[u]
                    pe.wait_ge(N["exp"], n + 1)
                    if u >= 2:
                        pe.wait_ge(N["pTe"], u - 1)
                    for b in range(k):
                        last = pe.transpose(K.ps[:, 4 + u % 2, b * P:(b + 1) * P],
                                            LG[:, n % 4, (b0 + b) * P:(b0 + b + 1) * P], K.ident[:])
                    last.then_inc(N["pT"], 1)

                def values(u):
                    n, b0, k = units[u]
                    h, t = its[n]
                    pe.wait_ge(N["pTe"], u + 1)
                    if n >= 1 and b0 == 0:
                        pe.wait_ge(N["od"], n)
                    for b in range(k):
                        last = pe.matmul(K.ps[:, 6, 0:P], PT[:, u % 2, b], V[:, b0 + b, h],
                                         start=(b0 + b == 0), stop=(b0 + b == nb[n] - 1))
                    last.then_inc(N["v"], 1)

                def turn_back(n):
                    pe.wait_ge(N["od"], n + 1)
                    if n >= 1:
                        pe.wait_ge(N["oe"], n)
                    pe.transpose(K.ps[:, 3, 0:P], OQ[:, n % 2], K.ident[:]
                                 ).then_inc(N["b"], 1)

                def decode(n):
                    if n == LOGF and fox:
                        pe.wait_ge(M["qr"], 1)
                        pe.wait_ge(M["lf_in"], 16 * R)
                        for g in range(NP):
                            last = pe.transpose(BANK[0:R, g * P:(g + 1) * P], LF[:, g].rearrange("p b h -> p (b h)"),
                                                K.ident[:])
                        last.then_inc(M["lfT"], 1)
                    if n == MAX:
                        pe.wait_ge(M["sc"], NB)
                        if fox:
                            pe.wait_ge(M["lfs"], 1)
                        for g in range(NP):
                            last = pe.transpose(BANK[0:R, g * P:(g + 1) * P], SB[:, g].rearrange("p b h -> p (b h)"),
                                                K.ident[:])
                        last.then_inc(M["scT"], 1)
                    if n == TURN:
                        pe.wait_ge(M["p"], 1)
                        for g in range(NP):
                            last = pe.transpose(BANK[:, g * R:(g + 1) * R], DL[:, g * P:(g + 1) * P],
                                                K.ident[0:R, 0:R])
                        last.then_inc(M["pT"], 1)
                    if n in values_at:
                        b = values_at[n]
                        pe.wait_ge(M["pTe"], 1)
                        pe.wait_ge(M[f"v_in{b % 2}"], per_load * (b // 2 + 1))
                        for h in range(H):
                            r = b * H + h
                            for g in range(NP):
                                last = pe.matmul(BANK[:, r:r + 1], KV[b % 2][:, g, h], PC[:, g, r:r + 1],
                                                 start=(g == 0), stop=(g == NP - 1))
                        last.then_inc(M["o"], 1)
                    if n == NEW and fox:
                        pe.wait_ge(M["newv"], 1)
                        pe.wait_ge(M["oa"], 1)
                        pe.matmul(BANK[:, 0:R], V3[:], K.ident[0:R, 0:R], start=True, stop=True
                                  ).then_inc(M["newT"], 1)

                for h in range(H):
                    last = pe.transpose(BANK[0:NB, h * P:(h + 1) * P], K.OT[:, h, SEQ:TOK], K.ident[:])
                last.then_inc(M["q"], 1)
                scores(0)
                scores(1)
                for n in range(len(its)):
                    if n + 2 < len(its):
                        scores(n + 2)
                    for u in of_tile[n]:
                        turn(u)
                        if u >= 1:
                            values(u - 1)
                    if n >= 2:
                        turn_back(n - 2)
                    decode(n)
                values(len(units) - 1)
                turn_back(len(its) - 2)
                turn_back(len(its) - 1)

            @block.vector
            def _(dve):
                v = K.V(dve)
                if fox:
                    dve.wait_ge(N["mask"], 1)

                def logits(n):
                    h, t = its[n]
                    w = nb[n] * P
                    if n >= 4:
                        dve.wait_ge(N["pT"], of_tile[n - 4][-1] + 1)
                    lg = LG[:, n % 4, 0:w]
                    rq = RQ[:, h, t:t + 1]
                    if fox:
                        dve.wait_ge(N["rel"], n + 1)
                    for x in half_of[n]:
                        _, a, m = halves[x]
                        dve.wait_ge(N["s"], x + 1)
                        if fox:
                            ins = dve.scalar_tensor_tensor(lg[:, a:a + m], K.ps[:, x % 3, 0:m], rq,
                                                           lg[:, a:a + m], ALU.mult, ALU.subtract)
                        else:
                            ins = dve.tensor_scalar(lg[:, a:a + m], K.ps[:, x % 3, 0:m], rq, None, ALU.mult)
                        ins.then_inc(N["lg"], 1)
                    dve.wait_ge(N["lg"], half_of[n][-1] + 1)
                    if fox:
                        v.do(dve.tensor_tensor(lg[:, w - P:w], lg[:, w - P:w], MK[:], ALU.add))
                    dve.tensor_reduce(NM[:, n % 4:n % 4 + 1], lg, AX.X, ALU.max, negate=True).then_inc(N["max"], 1)

                def invert_sum(n):
                    dve.wait_ge(N["exp"], n + 1)
                    dve.reciprocal(RS[:, n % 4:n % 4 + 1], RS[:, n % 4:n % 4 + 1]).then_inc(N["rs"], 1)

                def decode_queries():
                    dve.wait_ge(M["qsq"], 1)
                    v.do(dve.tensor_reduce(QS[:], QR, AX.X, ALU.add))
                    v.do(dve.tensor_scalar(QS[:], QS[:], 1.0 / P, EPS, ALU.mult, ALU.add))
                    rsqrt(v, QS[:], QN[:], QM[:])
                    v.do(dve.tensor_scalar(QN[:], QN[:], SCALE, None, ALU.mult))
                    v.do(dve.tensor_tensor(QR, heads(BANK[0:NB]), QN[:].unsqueeze(2).broadcast_to([NB, H, P]),
                                           ALU.mult))
                    dve.tensor_tensor(QR, QR, w_bc[0:NB].unsqueeze(1).broadcast_to([NB, H, P]), ALU.mult
                                      ).then_inc(M["qr"], 1)

                def decode_keys(b):
                    dve.wait_ge(M[f"k_in{b % 2}"], per_load * (b // 2 + 1))
                    dve.wait_ge(M[f"qb{b % 2}"], 16 * (b // 2 + 1))
                    kv = KV[b % 2]
                    flat = kv.rearrange("p g h d -> p g (h d)")
                    dve.tensor_tensor(flat, flat, QB[:, b % 2].unsqueeze(1).broadcast_to([P, NP, H * P]), ALU.mult
                                      ).then_inc(M["used"], 1)
                    dve.wait_ge(M["used"], b + 1)
                    dve.tensor_reduce(SB[:, :, b], kv, AX.X, ALU.add).then_inc(M["sc"], 1)

                def decode_sum_logf():
                    dve.wait_ge(M["q_out"], 16)
                    dve.wait_ge(M["used"], NB)
                    dve.wait_ge(M["lfT"], 1)
                    dve.wait_ge(M["row_in"], 64)
                    v.do(dve.memset(DL, 1.0))
                    dve.tensor_tensor_scan(CC, DL, BANK[0:R, 0:PW], 0.0, ALU.mult, ALU.add).then_inc(M["lfs"], 1)
                    dve.wait_ge(M["lfs"], 1)
                    v.do(dve.tensor_tensor(LN[:], LN[:], CC[:, PW - 1:PW], ALU.add))
                    v.do(dve.tensor_scalar(CC, CC, LN[:, 0:1], None, ALU.subtract))

                def decode_max():
                    dve.wait_ge(M["scT"], 1)
                    if fox:
                        v.do(dve.tensor_tensor(DL, BANK[0:R, 0:PW], CC, ALU.subtract))
                        v.do(dve.tensor_tensor(Q3[:], Q3[:], K3[:], ALU.mult))
                        v.do(dve.tensor_reduce(SN[:, 0:1], Q3[:], AX.X, ALU.add))
                        v.do(dve.tensor_reduce(DM[:], DL, AX.X, ALU.max))
                        v.do(dve.tensor_tensor(DM[:], DM[:], SN[:, 0:1], ALU.max))
                        dve.tensor_scalar(DM[:], DM[:], -1.0, None, ALU.mult).then_inc(M["max"], 1)
                    else:
                        dve.wait_ge(M["q_out"], 16)
                        v.do(dve.tensor_copy(DL, BANK[0:R, 0:PW]))
                        dve.tensor_reduce(DM[:], DL, AX.X, ALU.max, negate=True).then_inc(M["max"], 1)

                def decode_normalise():
                    dve.wait_ge(M["exp"], 1)
                    if fox:
                        v.do(dve.tensor_tensor(DS[:], DS[:], SN[:, 1:2], ALU.add))
                    v.do(dve.reciprocal(DS[:], DS[:]))
                    dve.tensor_scalar(DL, DL, DS[:, 0:1], None, ALU.mult).then_inc(M["p"], 1)
                    if fox:
                        v.do(dve.tensor_tensor(SN[:, 2:3], SN[:, 1:2], DS[:], ALU.mult))
                        dve.tensor_scalar(V3[:], V3[:], SN[:, 2:3], None, ALU.mult).then_inc(M["newv"], 1)

                def decode_add_new():
                    dve.wait_ge(M["newT"], 1)
                    dve.wait_ge(M["oa"], 1)
                    v.do(dve.tensor_tensor(K.OT[:, :, SEQ:TOK].rearrange("p h b -> p b h"),
                                           OA[:].rearrange("p (b h) -> p b h", b=NB),
                                           BANK[:, 0:R].rearrange("p (b h) -> p b h", b=NB), ALU.add))

                logits(0)
                logits(1)
                for n in range(len(its)):
                    if n + 2 < len(its):
                        logits(n + 2)
                    invert_sum(n)
                    if n == 0:
                        decode_queries()
                    if n in keys_at:
                        decode_keys(keys_at[n])
                    if n == LOGF and fox:
                        decode_sum_logf()
                    if n == MAX:
                        decode_max()
                    if n == EXP:
                        decode_normalise()
                    if n == LAST and fox:
                        decode_add_new()

            @block.scalar
            def _(act):
                a = K.A(act)

                def exps(n):
                    w = nb[n] * P
                    act.wait_ge(N["max"], n + 1)
                    act.activation(LG[:, n % 4, 0:w], LG[:, n % 4, 0:w], ACT.Exp, bias=NM[:, n % 4:n % 4 + 1],
                                   accum_out=RS[:, n % 4:n % 4 + 1]).then_inc(N["exp"], 1)

                def turned(u):
                    k = units[u][2]
                    act.wait_ge(N["pT"], u + 1)
                    if u >= 2:
                        act.wait_ge(N["v"], u - 1)
                    act.activation(PT[:, u % 2, 0:k], heads(K.ps[:, 4 + u % 2])[:, 0:k], ACT.Identity
                                   ).then_inc(N["pTe"], 1)

                def divide(n):
                    act.wait_ge(N["v"], of_tile[n][-1] + 1)
                    act.wait_ge(N["rs"], n + 1)
                    if n >= 2:
                        act.wait_ge(N["b"], n - 1)
                    act.activation(OQ[:, n % 2], K.ps[:, 6, 0:P], ACT.Identity,
                                   scale=RS[:, n % 4:n % 4 + 1]).then_inc(N["od"], 1)

                def out(n):
                    h, t = its[n]
                    act.wait_ge(N["b"], n + 1)
                    act.activation(K.OT[:, h, t * P:(t + 1) * P], K.ps[:, 3, 0:P], ACT.Identity).then_inc(N["oe"], 1)

                def decode(n):
                    if n == EXP:
                        act.wait_ge(M["max"], 1)
                        last = act.activation(DL, DL, ACT.Exp, bias=DM[:], accum_out=DS[:])
                        if fox:
                            a.step(last)
                            last = act.activation(SN[:, 1:2], SN[:, 0:1], ACT.Exp, bias=DM[:])
                        last.then_inc(M["exp"], 1)
                    if n == TURN:
                        act.wait_ge(M["pT"], 1)
                        act.activation(PC[:].rearrange("p g r -> p (g r)"), BANK[:, 0:NP * R], ACT.Identity
                                       ).then_inc(M["pTe"], 1)
                    if n == TAKE:
                        act.wait_ge(M["o"], NB)
                        dst = K.OT[:, :, SEQ:TOK].rearrange("p h b -> p b h")
                        act.activation(OA[:].rearrange("p (b h) -> p b h", b=NB) if fox else dst,
                                       BANK[:, 0:R].rearrange("p (b h) -> p b h", b=NB), ACT.Identity
                                       ).then_inc(M["oa"], 1)

                act.wait_ge(M["q"], 1)
                act.activation(QR, heads(BANK[0:NB]), ACT.Square).then_inc(M["qsq"], 1)
                exps(0)
                for n in range(len(its)):
                    if n + 1 < len(its):
                        exps(n + 1)
                    for u in of_tile[n]:
                        turned(u)
                        if n >= 1 and u == of_tile[n][0]:
                            divide(n - 1)
                    if n >= 2:
                        out(n - 2)
                    decode(n)
                divide(len(its) - 1)
                out(len(its) - 2)
                out(len(its) - 1)


def memory_norm(K, MH, ML):
    nc, i = K.nc, K.i
    with ExitStack() as c:
        sb = lambda n_, s, d=F32: c.enter_context(nc.sbuf_tensor("y" + n_, s, d))
        X = sb("_x", [P, 2, D])
        SQ = sb("_sq", [P, D])
        SS, RS, TM = sb("_ss", [P, 2]), sb("_rs", [P, 2]), sb("_tm", [P, 2])
        x_in, sq, sc = K.sem("mem_in"), K.sem("mem_sq"), K.sem("mem_scaled")
        tr, hi, lo = K.sem("mem_tr"), K.sem("mem_hi"), K.sem("mem_lo")
        with nc.Block(no_gpsimd_drain=True) as block:
            @block.sync
            def _(sp):
                for t in range(2):
                    sp.dma_start(X[:, t], i["mem_prompt"][0, t * P:(t + 1) * P]).then_inc(x_in, 16)

            @block.scalar
            def _(act):
                act.wait_ge(x_in, 32)
                for t in range(2):
                    act.activation(SQ[:], X[:, t], ACT.Square, accum_out=SS[:, t:t + 1]).then_inc(sq, 1)
                    act.wait_ge(sq, t + 1)
                for k in range(KD):
                    act.wait_ge(tr, k + 1)
                    w = K.par[:, PROW["mem_norm_w"] + k:PROW["mem_norm_w"] + k + 1]
                    act.activation(MH[:, k], K.ps[:, k % 4, 0:MEM], ACT.Identity, scale=w).then_inc(hi, 1)

            @block.vector
            def _(dve):
                v = K.V(dve)
                dve.wait_ge(sq, 2)
                v.do(dve.tensor_scalar(SS[:], SS[:], 1.0 / D, EPS, ALU.mult, ALU.add))
                rsqrt(v, SS[:], RS[:], TM[:])
                for t in range(2):
                    dve.tensor_scalar(X[:, t], X[:, t], RS[:, t:t + 1], None, ALU.mult).then_inc(sc, 1)
                for k in range(KD):
                    dve.wait_ge(hi, k + 1)
                    w = K.par[:, PROW["mem_norm_w"] + k:PROW["mem_norm_w"] + k + 1]
                    dve.scalar_tensor_tensor(ML[:, k], K.ps[:, k % 4, 0:MEM], w, MH[:, k].bitcast(F32), ALU.mult,
                                             ALU.subtract).then_inc(lo, 1)

            @block.tensor
            def _(pe):
                pe.wait_ge(sc, 2)
                for k in range(KD):
                    if k >= 4:
                        pe.wait_ge(lo, k - 3)
                    for t in range(2):
                        last = pe.transpose(K.ps[:, k % 4, t * P:(t + 1) * P], X[:, t, k * P:(k + 1) * P], K.ident[:])
                    last.then_inc(tr, 1)


def build(nc, ins, outs):
    with ExitStack() as ctx:
        K = Kernel(nc, ins, outs, ctx)
        dram = lambda name, shape: nc.dram_tensor(name, shape, F32).ap()
        K.d_rows = dram("rows_g_c_beta", (3, H, SEQ))
        K.d_ab = dram("decode_alpha_beta_rows", (2, H, NB))
        K.d_lf = dram("decode_logf", (NB, H))
        K.d_qk = dram("decode_qk", (2, NB, H, P))
        K.d_q = dram("decode_q", (NB, H, P))

        at = {}

        def plan(name, n, label=None):
            at[label or name] = len(K.tiles)
            K.plan_in(name, n)

        def plan_merge(n):
            at[f"merge{n}"] = len(K.tiles)
            wb = ins["w_branch"][0, n]
            for d in range(KD):
                a = OFF["gate"] + n * D + d * P
                K.plan(ins["w_in"][0, :, a:a + P].rearrange("(k p) c -> p k c", p=P), KD, "act")
                K.plan(wb[:, d * P:(d + 1) * P].rearrange("(k p) c -> p k c", p=P), 4, "dve")

        plan("dn_qkv", 12)
        plan("dn_z", 4)
        plan_merge(0)
        plan("lru_x", 4)
        plan("lru_g", 4)
        plan_merge(1)
        plan("fk", 4)
        plan("fv", 4)
        plan("fq", 4)
        plan("fg", 4)
        plan_merge(2)
        at["mem_kv"] = len(K.tiles)
        for e in range(8):
            K.plan(ins["w_mem_kv"][0, :, e * P:(e + 1) * P].rearrange("(k p) c -> p k c", p=P), KD, "act")
        plan("mq", 4)
        plan("mg", 4)
        plan_merge(3)
        at["w_out"] = len(K.tiles)
        for e in range(KD):
            K.plan(ins["w_out"][0, :, e * P:(e + 1) * P].rearrange("(k p) c -> p k c", p=P), KD, "act")

        def branch_end(t_gate, name, n, tag):
            with ExitStack() as c:
                K.brH = c.enter_context(nc.sbuf_tensor(tag + "_brH", [P, H, TOK], F32R))
                K.brL = c.enter_context(nc.sbuf_tensor(tag + "_brL", [P, H, TOK], F32R))
                gate_branch(K, t_gate, name, K.OT, tag)
                merge_branch(K, at[f"merge{n}"], n)
            K.stage_ends()

        setup(K)
        small_columns(K)
        conv_tiles(K, at["dn_qkv"], 12, "dn_conv_w", 0, K.hpar, True,
                   lambda j: K.OT[:, j] if j < H else K.merged[:, j - H], "ca", "dn_conv", "dn_conv_s")
        delta_rule(K)
        delta_decode(K)
        branch_end(at["dn_z"], "dn_z", 0, "ga")
        conv_tiles(K, at["lru_x"], 4, "lru_conv_w", 12, K.par, False, lambda j: K.OT[:, j], "cb", "lru_conv",
                   "lru_conv_s")
        lru(K)
        branch_end(at["lru_g"], "lru_g", 1, "gb")
        sizes = [P] * TT8 + [NB]
        cols = lambda j: slice(j * P, j * P + sizes[j])
        rows_of = lambda p, s: [outs[p][0, 0, t * P:(t + 1) * P] for t in range(TT8)] + [outs[s][0, :, 0]]
        with ExitStack() as c:
            sb = lambda n_, s: c.enter_context(nc.sbuf_tensor(n_, s, F32))
            KX = sb("fox_kT", [P, H, TOK])
            VR = sb("fox_v_rows", [P, TT8, H, P])
            RQ = sb("fox_rq", [P, H, TT8])
            with nc.sbuf_tensor("fox_vT", [P, H, TOK], F32) as VX, \
                    nc.sbuf_tensor("fox_v_new_rows", [NB, H, P], F32) as VS:
                with nc.sbuf_tensor("fox_k_new_rows", [NB, H, P], F32) as KS:
                    project_tiles(K, at["fk"], 4, BROW["fk"], KX, "fk")
                    KR = K.OT[:].rearrange("p h t -> p (h t)")[:, 0:SEQ * H].rearrange(
                        "p (t h d) -> p t h d", t=TT8, h=H)
                    k_rows = [KR[:, j] for j in range(TT8)] + [KS[:]]
                    turns = RowTurns(K, "fkr")
                    after = [turns.out(j // 5, KX[:, :, cols(j)], k_rows[j], n) for j, n in enumerate(sizes)]
                    w = K.par[:, PROW["fox_qn_w"]:PROW["fox_qn_w"] + 1]
                    for j, n in enumerate(sizes):
                        turns.back(2 + j // 5, k_rows[j], KX[:, :, cols(j)], n, w, j + 1)
                    project_tiles(K, at["fv"], 4, BROW["fv"], VX, "fv", turns=turns,
                                  rows=(k_rows, sizes, K.knw, after),
                                  stores=[((turns.normed, j + 1), d, k_rows[j])
                                          for j, d in enumerate(rows_of("fox_k", "fox_k_s"))])
                v_rows = [VR[:, j] for j in range(TT8)] + [VS[:]]
                turns = RowTurns(K, "fvr")
                after = [turns.out(j // 3, VX[:, :, cols(j)], v_rows[j], n) for j, n in enumerate(sizes)]
                project_tiles(K, at["fq"], 4, BROW["fq"], K.OT, "fq", turns=turns, RQ=RQ, preload=False,
                              stores=[((turns.moved, after[j]), d, v_rows[j])
                                      for j, d in enumerate(rows_of("fox_v", "fox_v_s"))])
            attend(K, KX, VR, RQ, "fa", True)
        branch_end(at["fg"], "fg", 2, "gc")
        with ExitStack() as c:
            sb = lambda n_, s, d=F32: c.enter_context(nc.sbuf_tensor(n_, s, d))
            KX, VX = sb("mem_kT", [P, H, MEM]), sb("mem_vT", [P, H, MEM])
            KR, VR = sb("mem_k_rows", [P, 2, H, P]), sb("mem_v_rows", [P, 2, H, P])
            RQ = sb("mem_rq", [P, H, TT8])
            with ExitStack() as c2:
                MH = c2.enter_context(nc.sbuf_tensor("memH", [P, KD, MEM], F32R))
                ML = c2.enter_context(nc.sbuf_tensor("memL", [P, KD, MEM], F32R))
                memory_norm(K, MH, ML)
                t = at["mem_kv"]
                project_tiles(K, t, 4, None, KX, "mk", x=(MH, ML), cols=MEM)
                project_tiles(K, t + 4, 4, None, VX, "mv", x=(MH, ML), cols=MEM)
            turns = RowTurns(K, "mr")
            cols = lambda j: slice(j * P, (j + 1) * P)
            after = [turns.out(0, KX[:, :, cols(j)], KR[:, j], P) for j in range(2)]
            v_after = [turns.out(1, VX[:, :, cols(j)], VR[:, j], P) for j in range(2)]
            w = K.par[:, PROW["mem_qn_w"]:PROW["mem_qn_w"] + 1]
            for j in range(2):
                turns.back(2, KR[:, j], KX[:, :, cols(j)], P, w, j + 1)
            tile = lambda p, j: outs[p][0, 0, j * P:(j + 1) * P]
            project_tiles(K, at["mq"], 4, BROW["mq"], K.OT, "mq", turns=turns, RQ=RQ, preload=False,
                          rows=([KR[:, j] for j in range(2)], [P, P], K.mknw, after),
                          stores=[((turns.normed, j + 1), tile("mem_k", j), KR[:, j]) for j in range(2)] +
                                 [((turns.moved, v_after[j]), tile("mem_v", j), VR[:, j]) for j in range(2)])
            attend(K, KX, VR, RQ, "ma", False)
        branch_end(at["mg"], "mg", 3, "gd")
        K.OT_space.close()
        output(K, at["w_out"])


INS = ["x_prompt", "x_sample", "cache_fox_k", "cache_fox_v", "cache_fox_logf", "cache_mem_k", "cache_mem_v",
       "state_dn", "state_dn_conv", "state_lru_h", "state_lru_conv", "page_table", "mem_prompt", "norm_w", "w_in",
       "b_in", "dn_conv_w", "dn_A_log", "dn_dt_bias", "dn_onorm_w", "lru_conv_w", "lru_conv_b", "lru_w_r",
       "lru_b_r", "lru_w_i", "lru_b_i", "lru_lambda", "fox_qn_w", "fox_kn_w", "mem_norm_w", "w_mem_kv",
       "mem_qn_w", "mem_kn_w", "w_branch", "w_out"]
OUTS = [("y", (1, SEQ, D)), ("y_s", (NB, 1, D)),
        ("fox_k", (1, 1, SEQ, H, P)), ("fox_v", (1, 1, SEQ, H, P)), ("fox_logf", (1, 1, SEQ, H)),
        ("mem_k", (1, 1, MEM, H, P)), ("mem_v", (1, 1, MEM, H, P)), ("dn_state", (1, 1, H, P, P)),
        ("dn_conv", (1, 1, 3, 1536)), ("lru_h", (1, 1, BW)), ("lru_conv", (1, 1, 3, BW)),
        ("fox_k_s", (1, NB, 1, H, P)), ("fox_v_s", (1, NB, 1, H, P)), ("fox_logf_s", (1, NB, 1, H)),
        ("dn_state_s", (1, NB, H, P, P)), ("dn_conv_s", (1, NB, 3, 1536)), ("lru_h_s", (1, NB, BW)),
        ("lru_conv_s", (1, NB, 3, BW))]


def kernel(**inputs):
    import concourse.bacc as bacc
    import numpy as np
    from concourse.bass_utils import run_bass_kernel_spmd

    nc = bacc.Bacc("TRN2", target_bir_lowering=False, num_devices=1)
    arrays, ins, outs = {}, {}, {}
    for name in INS:
        a = np.ascontiguousarray(inputs[name])
        arrays["in_" + name] = a
        ins[name] = nc.dram_tensor("in_" + name, a.shape, mybir.dt.from_np(a.dtype), kind="ExternalInput").ap()
    for name, shape in OUTS:
        outs[name] = nc.dram_tensor("out_" + name, shape, F32, kind="ExternalOutput").ap()
    build(nc, ins, outs)
    r = run_bass_kernel_spmd(nc, [arrays], core_ids=[0])
    return tuple(r.results[0]["out_" + name] for name, _ in OUTS)
```

```python
from contextlib import ExitStack

import concourse.bass as bass
from concourse import mybir

F32 = mybir.dt.float32
F32R = mybir.dt.float32r
I32 = mybir.dt.int32
I8 = mybir.dt.int8
ALU = mybir.AluOpType
ACT = mybir.ActivationFunctionType
AX = mybir.AxisListType

P = 128
D = 1024
KD = D // P
SEQ = 1024
NB = 8
TOK = SEQ + NB
G3 = TOK // 3
TT8 = SEQ // P
H = 4
BW = 512
CONV = 4
CH = 128
NCH = SEQ // CH
MEM = 256
PAGES = 4
PAGE = 128
PAST = PAGES * PAGE
EPS = 1e-6
LRU_C = 8.0
SCALE = float(P) ** -0.5
NEG = -1e30
RSQRT_SEED = float(0x5F3759DF)

OFF = {}
_o = 0
for _n, _w in (("dn_qkv", 1536), ("dn_z", 512), ("dn_b", 4), ("dn_a", 4), ("lru_x", 512), ("lru_g", 512),
               ("fq", 512), ("fk", 512), ("fv", 512), ("ff", 4), ("fg", 512), ("mq", 512), ("mg", 512),
               ("gate", 4096)):
    OFF[_n] = _o
    _o += _w
BROW = {}
_r = 0
for _n, _w in (("dn_qkv", 12), ("dn_z", 4), ("lru_x", 4), ("lru_g", 4), ("fq", 4), ("fk", 4), ("fv", 4),
               ("fg", 4), ("mq", 4), ("mg", 4), ("gate", 32)):
    BROW[_n] = _r
    _r += _w
NBROW = _r
PROW = {}
_r = 0
for _n, _w in (("dn_conv_w", 48), ("lru_conv_w", 16), ("lru_conv_b", 4), ("lru_b_r", 4), ("lru_b_i", 4),
               ("lru_lambda", 4), ("fox_qn_w", 1), ("mem_qn_w", 1), ("dn_onorm_w", 1), ("norm_w", 8),
               ("mem_norm_w", 8)):
    PROW[_n] = _r
    _r += _w
NPROW = _r


class Steps:

    def __init__(self, eng, sem, state):
        self.eng, self.sem, self.state = eng, sem, state

    def step(self, ins):
        ins.then_inc(self.sem, 1)
        self.state[0] += 1

    def wait(self):
        self.eng.wait_ge(self.sem, self.state[0])

    def do(self, ins):
        self.step(ins)
        self.wait()


def heads(ap):
    return ap.rearrange("p (h d) -> p h d", h=H)


def rsqrt(v, x, y, t):
    eng = v.eng
    yi, yf = y.bitcast(I32), y
    v.do(eng.tensor_scalar(yi, x.bitcast(I32), 1, None, ALU.logical_shift_right))
    v.do(eng.tensor_scalar(yi, yi, -1.0, RSQRT_SEED, ALU.mult, ALU.add))
    for _ in range(3):
        v.do(eng.tensor_tensor(t, yf, yf, ALU.mult))
        v.do(eng.scalar_tensor_tensor(t, t, -0.5, x, ALU.mult, ALU.mult))
        v.do(eng.scalar_tensor_tensor(yf, t, 1.5, yf, ALU.add, ALU.mult))


def log1p_exp(v, z, u, s, s2, acc):
    eng = v.eng
    v.do(eng.tensor_scalar(s, u, 2.0, None, ALU.add))
    v.do(eng.reciprocal(s, s))
    v.do(eng.tensor_tensor(s, s, u, ALU.mult))
    v.do(eng.tensor_tensor(s2, s, s, ALU.mult))
    v.do(eng.tensor_scalar(acc, s2, 1.0 / 17, None, ALU.mult))
    for c in (15, 13, 11, 9, 7, 5, 3):
        v.do(eng.scalar_tensor_tensor(acc, acc, 1.0 / c, s2, ALU.add, ALU.mult))
    v.do(eng.scalar_tensor_tensor(acc, acc, 1.0, s, ALU.add, ALU.mult))
    v.do(eng.tensor_scalar(s, z, 0.0, None, ALU.max))
    v.do(eng.scalar_tensor_tensor(acc, acc, 2.0, s, ALU.mult, ALU.add))


class Kernel:

    def __init__(self, nc, ins, outs, ctx):
        self.nc, self.i, self.o, self.ctx = nc, ins, outs, ctx
        sb = lambda n, s, d=F32: ctx.enter_context(nc.sbuf_tensor(n, s, d))
        sem = lambda n: ctx.enter_context(nc.semaphore(n))
        self.hH, self.hL = sb("hH", [P, KD, TOK], F32R), sb("hL", [P, KD, TOK], F32R)
        self.slots_at = nc.sbuf_base
        self.raw = sb("w_raw", [P, 2, KD, P])
        self.wH, self.wL = sb("wH", [P, 2, KD, P], F32R), sb("wL", [P, 2, KD, P], F32R)
        self.ident = sb("ident", [P, P])
        self.ones = sb("ones", [P, 1])
        self.bias, self.hbias = sb("bias", [P, NBROW]), sb("half_bias", [P, NBROW])
        self.par, self.hpar = sb("par", [P, NPROW]), sb("half_par", [P, NPROW])
        self.TK = sb("token_scalars", [P, TT8, 3, H])
        self.knw, self.mknw = sb("fox_kn_bc", [P, P]), sb("mem_kn_bc", [P, P])
        self.qnw, self.mqnw = sb("fox_qn_bc", [P, P]), sb("mem_qn_bc", [P, P])
        self.alpha = sb("decode_alpha_beta", [P, 2, H, NB])
        self.convs = sb("conv_states", [P, 16, 32])
        self.ps = ctx.enter_context(nc.psum_tensor("ps", [P, 8, 512], F32))
        self.merged = sb("merged", [P, KD, TOK])
        self.OT_space = ExitStack()
        self.OT = self.OT_space.enter_context(nc.sbuf_tensor("branch_in", [P, H, TOK], F32))
        self.w_loaded = [sem("w_loaded0"), sem("w_loaded1")]
        self.w_hi, self.w_lo = sem("w_hi"), sem("w_lo")
        self.tile_done = sem("tile_done")
        self.evac_act, self.evac_dve = sem("evac_act"), sem("evac_dve")
        self.tiles = []
        self.at_load = self.at_hi = self.at_lo = 0
        self.v_sem, self.v_n = sem("vector_step"), [0]
        self.a_sem, self.a_n = sem("scalar_step"), [0]
        self.p_sem, self.p_n = sem("pool_step"), [0]
        self.stored, self.n_stored = sem("stored"), 0
        self.y_out = [sem(f"y_out{q}") for q in range(6)]
        self.stage = []

    def sem(self, name):
        s = self.nc.alloc_semaphore(name=name)
        self.stage.append(s)
        return s

    def stage_ends(self):
        self.nc.clear_and_free_semaphores(self.stage)
        self.nc.all_engine_barrier()
        self.stage = []

    def borrowed(self, name, slot, shape):
        return self.nc.alloc_sbuf_tensor_at(name, shape, F32, offset=self.slots_at + slot * 2 * KD * P * 4)

    def V(self, eng):
        return Steps(eng, self.v_sem, self.v_n)

    def A(self, eng):
        return Steps(eng, self.a_sem, self.a_n)

    def G(self, eng):
        return Steps(eng, self.p_sem, self.p_n)

    def store(self, eng, dst, src):
        eng.dma_start(dst, src).then_inc(self.stored, 16)
        self.n_stored += 16

    def plan(self, src, nk, evac):
        self.tiles.append((src, nk, evac))

    def plan_in(self, name, n, evac="act"):
        for t in range(n):
            a = OFF[name] + t * P
            self.plan(self.i["w_in"][0, :, a:a + P].rearrange("(k p) c -> p k c", p=P), KD, evac)

    def loads(self, sp, upto):
        for t in range(self.at_load, min(upto, len(self.tiles))):
            src, nk, _ = self.tiles[t]
            if t >= 2:
                sp.wait_ge(self.w_lo, t - 1)
            sp.dma_start(self.raw[:, t % 2, 0:nk], src).then_inc(self.w_loaded[t % 2], 16)
            self.at_load = t + 1

    def split_hi(self, act, upto):
        for t in range(self.at_hi, min(upto, len(self.tiles))):
            nk = self.tiles[t][1]
            act.wait_ge(self.w_loaded[t % 2], 16 * (t // 2 + 1))
            if t >= 2:
                act.wait_ge(self.tile_done, t - 1)
            act.activation(self.wH[:, t % 2, 0:nk], self.raw[:, t % 2, 0:nk], ACT.Identity).then_inc(self.w_hi, 1)
            self.at_hi = t + 1

    def split_lo(self, pool, upto):
        for t in range(self.at_lo, min(upto, len(self.tiles))):
            nk = self.tiles[t][1]
            pool.wait_ge(self.w_hi, t + 1)
            pool.tensor_tensor(self.wL[:, t % 2, 0:nk], self.raw[:, t % 2, 0:nk],
                               self.wH[:, t % 2, 0:nk].bitcast(F32), ALU.subtract).then_inc(self.w_lo, 1)
            self.at_lo = t + 1

    def psum(self, t):
        return self.ps[:, 3 * (t % 2):3 * (t % 2) + 3, 0:G3]

    def emptied(self, t):
        kind = self.tiles[t][2]
        n = sum(1 for x in self.tiles[:t + 1] if x[2] == kind)
        return (self.evac_act if kind == "act" else self.evac_dve), n

    def project(self, pe, t, xH, xL, groups=3, cols=None, meanwhile=None):
        _, nk, _ = self.tiles[t]
        pe.wait_ge(self.w_lo, t + 1)
        if t >= 2:
            pe.wait_ge(*self.emptied(t - 2))
        width = TOK // 3 if groups == 3 else cols
        for k in range(nk):
            for n, (w, x) in enumerate(((self.wH, xH), (self.wH, xL), (self.wL, xH))):
                for g in range(groups):
                    last = pe.matmul(self.ps[:, 3 * (t % 2) + g, 0:width], w[:, t % 2, k],
                                     x[:, k, g * width:(g + 1) * width],
                                     start=(k == 0 and n == 0), stop=(k == nk - 1 and n == 2))
            if k == nk - 1:
                last.then_inc(self.tile_done, 1)
            if meanwhile:
                meanwhile(k)


def setup(K):
    nc, i = K.nc, K.i
    with ExitStack() as c:
        sb = lambda n, s, d=F32: c.enter_context(nc.sbuf_tensor(n, s, d))
        X = sb("x_rows", [P, TT8 + 1, D])
        SQ = sb("x_square", [P, D])
        SS, RS, TM = sb("x_ss", [P, 9]), sb("x_rstd", [P, 9]), sb("x_tm", [P, 9])
        BR, PR = sb("bias_rows", [NBROW, P]), sb("par_rows", [NPROW, P])
        ST = sb("state_rows", [24, 1536])
        SL = sb("lru_state_rows", [32, 512])
        x_in, par_in = [K.sem(f"x_in{t}") for t in range(9)], K.sem("par_in")
        made, squared, scaled = K.sem("constants_made"), K.sem("x_squared"), K.sem("x_scaled")
        tabT, tab = K.sem("tables_transposed"), K.sem("tables_ready")
        filled = K.sem("x_ss_filled")
        xT, hi, lo = K.sem("x_transposed"), K.sem("h_hi"), K.sem("h_lo")
        par_dmas = []

        def par(dst, src):
            par_dmas.append((dst, src))

        rows = lambda ap: ap.rearrange("(r p) -> r p", p=P)
        segments = [("dn_qkv", 16), ("lru_x", 20), ("fg", 4), ("mq", 40)]
        b = i["b_in"][0]
        for name, n in segments:
            par(BR[BROW[name]:BROW[name] + n, :], rows(b[OFF[name]:OFF[name] + n * P]))
        par(PR[PROW["dn_conv_w"]:PROW["dn_conv_w"] + 48, :], i["dn_conv_w"][0].rearrange("j (t p) -> (j t) p", p=P))
        par(PR[PROW["lru_conv_w"]:PROW["lru_conv_w"] + 16, :], i["lru_conv_w"][0].rearrange("j (t p) -> (j t) p", p=P))
        for name, n in (("lru_conv_b", 4), ("lru_b_r", 4), ("lru_b_i", 4), ("lru_lambda", 4), ("fox_qn_w", 1),
                        ("mem_qn_w", 1), ("dn_onorm_w", 1), ("norm_w", 8), ("mem_norm_w", 8)):
            par(PR[PROW[name]:PROW[name] + n, :], rows(i[name][0]))
        par(ST[:], i["state_dn_conv"][0].rearrange("b j c -> (b j) c"))
        par(SL[0:24, :], i["state_lru_conv"][0].rearrange("b j c -> (b j) c"))
        par(SL[24:32, :], i["state_lru_h"][0])
        for dst, name in ((K.knw, "fox_kn_w"), (K.mknw, "mem_kn_w"), (K.qnw, "fox_qn_w"), (K.mqnw, "mem_qn_w")):
            par(dst[:], i[name][0:1].broadcast_to([P, P]))

        with nc.Block(no_gpsimd_drain=True) as block:
            @block.sync
            def _(sp):
                for t in range(TT8):
                    sp.dma_start(X[:, t], i["x_prompt"][0, t * P:(t + 1) * P]).then_inc(x_in[t], 16)
                sp.dma_start(X[0:NB, TT8], i["x_sample"][:, 0]).then_inc(x_in[TT8], 16)
                for dst, src in par_dmas:
                    sp.dma_start(dst, src).then_inc(par_in, 16)
                K.loads(sp, 2)
                for src, dst in (("state_dn_conv", "dn_conv_s"), ("state_lru_conv", "lru_conv_s")):
                    K.store(sp, K.o[dst][0, :, 0:2], i[src][0, :, 1:3])

            @block.gpsimd
            def _(pool):
                pool.memset(K.ident[:], 0.0).then_inc(made, 1)
                pool.wait_ge(made, 1)
                pool.affine_select(out=K.ident[:], in_=K.ident[:], compare_op=ALU.not_equal, fill=1.0, base=0,
                                   pattern=[[-1, P]], channel_multiplier=1).then_inc(made, 1)
                pool.memset(K.ones[:], 1.0).then_inc(made, 1)
                K.split_lo(pool, 1)

            @block.scalar
            def _(act):
                act.wait_ge(filled, 1)
                a = K.A(act)
                for t in range(9):
                    n = P if t < TT8 else NB
                    act.wait_ge(x_in[t], 16)
                    act.activation(SQ[0:n], X[0:n, t], ACT.Square, accum_out=SS[0:n, t:t + 1]).then_inc(squared, 1)
                    act.wait_ge(squared, t + 1)
                K.split_hi(act, 1)
                act.wait_ge(tabT, 1)
                a.do(act.activation(K.bias[:], K.ps[:, 6, 0:NBROW], ACT.Identity))
                a.do(act.activation(K.par[:], K.ps[:, 6, 128:128 + NPROW], ACT.Identity))
                act.activation(K.hbias[:], K.bias[:], ACT.Identity, scale=0.5).then_inc(tab, 1)
                act.activation(K.hpar[:], K.par[:], ACT.Identity, scale=0.5).then_inc(tab, 1)
                act.activation(K.convs[:, 0:12, 0:24], K.ps[:, 7, 0:12 * 24].rearrange("p (t r) -> p t r", t=12),
                               ACT.Identity).then_inc(tab, 1)
                act.activation(K.convs[:, 12:16, :], K.ps[:, 7, 288:288 + 128].rearrange("p (t r) -> p t r", t=4),
                               ACT.Identity).then_inc(tab, 1)
                for k in range(KD):
                    q = 3 * (k % 2)
                    act.wait_ge(xT, k + 1)
                    w = K.par[:, PROW["norm_w"] + k:PROW["norm_w"] + k + 1]
                    act.activation(K.hH[:, k, 0:SEQ].rearrange("p (a b) -> p a b", a=2), K.ps[:, q:q + 2, :],
                                   ACT.Identity, scale=w)
                    act.activation(K.hH[:, k, SEQ:TOK], K.ps[:, q + 2, 0:NB], ACT.Identity, scale=w).then_inc(hi, 1)

            @block.vector
            def _(dve):
                v = K.V(dve)
                dve.memset(SS[:], 1.0).then_inc(filled, 1)
                dve.wait_ge(squared, 9)
                v.do(dve.tensor_scalar(SS[:], SS[:], 1.0 / D, EPS, ALU.mult, ALU.add))
                rsqrt(v, SS[:], RS[:], TM[:])
                for t in range(9):
                    n = P if t < TT8 else NB
                    dve.tensor_scalar(X[0:n, t], X[0:n, t], RS[0:n, t:t + 1], None, ALU.mult).then_inc(scaled, 1)
                for k in range(KD):
                    q = 3 * (k % 2)
                    dve.wait_ge(hi, k + 1)
                    w = K.par[:, PROW["norm_w"] + k:PROW["norm_w"] + k + 1]
                    dve.scalar_tensor_tensor(
                        K.hL[:, k, 0:SEQ].rearrange("p (a b) -> p a b", a=2), K.ps[:, q:q + 2, :], w,
                        K.hH[:, k, 0:SEQ].bitcast(F32).rearrange("p (a b) -> p a b", a=2), ALU.mult, ALU.subtract)
                    dve.scalar_tensor_tensor(K.hL[:, k, SEQ:TOK], K.ps[:, q + 2, 0:NB], w,
                                             K.hH[:, k, SEQ:TOK].bitcast(F32), ALU.mult,
                                             ALU.subtract).then_inc(lo, 1)

            @block.tensor
            def _(pe):
                pe.wait_ge(made, 3)
                pe.wait_ge(par_in, 16 * len(par_dmas))
                pe.transpose(K.ps[:, 6, 0:NBROW], BR[:], K.ident[0:NBROW, 0:NBROW])
                pe.transpose(K.ps[:, 6, 128:128 + NPROW], PR[:], K.ident[0:NPROW, 0:NPROW])
                for t in range(12):
                    pe.transpose(K.ps[:, 7, 24 * t:24 * t + 24], ST[:, t * P:(t + 1) * P], K.ident[0:24, 0:24])
                for t in range(4):
                    last = pe.transpose(K.ps[:, 7, 288 + 32 * t:320 + 32 * t], SL[:, t * P:(t + 1) * P],
                                        K.ident[0:32, 0:32])
                last.then_inc(tabT, 1)
                pe.wait_ge(scaled, 9)
                for k in range(KD):
                    q = 3 * (k % 2)
                    if k >= 2:
                        pe.wait_ge(lo, k - 1)
                    for t in range(TT8):
                        pe.transpose(K.ps[:, q + t // 4, (t % 4) * P:(t % 4 + 1) * P], X[:, t, k * P:(k + 1) * P],
                                     K.ident[:])
                    pe.transpose(K.ps[:, q + 2, 0:NB], X[0:NB, TT8, k * P:(k + 1) * P],
                                 K.ident[0:NB, 0:NB]).then_inc(xT, 1)


class SmallColumns:

    DNA, FF, DNB = 0, 32, 64
    M = 96

    def __init__(self, K, sb):
        M = self.M
        self.K = K
        self.W, self.WH, self.WL = sb("sw", [P, KD, M]), sb("swH", [P, KD, M], F32R), sb("swL", [P, KD, M], F32R)
        self.col = sb("sw_cols", [M, 8])
        self.Z, self.SP = sb("sz", [M, TOK]), sb("ssp", [M, TOK])
        self.T1, self.U, self.S, self.S2 = (K.merged[0:M, H + x] for x in range(4))
        self.SC, self.MK = sb("s_scan", [M, SEQ]), sb("s_mask", [M, SEQ])
        self.EX = sb("s_exp", [M, NB])
        self.VT = sb("s_value_rows", [P, TT8 + 1, M])
        self.N = {x: K.sem("small_" + x) for x in
                  ("loaded", "prep", "split", "done", "z", "t1", "u", "val", "beta", "tr", "moved", "out",
                   "rows_out")}

    def pool(self, pool):
        W, col, MK, prep = self.W, self.col, self.MK, self.N["prep"]
        pool.memset(W[:], 0.0)
        pool.memset(col[:], 0.0)
        pool.memset(MK[:], 1.0).then_inc(prep, 1)
        pool.wait_ge(prep, 1)
        pool.memset(MK[0:32].rearrange("p (a b) -> p a b", b=CH)[:, :, 0:1], 0.0)
        pool.memset(col[0:32, 3:4], 1.0)
        pool.memset(col[32:64, 3:4], -1.0)
        pool.memset(col[64:96, 3:4], -1.0).then_inc(prep, 1)
        pool.wait_ge(prep, 2)

    def sync_loads(self, sp):
        i, col, loaded = self.K.i, self.col, self.N["loaded"]
        sp.wait_ge(self.N["prep"], 2)
        for name, r in (("dn_a", self.DNA), ("ff", self.FF), ("dn_b", self.DNB)):
            a = OFF[name]
            sp.dma_start(self.W[:, :, r:r + 4], i["w_in"][0, :, a:a + 4].rearrange("(k p) c -> p k c", p=P)
                         ).then_inc(loaded, 16)
            sp.dma_start(col[r:r + 4, 0:1], i["b_in"][0, a:a + 4].rearrange("(c a) -> c a", a=1)
                         ).then_inc(loaded, 16)
        sp.dma_start(col[0:4, 1:2], i["dn_dt_bias"][0].rearrange("(c a) -> c a", a=1)).then_inc(loaded, 16)
        sp.dma_start(col[0:4, 2:3], i["dn_A_log"][0].rearrange("(c a) -> c a", a=1)).then_inc(loaded, 16)

    def sync_stores(self, sp):
        K, VT, SC, EX, rows_out = self.K, self.VT, self.SC, self.EX, self.N["rows_out"]
        DNA, FF, DNB = self.DNA, self.FF, self.DNB
        sp.wait_ge(self.N["out"], 1)
        for t in range(TT8):
            K.store(sp, K.o["fox_logf"][0, 0, t * P:(t + 1) * P], VT[:, t, FF:FF + 4])
        K.store(sp, K.o["fox_logf_s"][0, :, 0], VT[0:NB, TT8, FF:FF + 4])
        sp.dma_start(K.d_rows[0], SC[DNA:DNA + 4]).then_inc(rows_out, 16)
        sp.dma_start(K.d_rows[1], SC[FF:FF + 4]).then_inc(rows_out, 16)
        sp.dma_start(K.d_rows[2], SC[DNB:DNB + 4]).then_inc(rows_out, 16)
        sp.dma_start(K.d_ab[0], EX[DNA:DNA + 4]).then_inc(rows_out, 16)
        sp.dma_start(K.d_ab[1], EX[DNB:DNB + 4]).then_inc(rows_out, 16)
        sp.dma_start(K.d_lf, VT[0:NB, TT8, FF:FF + 4]).then_inc(rows_out, 16)
        sp.wait_ge(rows_out, 96)
        sp.dma_start(K.alpha[:].rearrange("p a h b -> p (a h b)"),
                     K.d_ab.rearrange("a h b -> (a h b)").unsqueeze(0).broadcast_to([P, 64])
                     ).then_inc(rows_out, 16)
        sp.wait_ge(rows_out, 112)

    def act_split(self, act):
        N, col = self.N, self.col
        a = self.K.A(act)
        act.wait_ge(N["loaded"], 16 * 8)
        a.do(act.activation(self.WH[:], self.W[:], ACT.Identity))
        act.activation(col[:, 5:6], col[:, 2:3], ACT.Exp).then_inc(N["split"], 1)

    def act_logits(self, act):
        N, col = self.N, self.col
        act.wait_ge(N["done"], 1)
        act.wait_ge(N["split"], 3)
        act.activation(self.Z[:].rearrange("p (a b) -> p a b", a=3), self.K.ps[0:self.M, 3:6, 0:G3], ACT.Identity,
                       scale=col[:, 3:4], bias=col[:, 4:5]).then_inc(N["z"], 1)
        act.wait_ge(N["t1"], 1)
        act.activation(self.U, self.T1, ACT.Exp).then_inc(N["u"], 1)

    def act_beta(self, act):
        N, DNB = self.N, self.DNB
        act.wait_ge(N["val"], 2)
        act.activation(self.SC[DNB:DNB + 32], self.SP[DNB:DNB + 32, 0:SEQ], ACT.Exp)
        act.activation(self.EX[:], self.SP[:, SEQ:TOK], ACT.Exp).then_inc(N["beta"], 1)

    def act_turned(self, act):
        K, N, M, VT = self.K, self.N, self.M, self.VT
        pair = lambda: K.ps[:, 6:8, 0:4 * M].rearrange("p a (b m) -> p a b m", m=M)
        act.wait_ge(N["tr"], 1)
        for t in range(TT8):
            last = act.activation(K.TK[:, t], K.ps[:, 6 + t // 4, (t % 4) * M:(t % 4 + 1) * M].rearrange(
                "p (g m) -> p g m", g=3)[:, :, 0:H], ACT.Identity)
        last.then_inc(N["moved"], 1)
        act.wait_ge(N["tr"], 2)
        act.activation(VT[:, 0:TT8].rearrange("p (a b) m -> p a b m", a=2), pair(), ACT.Identity
                       ).then_inc(N["moved"], 1)
        act.wait_ge(N["tr"], 3)
        act.activation(VT[0:NB, TT8], K.ps[0:NB, 6, 0:M], ACT.Identity).then_inc(N["out"], 1)

    def dve_split(self, dve):
        N, col = self.N, self.col
        v = self.K.V(dve)
        dve.wait_ge(N["split"], 1)
        dve.tensor_tensor(self.WL[:], self.W[:], self.WH[:].bitcast(F32), ALU.subtract).then_inc(N["split"], 1)
        v.do(dve.scalar_tensor_tensor(col[:, 4:5], col[:, 0:1], col[:, 3:4], col[:, 1:2], ALU.mult, ALU.add))
        dve.tensor_scalar(col[:, 5:6], col[:, 5:6], -1.0, None, ALU.mult).then_inc(N["split"], 1)
        dve.wait_ge(N["split"], 3)

    def dve_values(self, dve):
        N, col, Z, T1, SP, SC = self.N, self.col, self.Z, self.T1, self.SP, self.SC
        v = self.K.V(dve)
        dve.wait_ge(N["z"], 1)
        v.do(dve.tensor_scalar(T1, Z[:], -1.0, None, ALU.mult))
        dve.tensor_tensor(T1, T1, Z[:], ALU.min).then_inc(N["t1"], 1)
        dve.wait_ge(N["u"], 1)
        log1p_exp(v, Z[:], self.U, self.S, self.S2, SP[:])
        dve.tensor_scalar(SP[:], SP[:], col[:, 5:6], None, ALU.mult).then_inc(N["val"], 1)
        dve.wait_ge(N["val"], 1)
        dve.tensor_tensor_scan(SC[:], self.MK[:], SP[:, 0:SEQ], 0.0, ALU.mult, ALU.add).then_inc(N["val"], 1)

    def pe_logits(self, pe):
        K, N = self.K, self.N
        pe.wait_ge(N["split"], 2)
        for k in range(KD):
            for n, (w, x) in enumerate(((self.WH, K.hH), (self.WH, K.hL), (self.WL, K.hH))):
                for g in range(3):
                    last = pe.matmul(K.ps[0:self.M, 3 + g, 0:G3], w[:, k], x[:, k, g * G3:(g + 1) * G3],
                                     start=(k == 0 and n == 0), stop=(k == KD - 1 and n == 2))
        last.then_inc(N["done"], 1)

    def pe_turn(self, pe):
        K, N, M = self.K, self.N, self.M
        pe.wait_ge(N["beta"], 1)
        for x, SRC in enumerate((self.SC, self.SP)):
            if x:
                pe.wait_ge(N["moved"], x)
            for t in range(TT8):
                last = pe.transpose(K.ps[:, 6 + t // 4, (t % 4) * M:(t % 4 + 1) * M], SRC[:, t * P:(t + 1) * P],
                                    K.ident[0:M, 0:M])
            last.then_inc(N["tr"], 1)
        pe.wait_ge(N["moved"], 2)
        pe.transpose(K.ps[0:NB, 6, 0:M], self.SP[:, SEQ:TOK], K.ident[0:M, 0:M]).then_inc(N["tr"], 1)


def conv_tiles(K, t0, n, name, state0, par, silu, OUT, tag, prompt_out, sample_out,
               masks=None, squares=0, small=False):
    nc = K.nc
    PAD = CONV - 1
    taps = PROW[name]
    end_lo = t0 + n if masks else t0 + n + 1
    with ExitStack() as c:
        sb = lambda n_, s, d=F32: c.enter_context(nc.sbuf_tensor(tag + n_, s, d))
        XI = sb("_in", [P, 2, PAD + TOK])
        TH = sb("_th", [P, 2, TOK]) if silu else None
        XL = sb("_last", [P, n, PAD + NB])
        XR = sb("_last_rows", [PAD + NB, n * P])
        SQ = sb("_sq", [P, 2, SEQ]) if squares else None
        padded, conv, th, fin = (K.sem(tag + x) for x in ("_padded", "_conv", "_tanh", "_silu"))
        sq, sums = K.sem(tag + "_sq"), K.sem(tag + "_sums")
        last_tr, last_ev = (K.sem(tag + x) for x in ("_last_turned", "_last_moved"))

        def tap(j, t):
            return par[:, taps + j * n + t:taps + j * n + t + 1]

        small = SmallColumns(K, lambda n_, s, d=F32: c.enter_context(nc.sbuf_tensor(n_, s, d))) if small else None

        with nc.Block(no_gpsimd_drain=True) as block:
            @block.sync
            def _(sp):
                if small:
                    small.sync_loads(sp)
                    K.loads(sp, t0 + 5)
                    small.sync_stores(sp)
                K.loads(sp, t0 + n if masks else t0 + n + 2)
                sp.wait_ge(last_ev, 1)
                K.store(sp, K.o[prompt_out][0, 0], XR[0:PAD])
                K.store(sp, K.o[sample_out][0, :, 2], XR[PAD:PAD + NB])
                sp.wait_ge(K.stored, K.n_stored)

            @block.gpsimd
            def _(pool):
                if small:
                    small.pool(pool)
                pool.memset(XI[:, :, 0:PAD], 0.0).then_inc(padded, 1)
                if masks:
                    for x in range(15):
                        K.split_lo(pool, min(t0 + 1 + x, t0 + n))
                        masks.part(pool, x)
                K.split_lo(pool, end_lo)

            @block.scalar
            def _(act):
                if small:
                    small.act_split(act)
                for j in range(n + 1):
                    if j < n:
                        t = t0 + j
                        K.split_hi(act, min(t + 2, end_lo))
                        act.wait_ge(K.tile_done, t + 1)
                        if j >= 2:
                            act.wait_ge(conv, j - 1)
                        b = BROW[CONV_OF[name]] + j
                        act.activation(XI[:, j % 2, PAD:].rearrange("p (a b) -> p a b", a=3), K.psum(t), ACT.Identity,
                                       bias=K.bias[:, b:b + 1]).then_inc(K.evac_act, 1)
                    if small and j == 0:
                        small.act_logits(act)
                    if small and j == 2:
                        small.act_beta(act)
                    if small and j == 3:
                        small.act_turned(act)
                    if silu and j >= 1:
                        act.wait_ge(conv, j)
                        if j >= 3:
                            act.wait_ge(fin, j - 2)
                        act.activation(TH[:, (j - 1) % 2], OUT(j - 1), ACT.Tanh).then_inc(th, 1)
                    if 2 <= j < squares + 2:
                        act.wait_ge(fin, j - 1)
                        if j >= 4:
                            act.wait_ge(sums, j - 3)
                        act.activation(SQ[:, j % 2], OUT(j - 2)[:, 0:SEQ], ACT.Square).then_inc(sq, 1)
                act.wait_ge(last_tr, 1)
                act.activation(XR[:].rearrange("p (a b) -> p a b", b=512),
                               K.ps[0:PAD + NB, 0:n // 4, :], ACT.Identity).then_inc(last_ev, 1)

            @block.vector
            def _(dve):
                v = K.V(dve)
                if small:
                    small.dve_split(dve)
                dve.wait_ge(padded, 1)
                for j in range(n + 1):
                    if small and j == 1:
                        small.dve_values(dve)
                    if j < n:
                        dve.wait_ge(*K.emptied(t0 + j))
                        x, y = XI[:, j % 2], OUT(j)[:, 0:SEQ]
                        xs, ys = XI[:, j % 2, PAD + SEQ:], OUT(j)[:, SEQ:TOK]
                        st = K.convs[:, state0 + j, 0:24].rearrange("p (b j) -> p j b", j=PAD)
                        if silu:
                            v.step(dve.tensor_scalar(y, x[:, PAD:PAD + SEQ], tap(3, j), None, ALU.mult))
                            v.step(dve.tensor_scalar(ys, xs, tap(3, j), None, ALU.mult))
                        else:
                            cb = K.par[:, PROW["lru_conv_b"] + j:PROW["lru_conv_b"] + j + 1]
                            v.step(dve.tensor_scalar(y, x[:, PAD:PAD + SEQ], tap(3, j), cb, ALU.mult, ALU.add))
                            v.step(dve.tensor_scalar(ys, xs, tap(3, j), cb, ALU.mult, ALU.add))
                        v.step(dve.tensor_copy(XL[:, j], x[:, SEQ:SEQ + PAD + NB]))
                        for k in range(PAD):
                            v.wait()
                            v.step(dve.scalar_tensor_tensor(y, x[:, k:k + SEQ], tap(k, j), y, ALU.mult, ALU.add))
                            ins = dve.scalar_tensor_tensor(ys, st[:, k], tap(k, j), ys, ALU.mult, ALU.add)
                            if k == PAD - 1:
                                ins.then_inc(conv, 1)
                            else:
                                v.step(ins)
                    if silu and j >= 1:
                        dve.wait_ge(th, j)
                        dve.scalar_tensor_tensor(OUT(j - 1), TH[:, (j - 1) % 2], 1.0, OUT(j - 1), ALU.add,
                                                 ALU.mult).then_inc(fin, 1)
                if not silu:
                    dve.wait_ge(conv, n)

            @block.tensor
            def _(pe):
                for j in range(n):
                    if small and j == 1:
                        small.pe_logits(pe)
                        pe.wait_ge(small.N["z"], 1)
                    K.project(pe, t0 + j, K.hH, K.hL)
                    if small and j == 3:
                        small.pe_turn(pe)
                        pe.wait_ge(small.N["out"], 1)
                    if 3 <= j < squares + 3:
                        pe.wait_ge(sq, j - 2)
                        for t in range(TT8):
                            x = (j - 3) * TT8 + t
                            last = pe.matmul(K.ps[:, 6, x:x + 1], SQ[:, (j - 1) % 2, t * P:(t + 1) * P], K.ones[:],
                                             start=True, stop=True)
                        last.then_inc(sums, 1)
                pe.wait_ge(conv, n)
                pe.wait_ge(*K.emptied(t0 + n - 1))
                for j in range(n):
                    last = pe.transpose(K.ps[0:PAD + NB, j // 4, (j % 4) * P:(j % 4 + 1) * P], XL[:, j], K.ident[:])
                last.then_inc(last_tr, 1)


CONV_OF = {"dn_conv_w": "dn_qkv", "lru_conv_w": "lru_x"}


class Side:

    def sync_first(self, sp): pass
    def sync_part(self, sp, j): pass
    def sync_last(self, sp): pass
    def sync_stores(self, sp): pass
    def pool_first(self, pool): pass
    def act_first(self, act): pass
    def act_before(self, act, j): pass
    def act_after(self, act, j): pass
    def act_last(self, act): pass
    def dve_first(self, dve): pass
    def dve_part(self, dve, j): pass
    def dve_last(self, dve): pass
    def pe_part(self, pe, j, k): pass
    def pe_last(self, pe): pass


def gate_branch(K, t0, name, G, tag, side=None):
    nc = K.nc
    with ExitStack() as c:
        sb = lambda n_, s, d=F32: c.enter_context(nc.sbuf_tensor(tag + n_, s, d))
        TH = sb("_gth", [P, TOK])
        th, silu = K.sem(tag + "_gth"), K.sem(tag + "_silu")
        with nc.Block(no_gpsimd_drain=True) as block:
            @block.sync
            def _(sp):
                K.loads(sp, t0 + 2)
                if side:
                    side.sync_first(sp)
                for j in range(2):
                    K.loads(sp, t0 + 3 + j)
                    if side:
                        side.sync_part(sp, j)
                if side:
                    side.sync_last(sp)
                K.loads(sp, t0 + 4 + 2)
                if side:
                    side.sync_stores(sp)
                    sp.wait_ge(K.stored, K.n_stored)

            @block.gpsimd
            def _(pool):
                if side:
                    side.pool_first(pool)
                K.split_lo(pool, t0 + 4 + 1)

            @block.scalar
            def _(act):
                if side:
                    side.act_first(act)
                for j in range(4):
                    t = t0 + j
                    K.split_hi(act, t + 2)
                    if side:
                        side.act_before(act, j)
                    act.wait_ge(K.tile_done, t + 1)
                    b = BROW[name] + j
                    act.activation(G[:, j].rearrange("p (a b) -> p a b", a=3), K.psum(t), ACT.Identity,
                                   scale=0.5, bias=K.hbias[:, b:b + 1]).then_inc(K.evac_act, 1)
                    if side:
                        side.act_after(act, j)
                    act.wait_ge(*K.emptied(t))
                    if j >= 1:
                        act.wait_ge(silu, j)
                    act.activation(TH[:], G[:, j], ACT.Tanh).then_inc(th, 1)
                if side:
                    side.act_last(act)

            @block.vector
            def _(dve):
                if side:
                    side.dve_first(dve)
                for j in range(4):
                    if side:
                        side.dve_part(dve, j)
                    dve.wait_ge(th, j + 1)
                    dve.scalar_tensor_tensor(G[:, j], TH[:], 1.0, G[:, j], ALU.add, ALU.mult).then_inc(silu, 1)
                if side:
                    side.dve_last(dve)
                dve.wait_ge(silu, 4)

            @block.tensor
            def _(pe):
                for j in range(4):
                    K.project(pe, t0 + j, K.hH, K.hL,
                              meanwhile=side and (lambda k, j=j: side.pe_part(pe, j, k)))
                if side:
                    side.pe_last(pe)


def merge_branch(K, t0, n, G):
    nc = K.nc
    with ExitStack() as c:
        sb = lambda n_, s, d=F32: c.enter_context(nc.sbuf_tensor(f"m{n}" + n_, s, d))
        brH, brL = sb("_brH", [P, H, TOK], F32R), sb("_brL", [P, H, TOK], F32R)
        TH = sb("_th", [P, 2, TOK])
        summed = K.sem(f"m{n}_summed")
        prod, hi, lo = K.sem(f"m{n}_prod"), K.sem(f"m{n}_br_hi"), K.sem(f"m{n}_br_lo")
        with nc.Block(no_gpsimd_drain=True) as block:
            @block.sync
            def _(sp):
                K.loads(sp, t0 + 16 + 2)

            @block.gpsimd
            def _(pool):
                K.split_lo(pool, t0 + (16 if n == 3 else 17))

            @block.scalar
            def _(act):
                K.split_hi(act, t0 + 2)
                for j in range(H):
                    act.wait_ge(prod, j + 1)
                    act.activation(brH[:, j], K.OT[:, j], ACT.Identity).then_inc(hi, 1)
                for d in range(KD):
                    t = t0 + 2 * d
                    K.split_hi(act, t + 2)
                    act.wait_ge(K.tile_done, t + 1)
                    if d >= 2:
                        act.wait_ge(*K.emptied(t - 3))
                        if n:
                            act.wait_ge(summed, d - 1)
                    b = BROW["gate"] + KD * n + d
                    act.activation(TH[:, d % 2].rearrange("p (a b) -> p a b", a=3), K.psum(t), ACT.Tanh,
                                   scale=0.5, bias=K.hbias[:, b:b + 1]).then_inc(K.evac_act, 1)
                    K.split_hi(act, min(t + 3, t0 + 16 if n == 3 else t + 3))

            @block.vector
            def _(dve):
                for j in range(H + 1):
                    if j < H:
                        dve.tensor_tensor(K.OT[:, j], G[:, j], K.OT[:, j], ALU.mult).then_inc(prod, 1)
                    if j:
                        dve.wait_ge(prod, j)
                        dve.wait_ge(hi, j)
                        dve.tensor_tensor(brL[:, j - 1], K.OT[:, j - 1], brH[:, j - 1].bitcast(F32), ALU.subtract
                                          ).then_inc(lo, 1)
                for d in range(KD):
                    t = t0 + 2 * d
                    dve.wait_ge(*K.emptied(t))
                    dve.wait_ge(K.tile_done, t + 2)
                    o = K.merged[:, d] if n == 0 else TH[:, d % 2]
                    dve.scalar_tensor_tensor(o.rearrange("p (a b) -> p a b", a=3),
                                             TH[:, d % 2].rearrange("p (a b) -> p a b", a=3), 1.0, K.psum(t + 1),
                                             ALU.add, ALU.mult).then_inc(K.evac_dve, 1)
                    if n:
                        dve.wait_ge(*K.emptied(t + 1))
                        dve.tensor_tensor(K.merged[:, d], K.merged[:, d], o, ALU.add).then_inc(summed, 1)
                if n:
                    dve.wait_ge(summed, KD)

            @block.tensor
            def _(pe):
                for d in range(KD):
                    K.project(pe, t0 + 2 * d, K.hH, K.hL)
                    if d == 0:
                        pe.wait_ge(lo, H)
                    K.project(pe, t0 + 2 * d + 1, brH, brL)


def output(K, t0):
    nc, i = K.nc, K.i
    NE, HALF = D // P, D // 2
    NX = len(K.y_out)
    units = [(e, t) for e in range(2) for t in range(TT8 + 1)]
    rows_of = lambda t: P if t < TT8 else NB
    with ExitStack() as c:
        sb = lambda n_, s, d=F32: c.enter_context(nc.sbuf_tensor("o" + n_, s, d))
        WH, WL = sb("_wH", [P, KD, D], F32R), sb("_wL", [P, KD, D], F32R)
        X = sb("_x", [P, NX, HALF])
        x_in = [K.sem(f"ox_in{q}") for q in range(NX)]
        hi, lo, done, y = K.sem("m_hi"), K.sem("m_lo"), K.sem("o_done"), K.sem("y_ready")
        with nc.Block(no_gpsimd_drain=True) as block:
            @block.sync
            def _(sp):
                def load(u):
                    e, t = units[u]
                    if u >= NX:
                        sp.wait_ge(K.y_out[u % NX], 16 * (u // NX))
                    src = i["x_prompt"][0, t * P:(t + 1) * P] if t < TT8 else i["x_sample"][:, 0]
                    sp.dma_start(X[0:rows_of(t), u % NX], src[:, e * HALF:(e + 1) * HALF]
                                 ).then_inc(x_in[u % NX], 16)

                for u in range(NX - 1):
                    load(u)
                K.loads(sp, len(K.tiles))
                for u, (e, t) in enumerate(units):
                    sp.wait_ge(y, u + 1)
                    dst = K.o["y"][0, t * P:(t + 1) * P] if t < TT8 else K.o["y_s"][:, 0]
                    sp.dma_start(dst[:, e * HALF:(e + 1) * HALF], X[0:rows_of(t), u % NX]
                                 ).then_inc(K.y_out[u % NX], 16)
                    if u + NX - 1 < len(units):
                        load(u + NX - 1)
                for q in range(NX):
                    sp.wait_ge(K.y_out[q], 16 * len(range(q, len(units), NX)))
                sp.wait_ge(K.stored, K.n_stored)

            @block.gpsimd
            def _(pool):
                for e in range(NE):
                    t = t0 + e
                    pool.wait_ge(K.w_hi, t + 1)
                    pool.tensor_tensor(WL[:, :, e * P:(e + 1) * P], K.raw[:, t % 2],
                                       WH[:, :, e * P:(e + 1) * P].bitcast(F32), ALU.subtract).then_inc(K.w_lo, 1)

            @block.scalar
            def _(act):
                def weights(e):
                    t = t0 + e
                    act.wait_ge(K.w_loaded[t % 2], 16 * (t // 2 + 1))
                    act.activation(WH[:, :, e * P:(e + 1) * P], K.raw[:, t % 2], ACT.Identity).then_inc(K.w_hi, 1)

                def activations(k):
                    act.activation(K.hH[:, k], K.merged[:, k], ACT.Identity, scale=0.5).then_inc(hi, 1)

                weights(0)
                weights(1)
                activations(0)
                for e in (2, 3):
                    activations(e - 1)
                    weights(e)
                for k in range(3, KD):
                    activations(k)
                for e in range(4, NE):
                    weights(e)

            @block.vector
            def _(dve):
                for k in range(KD):
                    dve.wait_ge(hi, k + 1)
                    dve.scalar_tensor_tensor(K.hL[:, k], K.merged[:, k], 0.5, K.hH[:, k].bitcast(F32), ALU.mult,
                                             ALU.subtract).then_inc(lo, 1)
                for u, (_, t) in enumerate(units):
                    n = rows_of(t)
                    dve.wait_ge(x_in[u % NX], 16 * (u // NX + 1))
                    dve.wait_ge(done, u + 1)
                    dve.tensor_tensor(X[0:n, u % NX], K.ps[0:n, u % 8], X[0:n, u % NX], ALU.add).then_inc(y, 1)

            @block.tensor
            def _(pe):
                for u, (e, t) in enumerate(units):
                    n = rows_of(t)
                    if t == 0:
                        pe.wait_ge(K.w_hi, t0 + NE // 2 * (e + 1))
                    if u >= 8:
                        pe.wait_ge(y, u - 7)
                    passes = [(k, x, WH) for k in range(KD) for x in (K.hH, K.hL)] + [(k, K.hH, WL) for k in range(KD)]
                    for m, (k, x, w) in enumerate(passes):
                        if u == 0 and m < 2 * KD and m % 2 == 0:
                            pe.wait_ge(lo, k + 1)
                        if t == 0 and m == 2 * KD:
                            pe.wait_ge(K.w_lo, t0 + NE // 2 * (e + 1))
                        last = pe.matmul(K.ps[0:n, u % 8], x[:, k, t * P:t * P + n],
                                         w[:, k, e * HALF:(e + 1) * HALF], start=(m == 0),
                                         stop=(m == len(passes) - 1))
                    last.then_inc(done, 1)


class DeltaMasks:

    def __init__(self, K, sb):
        self.LO, self.UP = sb("dn_lo", [P, 7, P], I8), sb("dn_up", [P, 7, P], I8)
        self.NEGM, self.STR, self.SEL = (sb(n, [P, P]) for n in ("dn_negm", "dn_strict", "dn_last"))
        self.made, self.n = K.sem("dn_masks"), 0

    def step(self, pool, ins):
        ins.then_inc(self.made, 1)
        self.n += 1
        pool.wait_ge(self.made, self.n)

    def part(self, pool, x):
        if x == 14:
            for M, fill, op, other, pattern, mul in (
                    (self.NEGM, 0.0, ALU.is_ge, NEG, [[1, P]], -1),
                    (self.STR, -1.0, ALU.is_gt, 0.0, [[1, P]], -1),
                    (self.SEL, 1.0, ALU.is_ge, 0.0, [[0, P]], 1)):
                self.step(pool, pool.memset(M[:], fill))
                self.step(pool, pool.affine_select(out=M[:], in_=M[:], compare_op=op, fill=other,
                                                   base=1 - P if M is self.SEL else 0, pattern=pattern,
                                                   channel_multiplier=mul))
            return
        l, lower = x // 2, x % 2 == 0
        s = 1 << l
        M = self.LO if lower else self.UP
        self.step(pool, pool.memset(M[:, l], 0))
        v = M[:, l].rearrange("p (b r) -> p b r", r=2 * s)
        v = v[:, :, 0:s] if lower else v[:, :, s:2 * s]
        self.step(pool, pool.memset(v, 1))
        for base, mul in (((-s, 1), (2 * s - 1, -1)) if lower else ((0, 1), (s - 1, -1))):
            self.step(pool, pool.affine_select(out=v, in_=v, compare_op=ALU.is_ge, fill=0, base=base,
                                               pattern=[[-2 * s * mul, P // (2 * s)], [0, s]],
                                               channel_multiplier=mul))


def unit_queries_and_keys(K):
    nc = K.nc
    n = 2 * H * TT8
    with ExitStack() as c:
        sb = lambda n_, s, d=F32: c.enter_context(nc.sbuf_tensor("u" + n_, s, d))
        SS, RN, TM = sb("_ss", [P, n]), sb("_rn", [P, n]), sb("_tm", [P, n])
        ROWS = sb("_rows", [n, P])
        R = sb("_d_rows", [NB, 2, H, P])
        DS, DR, DM = sb("_d_ss", [NB, 2, H]), sb("_d_rn", [NB, 2, H]), sb("_d_tm", [NB, 2, H])
        d_tr, d_sq, d_rows = K.sem("unit_d_tr"), K.sem("unit_d_sq"), K.sem("unit_d_rows")
        flat = lambda x: x[:].rearrange("b r h -> b (r h)")
        BC = sb("_bc", [P, 2 * H, SEQ])
        rn, tr, moved, out = K.sem("unit_rn"), K.sem("unit_tr"), K.sem("unit_moved"), K.sem("unit_out")
        back = [K.sem(f"unit_in{x}") for x in range(2 * H)]
        dst = [K.OT[:, h, 0:SEQ] for h in range(H)] + [K.merged[:, h, 0:SEQ] for h in range(H)]
        with nc.Block(no_gpsimd_drain=True) as block:
            @block.vector
            def _(dve):
                v = K.V(dve)
                v.do(dve.tensor_scalar(SS[:], K.ps[:, 6, 0:n], EPS, None, ALU.add))
                rsqrt(v, SS[:], RN[:], TM[:])
                dve.tensor_scalar(RN[:, 0:n // 2], RN[:, 0:n // 2], SCALE, None, ALU.mult).then_inc(rn, 1)
                dve.wait_ge(d_sq, 1)
                v.do(dve.tensor_reduce(DS[:], R[:], AX.X, ALU.add))
                v.do(dve.tensor_scalar(DS[:], DS[:], EPS, None, ALU.add))
                rsqrt(v, flat(DS), flat(DR), flat(DM))
                v.do(dve.tensor_scalar(DR[:, 0], DR[:, 0], SCALE, None, ALU.mult))
                for r in range(2):
                    dve.tensor_tensor(R[:, r], heads(K.ps[0:NB, r]), DR[:, r].unsqueeze(2).broadcast_to([NB, H, P]),
                                      ALU.mult).then_inc(d_rows, 1)
                for x in (0, 4, 1, 5, 2):
                    dve.wait_ge(back[x], 16)
                    v.step(dve.tensor_tensor(dst[x], dst[x], BC[:, x], ALU.mult))

            @block.gpsimd
            def _(pool):
                g = K.G(pool)
                for x in (6, 3, 7):
                    pool.wait_ge(back[x], 16)
                    g.step(pool.tensor_tensor(dst[x], dst[x], BC[:, x], ALU.mult))
                g.wait()

            @block.tensor
            def _(pe):
                for r, x in enumerate((K.OT, K.merged)):
                    for h in range(H):
                        last = pe.transpose(K.ps[0:NB, r, h * P:(h + 1) * P], x[:, h, SEQ:TOK], K.ident[:])
                last.then_inc(d_tr, 1)
                pe.wait_ge(rn, 1)
                pe.transpose(K.ps[0:n, 7, 0:P], RN[:], K.ident[:]).then_inc(tr, 1)

            @block.scalar
            def _(act):
                act.wait_ge(d_tr, 1)
                act.activation(R[:].rearrange("b r h d -> b r (h d)"), K.ps[0:NB, 0:2], ACT.Square).then_inc(d_sq, 1)
                act.wait_ge(tr, 1)
                act.activation(ROWS[:], K.ps[0:n, 7, 0:P], ACT.Identity).then_inc(moved, 1)

            @block.sync
            def _(sp):
                sp.wait_ge(moved, 1)
                sp.dma_start(K.d_unit.rearrange("x (t p) -> (x t) p", p=P), ROWS[:]).then_inc(out, 16)
                sp.wait_ge(out, 16)
                for x in (0, 6, 4, 1, 3, 5, 2, 7):
                    sp.dma_start(BC[:, x], K.d_unit[x:x + 1].broadcast_to([P, SEQ])).then_inc(back[x], 16)
                sp.wait_ge(d_rows, 2)
                sp.dma_start(K.d_qk.rearrange("r b h d -> b r h d"), R[:]).then_inc(out, 16)
                sp.wait_ge(out, 32)


def delta_rule(K, masks):
    nc = K.nc
    NPAIR = NCH // 2
    LV = 6
    LO, UP, NEGM, STR = masks.LO, masks.UP, masks.NEGM, masks.STR
    with ExitStack() as c:
        sb = lambda n_, s, d=F32: c.enter_context(nc.sbuf_tensor("d" + n_, s, d))
        slots = lambda n_, n: sb(n_, [P, n, H, P])
        XY = K.borrowed("d_xy", 0, [P, 4, H, P])
        X, Y = [XY[:, q] for q in range(2)], [XY[:, 2 + q] for q in range(2)]
        NU, QKT = K.borrowed("d_nu", 1, [P, 4, H, P]), K.borrowed("d_qkT", 2, [P, 4, H, P])
        QG = slots("_qgT", 4)
        VB, KBG, KD_ = slots("_vb", 2), slots("_kbg", 2), slots("_kdec", 2)
        M1, NWT, DT, W = slots("_m1", 2), slots("_nwT", 2), slots("_dT", 2), slots("_w", 2)
        O, SQ = slots("_o", 2), slots("_osq", 2)
        GC = sb("_gc", [P, 2, H, P])
        KN, U, ST, STG = (sb(n_, [P, H, P]) for n_ in ("_kn", "_u", "_state", "_st_decayed"))
        SC, GE, GL = sb("_sc", [P, 3, NCH, H]), sb("_ge", [P, NCH, H]), sb("_g_end", [P, NCH, H])
        OS, OR, OM = sb("_os", [P, 2, H]), sb("_or", [P, 2, H]), sb("_om", [P, 2, H])
        fl = lambda x: x[:].rearrange("p q h -> p (q h)")
        kT = lambda ch, h: K.merged[:, h, ch * CH:(ch + 1) * CH]
        vT = lambda ch, h: K.merged[:, H + h, ch * CH:(ch + 1) * CH]
        qT = lambda ch: K.OT[:, :, ch * CH:(ch + 1) * CH]
        S = {n_: K.sem("dn_" + n_) for n_ in
             ("rows_in", "gl", "gld", "sc", "diff", "decay", "w", "unit", "qg", "gram", "nu", "tok", "kn", "vb",
              "kb", "first0", "first1", "firsted", "m1", "m1e", "dxy", "upd", "wT", "wTe", "u", "ue", "o", "ocp", "on",
              "oT", "oTe", "ds", "state", "zero", "fin", "fine", "stg")}
        B = [K.ps[:, b].rearrange("p (h d) -> p h d", h=H) for b in range(8)]
        tokv = lambda ch, r: K.TK[:, ch, r]
        bc = lambda ap: ap.unsqueeze(2).broadcast_to([P, H, P])
        mb = lambda ap: ap.unsqueeze(1).broadcast_to([P, H, P])

        with nc.Block(no_gpsimd_drain=True) as block:
            @block.sync
            def _(sp):
                for ch in range(NCH):
                    if ch >= 1:
                        sp.wait_ge(S["qg"], ch)
                    for q, r in ((0, 0), (1, 2)):
                        sp.dma_start(GC[:, q], K.d_rows[r, :, ch * CH:(ch + 1) * CH].unsqueeze(0).broadcast_to(
                            [P, H, CH])).then_inc(S["rows_in"], 16)
                sp.wait_ge(S["u"], NCH)
                K.loads(sp, K.at_load + 2)
                sp.wait_ge(S["fine"], 1)
                K.store(sp, K.o["dn_state"][0, 0].rearrange("h v k -> v h k"), KN[:])
                sp.wait_ge(K.stored, K.n_stored)

            @block.gpsimd
            def _(pool):
                g = K.G(pool)
                pool.memset(ST[:], 0.0).then_inc(S["zero"], 1)

                def identity(p):
                    if p:
                        pool.wait_ge(S["u"], 2 * p - 1)
                    g.step(pool.tensor_copy(X[0], mb(K.ident[:])))
                    pool.tensor_copy(Y[0], mb(K.ident[:])).then_inc(S["first0"], 1)

                def prepare_gram(ch):
                    q = ch % 2
                    pool.wait_ge(S["rows_in"], 32 * (ch + 1))
                    if ch >= 2:
                        pool.wait_ge(S["nu"], ch - 1)
                    g.do(pool.tensor_tensor(DT[:, q], GC[:, 0], bc(tokv(ch, 0)), ALU.subtract))
                    pool.tensor_tensor(DT[:, q], DT[:, q], mb(NEGM[:]), ALU.add).then_inc(S["diff"], 1)
                    g.do(pool.tensor_tensor(W[:, q], GC[:, 1], mb(STR[:]), ALU.mult))
                    pool.wait_ge(S["decay"], ch + 1)
                    pool.tensor_tensor(W[:, q], W[:, q], DT[:, q], ALU.mult).then_inc(S["w"], 1)
                    pool.wait_ge(S["unit"], ch + 1)
                    if ch >= 4:
                        pool.wait_ge(S["o"], ch - 3)
                    pool.tensor_tensor(QG[:, ch % 4], qT(ch), GC[:, 0], ALU.mult).then_inc(S["qg"], 1)

                def prepare_rows(ch):
                    pool.wait_ge(S["kn"], ch + 1)
                    pool.wait_ge(S["sc"], 2)
                    if ch >= 2:
                        pool.wait_ge(S["ds"], ch - 1)
                    q = ch % 2
                    g.step(pool.tensor_tensor(KBG[:, q], KN[:], bc(SC[:, 0, ch]), ALU.mult))
                    pool.tensor_tensor(KD_[:, q], KN[:], bc(SC[:, 1, ch]), ALU.mult).then_inc(S["kb"], 1)

                prepare_gram(0)
                prepare_gram(1)
                for p in range(NPAIR):
                    identity(p)
                    prepare_rows(2 * p)
                    prepare_rows(2 * p + 1)
                    if p + 1 < NPAIR:
                        prepare_gram(2 * p + 2)
                        prepare_gram(2 * p + 3)

            @block.scalar
            def _(act):
                a = K.A(act)

                def prepare_gram(ch):
                    q = ch % 2
                    act.wait_ge(S["diff"], ch + 1)
                    act.activation(DT[:, q], DT[:, q], ACT.Exp).then_inc(S["decay"], 1)
                    act.activation(GC[:, 0], GC[:, 0], ACT.Exp).then_inc(S["unit"], 1)

                def prepare_rows(ch):
                    act.wait_ge(S["tok"], ch + 1)
                    if ch >= 1:
                        act.wait_ge(S["kb"], ch)
                    act.activation(KN[:], B[6], ACT.Identity).then_inc(S["kn"], 1)

                def output(ch):
                    act.wait_ge(S["oT"], ch + 1)
                    act.activation(qT(ch), B[6 + ch % 2], ACT.Identity,
                                   scale=K.par[:, PROW["dn_onorm_w"]:PROW["dn_onorm_w"] + 1]).then_inc(S["oTe"], 1)

                def identity():
                    a.step(act.activation(X[1], mb(K.ident[:]), ACT.Identity))
                    act.activation(Y[1], mb(K.ident[:]), ACT.Identity).then_inc(S["first1"], 1)

                identity()
                act.wait_ge(S["gl"], 1)
                act.activation(GL[:].rearrange("p c h -> p (c h)"), K.ps[:, 7, 0:NCH * H], ACT.Identity
                               ).then_inc(S["gld"], 1)
                act.wait_ge(S["gld"], 1)
                act.activation(GE[:], GL[:], ACT.Exp).then_inc(S["gld"], 1)
                a.step(act.activation(SC[:, 2], K.TK[:, :, 0], ACT.Exp))
                act.wait_ge(S["sc"], 1)
                act.activation(SC[:, 1], SC[:, 1], ACT.Exp).then_inc(S["gld"], 1)
                prepare_gram(0)
                prepare_gram(1)
                for p in range(NPAIR):
                    c0 = 2 * p
                    for l in range(1, LV + 1):
                        for q in range(2):
                            act.wait_ge(S["m1"], (p * LV + l - 1) * 2 + q + 1)
                            act.activation(M1[:, q], B[q], ACT.Identity).then_inc(S["m1e"], 1)
                        if l == 1:
                            prepare_rows(c0)
                        if l == 2:
                            prepare_rows(c0 + 1)
                        if l == 3 and p + 1 < NPAIR:
                            prepare_gram(c0 + 2)
                        if l == 4 and p:
                            output(c0 - 2)
                            output(c0 - 1)
                        if l == 5 and p + 1 < NPAIR:
                            prepare_gram(c0 + 3)
                    for q in range(2):
                        act.wait_ge(S["wT"], c0 + q + 1)
                        act.activation(NWT[:, q], B[q], ACT.Identity, scale=-1.0).then_inc(S["wTe"], 1)
                    for q in range(2):
                        ch = c0 + q
                        act.wait_ge(S["u"], ch + 1)
                        act.activation(U[:], B[2 + q], ACT.Identity).then_inc(S["ue"], 1)
                        if q and p + 1 < NPAIR:
                            identity()
                        act.wait_ge(S["o"], ch + 1)
                        if ch >= 2:
                            act.wait_ge(S["oT"], ch - 1)
                        act.activation(SQ[:, q], B[6 + q], ACT.Square)
                        act.activation(O[:, q], B[6 + q], ACT.Identity).then_inc(S["ocp"], 1)
                output(NCH - 2)
                output(NCH - 1)
                act.wait_ge(S["fin"], 1)
                act.activation(KN[:], B[5], ACT.Identity).then_inc(S["fine"], 1)

            @block.vector
            def _(dve):
                v = K.V(dve)

                def prepare_gram(ch):
                    q = ch % 2
                    dve.wait_ge(S["w"], ch + 1)
                    dve.wait_ge(S["gram"], ch + 1)
                    v.step(dve.tensor_tensor(NU[:, ch % 4], B[6], W[:, q], ALU.mult))
                    dve.tensor_tensor(QKT[:, ch % 4], B[7], DT[:, q], ALU.mult).then_inc(S["nu"], 1)

                def prepare_rows(ch):
                    dve.wait_ge(S["tok"], ch + 1)
                    dve.tensor_tensor(VB[:, ch % 2], B[7], bc(tokv(ch, 2)), ALU.mult).then_inc(S["vb"], 1)

                def square_sums(ch):
                    dve.wait_ge(S["ocp"], ch + 1)
                    v.step(dve.tensor_reduce(OS[:, ch % 2], SQ[:, ch % 2], AX.X, ALU.add))

                def root():
                    v.wait()
                    v.do(dve.tensor_scalar(fl(OS), fl(OS), 1.0 / P, EPS, ALU.mult, ALU.add))
                    rsqrt(v, fl(OS), fl(OR), fl(OM))

                def norm(ch):
                    dve.tensor_tensor(O[:, ch % 2], O[:, ch % 2], bc(OR[:, ch % 2]), ALU.mult).then_inc(S["on"], 1)

                dve.wait_ge(S["gld"], 2)
                dve.tensor_tensor(SC[:, 1], GL[:], K.TK[:, :, 0], ALU.subtract).then_inc(S["sc"], 1)
                dve.wait_ge(S["gld"], 3)
                dve.tensor_tensor(SC[:, 0], SC[:, 2], K.TK[:, :, 2], ALU.mult).then_inc(S["sc"], 1)
                dve.wait_ge(S["zero"], 1)
                prepare_gram(0)
                prepare_gram(1)
                for p in range(NPAIR):
                    c0 = 2 * p
                    for q in range(2):
                        ch = c0 + q
                        dve.wait_ge(S["firsted"], ch + 1)
                        dve.wait_ge(S[f"first{q}"], p + 1)
                        dve.wait_ge(S["nu"], ch + 1)
                        v.step(dve.copy_predicated(X[q], mb(LO[:, 0]), B[q]))
                        dve.copy_predicated(Y[q], mb(UP[:, 0]), NU[:, ch % 4]).then_inc(S["upd"], 1)
                    for l in range(1, LV + 1):
                        for q in range(2):
                            dve.wait_ge(S["dxy"], (p * LV + l - 1) * 2 + q + 1)
                            if l < LV:
                                v.step(dve.copy_predicated(X[q], mb(LO[:, l]), B[2 + q]))
                            dve.copy_predicated(Y[q], mb(UP[:, l]), B[4 + q]).then_inc(S["upd"], 1)
                        if l == 1:
                            prepare_rows(c0)
                            if p:
                                square_sums(c0 - 2)
                                square_sums(c0 - 1)
                        if l == 2:
                            prepare_rows(c0 + 1)
                            if p:
                                root()
                        if l == 3 and p:
                            norm(c0 - 2)
                            norm(c0 - 1)
                        if l in (5, 6) and p + 1 < NPAIR:
                            prepare_gram(c0 + l - 3)
                    for q in range(2):
                        ch = c0 + q
                        if ch >= 1:
                            dve.wait_ge(S["state"], ch)
                        dve.tensor_tensor(STG[:], ST[:], bc(GE[:, ch]), ALU.mult).then_inc(S["stg"], 1)
                        dve.wait_ge(S["stg"], ch + 1)
                        dve.wait_ge(S["ds"], ch + 1)
                        dve.tensor_tensor(ST[:], STG[:], B[4 + q], ALU.add).then_inc(S["state"], 1)
                square_sums(NCH - 2)
                square_sums(NCH - 1)
                root()
                norm(NCH - 2)
                norm(NCH - 1)

            @block.tensor
            def _(pe):
                def gram(ch):
                    if ch % 2 or ch == 0:
                        if ch:
                            pe.wait_ge(S["nu"], ch)
                    if ch % 2 == 0 and ch:
                        pe.wait_ge(S["kn"], ch)
                        pe.wait_ge(S["vb"], ch)
                        if ch >= 4:
                            pe.wait_ge(S["oTe"], ch - 2)
                    for r in range(2):
                        for h in range(H):
                            q = kT(ch, h) if r == 0 else qT(ch)[:, h]
                            last = pe.matmul(B[6 + r][:, h], kT(ch, h), q, start=True, stop=True)
                    last.then_inc(S["gram"], 1)

                def rows(ch):
                    if ch % 2 == 0:
                        pe.wait_ge(S["nu"], ch + 2)
                        if ch:
                            pe.wait_ge(S["ocp"], ch)
                    else:
                        pe.wait_ge(S["kn"], ch)
                        pe.wait_ge(S["vb"], ch)
                    for h in range(H):
                        pe.transpose(B[6][:, h], kT(ch, h), K.ident[:])
                    for h in range(H):
                        last = pe.transpose(B[7][:, h], vT(ch, h), K.ident[:])
                    last.then_inc(S["tok"], 1)

                def output(ch):
                    pe.wait_ge(S["on"], ch + 1)
                    for h in range(H):
                        last = pe.transpose(B[6 + ch % 2][:, h], O[:, ch % 2, h], K.ident[:])
                    last.then_inc(S["oT"], 1)

                pe.matmul(K.ps[:, 7, 0:NCH * H].rearrange("p (c h) -> p c h", h=H), masks.SEL[:], K.TK[:, :, 0],
                          start=True, stop=True).then_inc(S["gl"], 1)
                pe.wait_ge(S["gld"], 1)
                gram(0)
                gram(1)
                for p in range(NPAIR):
                    c0 = 2 * p
                    for q in range(2):
                        ch = c0 + q
                        pe.wait_ge(S["nu"], ch + 1)
                        if p:
                            pe.wait_ge(S["wTe"], c0)
                        for h in range(H):
                            last = pe.transpose(B[q][:, h], NU[:, ch % 4, h], K.ident[:])
                        last.then_inc(S["firsted"], 1)
                    for l in range(1, LV + 1):
                        for q in range(2):
                            pe.wait_ge(S["upd"], p * 14 + (l - 1) * 2 + q + 1)
                            for h in range(H):
                                last = pe.matmul(B[q][:, h], NU[:, (c0 + q) % 4, h], X[q][:, h], start=True,
                                                 stop=True)
                            last.then_inc(S["m1"], 1)
                        if l == 1:
                            rows(c0)
                        if l == 2:
                            rows(c0 + 1)
                        if l == 4 and p:
                            pe.wait_ge(S["kn"], c0 + 2)
                            pe.wait_ge(S["vb"], c0 + 2)
                            output(c0 - 2)
                            output(c0 - 1)
                        if l in (5, 6) and p + 1 < NPAIR:
                            gram(c0 + l - 3)
                        for q in range(2):
                            pe.wait_ge(S["m1e"], (p * LV + l - 1) * 2 + q + 1)
                            for h in range(H):
                                if l < LV:
                                    pe.matmul(B[2 + q][:, h], Y[q][:, h], M1[:, q, h], start=True, stop=True)
                                last = pe.matmul(B[4 + q][:, h], M1[:, q, h], Y[q][:, h], start=True, stop=True)
                            last.then_inc(S["dxy"], 1)
                    for q in range(2):
                        pe.wait_ge(S["upd"], p * 14 + 13 + q)
                        pe.wait_ge(S["kb"], c0 + q + 1)
                        for h in range(H):
                            last = pe.matmul(B[q][:, h], KBG[:, q, h], Y[q][:, h], start=True, stop=True)
                        last.then_inc(S["wT"], 1)
                    for q in range(2):
                        ch = c0 + q
                        if q == 0 and p + 1 < NPAIR:
                            pe.wait_ge(S["nu"], c0 + 4)
                        if q == 0 and p + 1 == NPAIR:
                            pe.wait_ge(S["oTe"], c0)
                        pe.wait_ge(S["wTe"], ch + 1)
                        if ch:
                            pe.wait_ge(S["state"], ch)
                        for h in range(H):
                            pe.matmul(B[2 + q][:, h], Y[q][:, h], VB[:, q, h], start=True, stop=False)
                            last = pe.matmul(B[2 + q][:, h], NWT[:, q, h], ST[:, h], start=False, stop=True)
                        last.then_inc(S["u"], 1)
                        for h in range(H):
                            pe.matmul(B[6 + q][:, h], QG[:, ch % 4, h], ST[:, h], start=(h == 0), stop=False)
                        pe.wait_ge(S["ue"], ch + 1)
                        for h in range(H):
                            last = pe.matmul(B[4 + q][:, h], KD_[:, q, h], U[:, h], start=True, stop=True)
                        last.then_inc(S["ds"], 1)
                        for h in range(H):
                            last = pe.matmul(B[6 + q][:, h], QKT[:, ch % 4, h], U[:, h], start=False,
                                             stop=(h == H - 1))
                        last.then_inc(S["o"], 1)
                for ch in (NCH - 2, NCH - 1):
                    output(ch)
                pe.wait_ge(S["state"], NCH)
                for h in range(H):
                    last = pe.transpose(B[5][:, h], ST[:, h], K.ident[:])
                last.then_inc(S["fin"], 1)


class DeltaDecode(Side):

    def __init__(self, K, c):
        nc = K.nc
        self.K = K
        sb = lambda n_, s, d=F32: c.enter_context(nc.sbuf_tensor("e" + n_, s, d))
        S4 = [P, NB, H, P]
        self.SD, self.ROW, self.T = sb("_state", S4), sb("_row", S4), sb("_prod", [P, H, P])
        self.SK, self.UU, self.O = sb("_sk", [P, NB, H]), sb("_u", [P, NB, H]), sb("_o", [P, NB, H])
        self.OR, self.OQ = sb("_or", [32, P]), sb("_oq", [32, P])
        self.OS, self.OR1, self.OM = sb("_os", [32, 1]), sb("_or1", [32, 1]), sb("_om", [32, 1])
        self.s_in = [K.sem(f"de_state_in{b}") for b in range(NB)]
        self.k_in = K.sem("de_k_in")
        self.q_in = [K.sem(f"de_q_in{x}") for x in range(2)]
        self.N = {x: K.sem("de_" + x) for x in ("k_used", "new", "o", "oT", "osq", "on", "ob")}

    def rows(self, r, b, n):
        return self.K.d_qk[r, b:b + n].rearrange("b h d -> (b h d)").unsqueeze(0).broadcast_to([P, n * H * P])

    def sync_first(self, sp):
        K = self.K
        sp.dma_start(self.ROW[:].rearrange("p b h d -> p (b h d)"), self.rows(1, 0, NB)).then_inc(self.k_in, 16)
        for b in range(NB):
            sp.dma_start(self.SD[:, b], K.i["state_dn"][0, b].rearrange("h v k -> v h k")).then_inc(self.s_in[b], 16)

    def sync_part(self, sp, x):
        n = NB // 2
        sp.wait_ge(self.N["k_used"], n * (x + 1))
        sp.dma_start(self.ROW[:, n * x:n * (x + 1)].rearrange("p b h d -> p (b h d)"), self.rows(0, n * x, n)
                     ).then_inc(self.q_in[x], 16)

    def sync_last(self, sp):
        for b in range(NB):
            sp.wait_ge(self.N["new"], b + 1)
            self.K.store(sp, self.K.o["dn_state_s"][0, b].rearrange("h v k -> v h k"), self.SD[:, b])

    def dve_part(self, dve, x):
        K, SK, UU, T, SD = self.K, self.SK, self.UU, self.T, self.SD
        v = K.V(dve)
        wide = lambda ap: ap.unsqueeze(2).broadcast_to([P, H, P])
        for b in range(NB // 2 * (x % 2), NB // 2 * (x % 2 + 1)):
            row = self.ROW[:, b]
            if x < 2:
                al, be = K.alpha[:, 0, :, b], K.alpha[:, 1, :, b]
                dve.wait_ge(self.s_in[b], 16)
                dve.wait_ge(self.k_in, 16)
                v.do(dve.tensor_tensor(T[:], SD[:, b], row, ALU.mult))
                v.do(dve.tensor_reduce(SK[:, b], T[:], AX.X, ALU.add))
                v.do(dve.tensor_tensor(SK[:, b], SK[:, b], al, ALU.mult))
                v.do(dve.tensor_tensor(UU[:, b], K.merged[:, H:2 * H, SEQ + b], SK[:, b], ALU.subtract))
                v.do(dve.tensor_tensor(UU[:, b], UU[:, b], be, ALU.mult))
                v.step(dve.tensor_tensor(SD[:, b], SD[:, b], wide(al), ALU.mult))
                dve.tensor_tensor(T[:], row, wide(UU[:, b]), ALU.mult).then_inc(self.N["k_used"], 1)
                v.wait()
                dve.wait_ge(self.N["k_used"], b + 1)
                dve.tensor_tensor(SD[:, b], SD[:, b], T[:], ALU.add).then_inc(self.N["new"], 1)
                dve.wait_ge(self.N["new"], b + 1)
            else:
                dve.wait_ge(self.q_in[x % 2], 16)
                v.do(dve.tensor_tensor(T[:], SD[:, b], row, ALU.mult))
                v.do(dve.tensor_reduce(self.O[:, b], T[:], AX.X, ALU.add))
        if x == 3:
            dve.sem_inc(self.N["o"], 1)

    def pe_last(self, pe):
        K, N = self.K, self.N
        pe.wait_ge(N["o"], 1)
        pe.transpose(K.ps[0:32, 6, 0:P], self.O[:].rearrange("p b h -> p (b h)"), K.ident[:]).then_inc(N["oT"], 1)
        pe.wait_ge(N["on"], 1)
        pe.transpose(K.ps[:, 7, 0:32], self.OR[:], K.ident[0:32, 0:32]).then_inc(N["ob"], 1)

    def act_last(self, act):
        K, N = self.K, self.N
        act.wait_ge(N["oT"], 1)
        act.activation(self.OQ[:], K.ps[0:32, 6, 0:P], ACT.Square, accum_out=self.OS[:]).then_inc(N["osq"], 1)
        act.wait_ge(N["ob"], 1)
        act.activation(K.OT[:, :, SEQ:TOK].rearrange("p h b -> p b h"),
                       K.ps[:, 7, 0:32].rearrange("p (b h) -> p b h", b=NB), ACT.Identity,
                       scale=K.par[:, PROW["dn_onorm_w"]:PROW["dn_onorm_w"] + 1]).then_inc(N["ob"], 1)
        act.wait_ge(N["ob"], 2)

    def dve_last(self, dve):
        K, N = self.K, self.N
        v = K.V(dve)
        dve.wait_ge(N["osq"], 1)
        v.do(dve.tensor_scalar(self.OS[:], self.OS[:], 1.0 / P, EPS, ALU.mult, ALU.add))
        rsqrt(v, self.OS[:], self.OR1[:], self.OM[:])
        dve.tensor_scalar(self.OR[:], K.ps[0:32, 6, 0:P], self.OR1[:, 0:1], None, ALU.mult).then_inc(N["on"], 1)


class Lru(Side):

    def __init__(self, K, c):
        nc = K.nc
        self.K = K
        sb = lambda n_, s, d=F32: c.enter_context(nc.sbuf_tensor("l" + n_, s, d))
        self.BD = sb("_blocks", [P, 2, H, P])
        self.A, self.U, self.A2 = sb("_a", [P, H, TOK]), sb("_u", [P, H, TOK]), sb("_a_squared", [P, TOK])
        self.SM = sb("_sp", [P, 6, H])
        self.HR = sb("_h_rows", [9, BW])
        self.N = {x: K.sem("lru_" + x) for x in ("zero", "w_in", "product", "gate", "nla", "a", "th", "u", "root",
                                                 "h", "hT", "hTe", "lam", "lamu")}
        self.lam = K.par[:, PROW["lru_lambda"]:PROW["lru_lambda"] + H]

    def pool_first(self, pool):
        pool.memset(self.BD[:], 0.0).then_inc(self.N["zero"], 1)

    def sync_first(self, sp):
        K = self.K
        sp.wait_ge(self.N["zero"], 1)
        for r, name in enumerate(("lru_w_r", "lru_w_i")):
            w = K.i[name][0].rearrange("(t a) e f -> a e t f", a=2)
            for a in range(2):
                sp.dma_start(self.BD[64 * a:64 * a + 64, r, :, 64 * a:64 * a + 64], w[a]).then_inc(self.N["w_in"], 16)

    def sync_stores(self, sp):
        K = self.K
        sp.wait_ge(self.N["hTe"], 1)
        K.store(sp, K.o["lru_h"][0], self.HR[0:1])
        K.store(sp, K.o["lru_h_s"][0], self.HR[1:9])

    def pe_part(self, pe, j, k):
        if k < 2:
            return
        K, N = self.K, self.N
        if (j, k) == (0, 2):
            pe.wait_ge(N["w_in"], 64)
        r, g = (k - 2) // 3, (k - 2) % 3
        x = 6 * j + k - 2
        if x >= 2:
            pe.wait_ge(N["gate"], x - 1)
        pe.matmul(K.ps[:, 6 + x % 2, 0:G3], self.BD[:, r, j], K.OT[:, j, g * G3:(g + 1) * G3], start=True,
                  stop=True).then_inc(N["product"], 1)

    def pe_last(self, pe):
        K, N = self.K, self.N
        pe.wait_ge(N["h"], H)
        for t in range(H):
            last = pe.transpose(K.ps[0:9, 6, t * P:(t + 1) * P], K.OT[:, t, SEQ - 1:TOK], K.ident[:])
        last.then_inc(N["hT"], 1)

    def act_first(self, act):
        act.wait_ge(self.N["lam"], 1)
        act.activation(self.SM[:, 1], self.SM[:, 1], ACT.Exp).then_inc(self.N["lamu"], 1)

    def act_before(self, act, j):
        K, N = self.K, self.N
        for r, (dst, name) in enumerate(((self.A, "lru_b_r"), (self.U, "lru_b_i"))):
            b = PROW[name] + j
            for g in range(3):
                x = 6 * j + 3 * r + g
                act.wait_ge(N["product"], x + 1)
                act.activation(dst[:, j, g * G3:(g + 1) * G3], K.ps[:, 6 + x % 2, 0:G3], ACT.Tanh, scale=0.5,
                               bias=K.hpar[:, b:b + 1]).then_inc(N["gate"], 1)

    def act_after(self, act, j):
        N = self.N
        act.wait_ge(N["nla"], j + 1)
        act.activation(self.U[:, j], self.A[:, j], ACT.Tanh).then_inc(N["th"], 1)
        act.activation(self.A[:, j], self.A[:, j], ACT.Exp, scale=-1.0).then_inc(N["a"], 1)

    def act_last(self, act):
        K, N = self.K, self.N
        for t in range(H):
            act.wait_ge(N["u"], t + 1)
            act.activation(self.U[:, t], self.U[:, t], ACT.Sqrt).then_inc(N["root"], 1)
        act.wait_ge(N["hT"], 1)
        act.activation(self.HR[:], K.ps[0:9, 6], ACT.Identity).then_inc(N["hTe"], 1)

    def dve_first(self, dve):
        SM, N, lam = self.SM, self.N, self.lam
        v = self.K.V(dve)
        v.do(dve.tensor_scalar(SM[:, 0], lam, -1.0, None, ALU.mult))
        dve.tensor_tensor(SM[:, 1], SM[:, 0], lam, ALU.min).then_inc(N["lam"], 1)
        dve.wait_ge(N["lamu"], 1)
        log1p_exp(v, SM[:, 0], SM[:, 1], SM[:, 2], SM[:, 3], SM[:, 4])
        v.do(dve.tensor_scalar(SM[:, 5], SM[:, 4], LRU_C / 2, None, ALU.mult))

    def dve_part(self, dve, j):
        K, N, A, U = self.K, self.N, self.A, self.U
        v = K.V(dve)
        dve.wait_ge(N["gate"], 6 * j + 6)
        v.step(dve.scalar_tensor_tensor(K.OT[:, j], U[:, j], 1.0, K.OT[:, j], ALU.add, ALU.mult))
        dve.tensor_scalar(A[:, j], A[:, j], 1.0, self.SM[:, 5, j:j + 1], ALU.add, ALU.mult).then_inc(N["nla"], 1)
        dve.wait_ge(N["a"], j + 1)
        v.do(dve.tensor_tensor(self.A2[:], A[:, j], A[:, j], ALU.mult))
        dve.scalar_tensor_tensor(U[:, j], self.A2[:], 1.0, U[:, j], ALU.add, ALU.mult).then_inc(N["u"], 1)
        dve.wait_ge(N["u"], j + 1)

    def dve_last(self, dve):
        K, N, A, U = self.K, self.N, self.A, self.U
        v = K.V(dve)
        for t in range(H):
            dve.wait_ge(N["root"], t + 1)
            v.do(dve.scalar_tensor_tensor(U[:, t], U[:, t], 0.5, K.OT[:, t], ALU.mult, ALU.mult))
            v.step(dve.tensor_tensor_scan(K.OT[:, t, 0:SEQ], A[:, t, 0:SEQ], U[:, t, 0:SEQ], 0.0, ALU.mult, ALU.add))
            v.do(dve.tensor_tensor(A[:, t, SEQ:TOK], A[:, t, SEQ:TOK], K.convs[:, 12 + t, 24:32], ALU.mult))
            dve.tensor_tensor(K.OT[:, t, SEQ:TOK], A[:, t, SEQ:TOK], U[:, t, SEQ:TOK], ALU.add).then_inc(N["h"], 1)


class RowTurns:

    BANK = 6

    def __init__(self, K, tag):
        self.K, self.tag = K, tag
        self.turned, self.moved = K.sem(tag + "_turned"), K.sem(tag + "_turn_moved")
        self.normed = K.sem(tag + "_normed")
        self.turns = []
        self.norm = None

    def out(self, tile, src, dst, n):
        self.turns.append((tile, "out", src, dst, n, len(self.turns)))
        return len(self.turns)

    def back(self, tile, src, dst, n, w, nth):
        self.turns.append((tile, "back", src, (dst, w, nth), n, len(self.turns)))

    def of(self, tile):
        return [x for x in self.turns if x[0] == tile]

    def pe(self, pe, turn):
        K = self.K
        _, kind, src, dst, n, m = turn
        if m:
            pe.wait_ge(self.moved, m)
        if kind == "back":
            pe.wait_ge(self.normed, dst[2])
        for h in range(H):
            if kind == "out":
                last = pe.transpose(K.ps[0:n, self.BANK, h * P:(h + 1) * P], src[:, h], K.ident[:])
            else:
                last = pe.transpose(K.ps[:, self.BANK, h * P:h * P + n], src[:, h], K.ident[0:n, 0:n])
        last.then_inc(self.turned, 1)

    def act(self, act, turn):
        K = self.K
        _, kind, src, dst, n, m = turn
        act.wait_ge(self.turned, m + 1)
        if kind == "out":
            act.activation(dst, heads(K.ps[0:n, self.BANK]), ACT.Identity).then_inc(self.moved, 1)
        else:
            act.activation(dst[0], heads(K.ps[:, self.BANK])[:, :, 0:n], ACT.Identity, scale=dst[1]
                           ).then_inc(self.moved, 1)


def project_tiles(K, t0, n, row, DST, tag, x=None, cols=TOK, turns=None, rows=None, stores=(), RQ=None,
                  preload=True):
    nc = K.nc
    xH, xL = x or (K.hH, K.hL)
    end = t0 + n
    of = lambda tile: turns.of(tile) if turns else []
    with ExitStack() as c:
        sb = lambda n_, s, d=F32: c.enter_context(nc.sbuf_tensor(tag + n_, s, d))
        if RQ is not None:
            SQ = sb("_sq", [P, 2, SEQ])
            QS, QM = sb("_qss", [P, H, TT8]), sb("_qtm", [P, H, TT8])
            sq, sums = K.sem(tag + "_qsq"), K.sem(tag + "_qsum")
        if rows is not None:
            row_list, sizes, norm, after = rows
            nt = len(sizes)
            T = sb("_t", [P, H, P])
            SS, RN, TM = (sb(x_, [P, nt, H]) for x_ in ("_ss", "_rn", "_tm"))
        flat = lambda x_: x_[:].rearrange("p a h -> p (a h)")
        with nc.Block(no_gpsimd_drain=True) as block:
            @block.sync
            def _(sp):
                K.loads(sp, end + 2 if preload else end)
                for (sem, count), dst, src in stores:
                    sp.wait_ge(sem, count)
                    K.store(sp, dst, src)
                if stores:
                    sp.wait_ge(K.stored, K.n_stored)

            @block.gpsimd
            def _(pool):
                K.split_lo(pool, end + 1 if preload else end)

            @block.scalar
            def _(act):
                for j in range(n):
                    t = t0 + j
                    K.split_hi(act, t + 2 if preload else min(t + 2, end))
                    for turn in of(j):
                        turns.act(act, turn)
                    act.wait_ge(K.tile_done, t + 1)
                    if row is None:
                        act.activation(DST[:, j], K.ps[:, 3 * (t % 2), 0:cols], ACT.Identity).then_inc(K.evac_act, 1)
                    else:
                        act.activation(DST[:, j].rearrange("p (a b) -> p a b", a=3), K.psum(t), ACT.Identity,
                                       bias=K.bias[:, row + j:row + j + 1]).then_inc(K.evac_act, 1)
                    if RQ is not None:
                        act.wait_ge(*K.emptied(t))
                        if j >= 2:
                            act.wait_ge(sums, j - 1)
                        act.activation(SQ[:, j % 2], DST[:, j, 0:SEQ], ACT.Square).then_inc(sq, 1)

            @block.tensor
            def _(pe):
                def norms(j):
                    pe.wait_ge(sq, j + 1)
                    for t in range(TT8):
                        q = j * TT8 + t
                        last = pe.matmul(K.ps[:, 7, q:q + 1], SQ[:, j % 2, t * P:(t + 1) * P], K.ones[:],
                                         start=True, stop=True)
                    last.then_inc(sums, 1)

                for j in range(n):
                    todo = of(j)

                    def meanwhile(k, todo=todo):
                        if k < len(todo):
                            turns.pe(pe, todo[k])

                    K.project(pe, t0 + j, xH, xL, groups=3 if row is not None else 1, cols=cols, meanwhile=meanwhile)
                    if RQ is not None and j >= 1:
                        norms(j - 1)
                if RQ is not None:
                    norms(n - 1)

            @block.vector
            def _(dve):
                v = K.V(dve)
                if rows is not None:
                    v.step(dve.memset(SS[:], 1.0))
                    v.do(dve.memset(T[:], 1.0))
                    for j, m in enumerate(sizes):
                        dve.wait_ge(turns.moved, after[j])
                        v.do(dve.tensor_tensor(T[0:m], row_list[j], row_list[j], ALU.mult))
                        v.do(dve.tensor_reduce(SS[0:m, j], T[0:m], AX.X, ALU.add))
                    v.do(dve.tensor_scalar(SS[:], SS[:], 1.0 / P, EPS, ALU.mult, ALU.add))
                    rsqrt(v, flat(SS), flat(RN), flat(TM))
                    for j, m in enumerate(sizes):
                        v.do(dve.tensor_tensor(row_list[j], row_list[j],
                                               RN[0:m, j].unsqueeze(2).broadcast_to([m, H, P]), ALU.mult))
                        dve.tensor_tensor(row_list[j], row_list[j], norm[0:m].unsqueeze(1).broadcast_to([m, H, P]),
                                          ALU.mult).then_inc(turns.normed, 1)
                if RQ is not None:
                    dve.wait_ge(sums, H)
                    v.do(dve.tensor_scalar(flat(QS), K.ps[:, 7, 0:H * TT8], 1.0 / P, EPS, ALU.mult, ALU.add))
                    rsqrt(v, flat(QS), flat(RQ), flat(QM))
                    v.do(dve.tensor_scalar(flat(RQ), flat(RQ), SCALE, None, ALU.mult))


def attend(K, KT, V, RQ, tag, fox):
    nc, i = K.nc, K.i
    its = [(h, t) for h in range(H) for t in range(TT8)]
    nb = [t + 1 if fox else MEM // P for _, t in its]
    UB = 4 if fox else MEM // P
    units = [(n, b, min(UB, nb[n] - b)) for n in range(len(its)) for b in range(0, nb[n], UB)]
    of_tile = [[u for u, x in enumerate(units) if x[0] == n] for n in range(len(its))]
    halves = [(n, a, min(512, nb[n] * P - a)) for n in range(len(its)) for a in range(0, nb[n] * P, 512)]
    half_of = [[x for x in range(len(halves)) if halves[x][0] == n] for n in range(len(its))]
    W = SEQ if fox else MEM
    NP = PAGES if fox else MEM // P
    PW = NP * P
    R = NB * H
    KEYS = lambda b: 3 + 3 * b // 2
    LOGF, MAX, EXP, TURN, VALUES, TAKE, NEW, LAST = 15, 16, 17, 18, (lambda b: 19 + 3 * b // 2), 30, 30, 31
    keys_at = {KEYS(b): b for b in range(NB)}
    values_at = {VALUES(b): b for b in range(NB)}
    with ExitStack() as c:
        sb = lambda n_, s, d=F32: c.enter_context(nc.sbuf_tensor(tag + n_, s, d))
        LG = sb("_logits", [P, 4, W])
        PT = sb("_pT", [P, 2, UB, P])
        OQ = sb("_o_rows", [P, 2, P])
        NM, RS = sb("_negmax", [P, 4]), sb("_sum", [P, 4])
        if fox:
            C = K.borrowed(tag + "_c_bc", 2, [P, 2, SEQ])
            MK = sb("_mask", [P, P])
        N = {x: K.sem(tag + "_" + x) for x in ("c_in0", "c_in1", "rel", "mask", "s", "lg", "max", "exp", "rs", "pT",
                                               "pTe", "v", "od", "b", "oe")}
        KV = [K.borrowed(f"{tag}_kv{q}", q, [P, NP, H, P])[:] for q in range(2)]
        QB = sb("_qb", [P, 2, H * P])
        QS, QN, QM = sb("_qs", [NB, H]), sb("_qn", [NB, H]), sb("_qm", [NB, H])
        SB = sb("_scores", [P, NP, NB, H])
        DLG = sb("_d_logits", [R, max(PW, H * P)])
        QR = DLG[0:NB, 0:H * P].rearrange("p (h d) -> p h d", h=H)
        DL = DLG[:, 0:PW]
        PC = sb("_p_cols", [P, NP, R])
        DM, DS = sb("_dm", [R, 1]), sb("_ds", [R, 1])
        OA = sb("_oa", [P, R])
        M = {x: K.sem(tag + "_d_" + x) for x in
             ("q", "qsq", "qr", "q_out", "qb0", "qb1", "k_in0", "k_in1", "used", "sc", "scT", "max", "exp", "p", "pT",
              "pTe", "v_in0", "v_in1", "o", "oa", "pg", "lf_in", "lfT", "lfs", "row_in", "newT", "newv")}
        if fox:
            PG = sb("_pages", [1, R], I32)
            LF = sb("_lf", [P, NP, NB, H])
            CC = QB[0:R, 0]
            LN, SN = sb("_lf_new", [R, 1]), sb("_s_new", [R, 4])
            Q3, K3, V3 = (sb(x, [R, P]) for x in ("_q3", "_k3", "_v3"))
        w_bc = K.qnw if fox else K.mqnw
        cache = ("cache_fox_k", "cache_fox_v") if fox else ("cache_mem_k", "cache_mem_v")
        per_load = 16 * (NP if fox else 1)
        BANK = K.ps[:, 7]
        with nc.Block(no_gpsimd_drain=True) as block:
            @block.sync
            def _(sp):
                def load_c(h):
                    if fox:
                        if h >= 2:
                            sp.wait_ge(N["rel"], TT8 * (h - 1))
                        sp.dma_start(C[:, h % 2], K.d_rows[1, h:h + 1].broadcast_to([P, SEQ])
                                     ).then_inc(N[f"c_in{h % 2}"], 16)

                def load(which, b, after, count):
                    src = i[cache[which]]
                    s = M[("k_in" if which == 0 else "v_in") + str(b % 2)]
                    pages = [sp.value_load(PG[0:1, b * NP + g:b * NP + g + 1], min_val=0, max_val=src.shape[1] - 1)
                             for g in range(NP)] if fox else None
                    if count:
                        sp.wait_ge(after, count)
                    if not fox:
                        sp.dma_start(KV[b % 2], src[0, b].rearrange("(g k) h d -> k g h d", k=P)).then_inc(s, 16)
                        return
                    for g in range(NP):
                        page = pages[g]
                        sp.dma_start(KV[b % 2][:, g], src[0, bass.ds(page, 1)].rearrange("a k h d -> k (a h) d")
                                     ).then_inc(s, 16)
                        if which == 0:
                            sp.dma_start(LF[:, g, b], i["cache_fox_logf"][0, bass.ds(page, 1)].rearrange(
                                "a k h -> k (a h)")).then_inc(M["lf_in"], 16)

                def load_q(b):
                    sp.dma_start(QB[:, b % 2], K.d_q[b:b + 1].rearrange("b h d -> b (h d)").broadcast_to([P, H * P])
                                 ).then_inc(M[f"qb{b % 2}"], 16)

                load_c(0)
                load_c(1)
                if fox:
                    sp.dma_start(PG[:], i["page_table"].rearrange("b g -> (b g)").unsqueeze(0)).then_inc(M["pg"], 16)
                    sp.wait_ge(M["pg"], 16)
                load(0, 0, None, 0)
                load(0, 1, None, 0)
                sp.wait_ge(M["qr"], 1)
                sp.dma_start(K.d_q, QR).then_inc(M["q_out"], 16)
                sp.wait_ge(M["q_out"], 16)
                load_q(0)
                load_q(1)
                if fox:
                    sp.dma_start(Q3[:], K.d_q.rearrange("b h d -> (b h) d")).then_inc(M["row_in"], 16)
                    sp.dma_start(K3[:], K.o["fox_k_s"][0, :, 0].rearrange("b h d -> (b h) d")).then_inc(M["row_in"], 16)
                    sp.dma_start(V3[:], K.o["fox_v_s"][0, :, 0].rearrange("b h d -> (b h) d")).then_inc(M["row_in"], 16)
                    sp.dma_start(LN[:], K.d_lf.rearrange("b (h a) -> (b h) a", a=1)).then_inc(M["row_in"], 16)
                for b in range(2, NB):
                    load(0, b, M["sc"], b - 1)
                    load_q(b)
                    if b == 5:
                        load_c(2)
                for b in range(NB):
                    if b < 2:
                        load(1, b, M["sc"], NB - 1 + b)
                    else:
                        load(1, b, M["o"], b - 1)
                    if b == 1:
                        load_c(3)
                sp.wait_ge(M["o"], NB - 1)
                K.loads(sp, K.at_load + 2)

            @block.gpsimd
            def _(pool):
                if not fox:
                    return
                g = K.G(pool)
                g.do(pool.memset(MK[:], 0.0))
                pool.affine_select(out=MK[:], in_=MK[:], compare_op=ALU.is_ge, fill=NEG, base=0,
                                   pattern=[[-1, P]], channel_multiplier=1).then_inc(N["mask"], 1)
                for n, (h, t) in enumerate(its):
                    pool.wait_ge(N[f"c_in{h % 2}"], 16 * (h // 2 + 1))
                    if n >= 4:
                        pool.wait_ge(N["pT"], of_tile[n - 4][-1] + 1)
                    w = nb[n] * P
                    pool.tensor_scalar(LG[:, n % 4, 0:w], C[:, h % 2, 0:w], K.TK[:, t, 1, h:h + 1], None, ALU.subtract
                                       ).then_inc(N["rel"], 1)

            @block.tensor
            def _(pe):
                def scores(n):
                    h, t = its[n]
                    for x in half_of[n]:
                        _, a, w = halves[x]
                        if x >= 3:
                            pe.wait_ge(N["lg"], x - 2)
                        pe.matmul(K.ps[:, x % 3, 0:w], K.OT[:, h, t * P:(t + 1) * P], KT[:, h, a:a + w],
                                  start=True, stop=True).then_inc(N["s"], 1)

                def turn(u):
                    n, b0, k = units[u]
                    pe.wait_ge(N["exp"], n + 1)
                    if u >= 2:
                        pe.wait_ge(N["pTe"], u - 1)
                    for b in range(k):
                        last = pe.transpose(K.ps[:, 4 + u % 2, b * P:(b + 1) * P],
                                            LG[:, n % 4, (b0 + b) * P:(b0 + b + 1) * P], K.ident[:])
                    last.then_inc(N["pT"], 1)

                def values(u):
                    n, b0, k = units[u]
                    h, t = its[n]
                    pe.wait_ge(N["pTe"], u + 1)
                    if n >= 1 and b0 == 0:
                        pe.wait_ge(N["od"], n)
                    for b in range(k):
                        last = pe.matmul(K.ps[:, 6, 0:P], PT[:, u % 2, b], V[:, b0 + b, h],
                                         start=(b0 + b == 0), stop=(b0 + b == nb[n] - 1))
                    last.then_inc(N["v"], 1)

                def turn_back(n):
                    pe.wait_ge(N["od"], n + 1)
                    if n >= 1:
                        pe.wait_ge(N["oe"], n)
                    pe.transpose(K.ps[:, 3, 0:P], OQ[:, n % 2], K.ident[:]
                                 ).then_inc(N["b"], 1)

                def decode(n):
                    if n == LOGF and fox:
                        pe.wait_ge(M["qr"], 1)
                        pe.wait_ge(M["lf_in"], 16 * R)
                        for g in range(NP):
                            last = pe.transpose(BANK[0:R, g * P:(g + 1) * P], LF[:, g].rearrange("p b h -> p (b h)"),
                                                K.ident[:])
                        last.then_inc(M["lfT"], 1)
                    if n == MAX:
                        pe.wait_ge(M["sc"], NB)
                        if fox:
                            pe.wait_ge(M["lfs"], 1)
                        for g in range(NP):
                            last = pe.transpose(BANK[0:R, g * P:(g + 1) * P], SB[:, g].rearrange("p b h -> p (b h)"),
                                                K.ident[:])
                        last.then_inc(M["scT"], 1)
                    if n == TURN:
                        pe.wait_ge(M["p"], 1)
                        for g in range(NP):
                            last = pe.transpose(BANK[:, g * R:(g + 1) * R], DL[:, g * P:(g + 1) * P],
                                                K.ident[0:R, 0:R])
                        last.then_inc(M["pT"], 1)
                    if n in values_at:
                        b = values_at[n]
                        pe.wait_ge(M["pTe"], 1)
                        pe.wait_ge(M[f"v_in{b % 2}"], per_load * (b // 2 + 1))
                        for h in range(H):
                            r = b * H + h
                            for g in range(NP):
                                last = pe.matmul(BANK[:, r:r + 1], KV[b % 2][:, g, h], PC[:, g, r:r + 1],
                                                 start=(g == 0), stop=(g == NP - 1))
                        last.then_inc(M["o"], 1)
                    if n == NEW and fox:
                        pe.wait_ge(M["newv"], 1)
                        pe.wait_ge(M["oa"], 1)
                        pe.matmul(BANK[:, 0:R], V3[:], K.ident[0:R, 0:R], start=True, stop=True
                                  ).then_inc(M["newT"], 1)

                for h in range(H):
                    last = pe.transpose(BANK[0:NB, h * P:(h + 1) * P], K.OT[:, h, SEQ:TOK], K.ident[:])
                last.then_inc(M["q"], 1)
                scores(0)
                scores(1)
                for n in range(len(its)):
                    if n + 2 < len(its):
                        scores(n + 2)
                    for u in of_tile[n]:
                        turn(u)
                        if u >= 1:
                            values(u - 1)
                    if n >= 2:
                        turn_back(n - 2)
                    decode(n)
                values(len(units) - 1)
                turn_back(len(its) - 2)
                turn_back(len(its) - 1)

            @block.vector
            def _(dve):
                v = K.V(dve)
                if fox:
                    dve.wait_ge(N["mask"], 1)

                def logits(n):
                    h, t = its[n]
                    w = nb[n] * P
                    if n >= 4:
                        dve.wait_ge(N["pT"], of_tile[n - 4][-1] + 1)
                    lg = LG[:, n % 4, 0:w]
                    rq = RQ[:, h, t:t + 1]
                    if fox:
                        dve.wait_ge(N["rel"], n + 1)
                    for x in half_of[n]:
                        _, a, m = halves[x]
                        dve.wait_ge(N["s"], x + 1)
                        if fox:
                            ins = dve.scalar_tensor_tensor(lg[:, a:a + m], K.ps[:, x % 3, 0:m], rq,
                                                           lg[:, a:a + m], ALU.mult, ALU.subtract)
                        else:
                            ins = dve.tensor_scalar(lg[:, a:a + m], K.ps[:, x % 3, 0:m], rq, None, ALU.mult)
                        ins.then_inc(N["lg"], 1)
                    dve.wait_ge(N["lg"], half_of[n][-1] + 1)
                    if fox:
                        v.do(dve.tensor_tensor(lg[:, w - P:w], lg[:, w - P:w], MK[:], ALU.add))
                    dve.tensor_reduce(NM[:, n % 4:n % 4 + 1], lg, AX.X, ALU.max, negate=True).then_inc(N["max"], 1)

                def invert_sum(n):
                    dve.wait_ge(N["exp"], n + 1)
                    dve.reciprocal(RS[:, n % 4:n % 4 + 1], RS[:, n % 4:n % 4 + 1]).then_inc(N["rs"], 1)

                def decode_queries():
                    dve.wait_ge(M["qsq"], 1)
                    v.do(dve.tensor_reduce(QS[:], QR, AX.X, ALU.add))
                    v.do(dve.tensor_scalar(QS[:], QS[:], 1.0 / P, EPS, ALU.mult, ALU.add))
                    rsqrt(v, QS[:], QN[:], QM[:])
                    v.do(dve.tensor_scalar(QN[:], QN[:], SCALE, None, ALU.mult))
                    v.do(dve.tensor_tensor(QR, heads(BANK[0:NB]), QN[:].unsqueeze(2).broadcast_to([NB, H, P]),
                                           ALU.mult))
                    dve.tensor_tensor(QR, QR, w_bc[0:NB].unsqueeze(1).broadcast_to([NB, H, P]), ALU.mult
                                      ).then_inc(M["qr"], 1)

                def decode_keys(b):
                    dve.wait_ge(M[f"k_in{b % 2}"], per_load * (b // 2 + 1))
                    dve.wait_ge(M[f"qb{b % 2}"], 16 * (b // 2 + 1))
                    kv = KV[b % 2]
                    flat = kv.rearrange("p g h d -> p g (h d)")
                    dve.tensor_tensor(flat, flat, QB[:, b % 2].unsqueeze(1).broadcast_to([P, NP, H * P]), ALU.mult
                                      ).then_inc(M["used"], 1)
                    dve.wait_ge(M["used"], b + 1)
                    dve.tensor_reduce(SB[:, :, b], kv, AX.X, ALU.add).then_inc(M["sc"], 1)

                def decode_sum_logf():
                    dve.wait_ge(M["q_out"], 16)
                    dve.wait_ge(M["used"], NB)
                    dve.wait_ge(M["lfT"], 1)
                    dve.wait_ge(M["row_in"], 64)
                    v.do(dve.memset(DL, 1.0))
                    dve.tensor_tensor_scan(CC, DL, BANK[0:R, 0:PW], 0.0, ALU.mult, ALU.add).then_inc(M["lfs"], 1)
                    dve.wait_ge(M["lfs"], 1)
                    v.do(dve.tensor_tensor(LN[:], LN[:], CC[:, PW - 1:PW], ALU.add))
                    v.do(dve.tensor_scalar(CC, CC, LN[:, 0:1], None, ALU.subtract))

                def decode_max():
                    dve.wait_ge(M["scT"], 1)
                    if fox:
                        v.do(dve.tensor_tensor(DL, BANK[0:R, 0:PW], CC, ALU.subtract))
                        v.do(dve.tensor_tensor(Q3[:], Q3[:], K3[:], ALU.mult))
                        v.do(dve.tensor_reduce(SN[:, 0:1], Q3[:], AX.X, ALU.add))
                        v.do(dve.tensor_reduce(DM[:], DL, AX.X, ALU.max))
                        v.do(dve.tensor_tensor(DM[:], DM[:], SN[:, 0:1], ALU.max))
                        dve.tensor_scalar(DM[:], DM[:], -1.0, None, ALU.mult).then_inc(M["max"], 1)
                    else:
                        dve.wait_ge(M["q_out"], 16)
                        v.do(dve.tensor_copy(DL, BANK[0:R, 0:PW]))
                        dve.tensor_reduce(DM[:], DL, AX.X, ALU.max, negate=True).then_inc(M["max"], 1)

                def decode_normalise():
                    dve.wait_ge(M["exp"], 1)
                    if fox:
                        v.do(dve.tensor_tensor(DS[:], DS[:], SN[:, 1:2], ALU.add))
                    v.do(dve.reciprocal(DS[:], DS[:]))
                    dve.tensor_scalar(DL, DL, DS[:, 0:1], None, ALU.mult).then_inc(M["p"], 1)
                    if fox:
                        v.do(dve.tensor_tensor(SN[:, 2:3], SN[:, 1:2], DS[:], ALU.mult))
                        dve.tensor_scalar(V3[:], V3[:], SN[:, 2:3], None, ALU.mult).then_inc(M["newv"], 1)

                def decode_add_new():
                    dve.wait_ge(M["newT"], 1)
                    dve.wait_ge(M["oa"], 1)
                    v.do(dve.tensor_tensor(K.OT[:, :, SEQ:TOK].rearrange("p h b -> p b h"),
                                           OA[:].rearrange("p (b h) -> p b h", b=NB),
                                           BANK[:, 0:R].rearrange("p (b h) -> p b h", b=NB), ALU.add))

                logits(0)
                logits(1)
                for n in range(len(its)):
                    if n + 2 < len(its):
                        logits(n + 2)
                    invert_sum(n)
                    if n == 0:
                        decode_queries()
                    if n in keys_at:
                        decode_keys(keys_at[n])
                    if n == LOGF and fox:
                        decode_sum_logf()
                    if n == MAX:
                        decode_max()
                    if n == EXP:
                        decode_normalise()
                    if n == LAST and fox:
                        decode_add_new()

            @block.scalar
            def _(act):
                a = K.A(act)

                def exps(n):
                    w = nb[n] * P
                    act.wait_ge(N["max"], n + 1)
                    act.activation(LG[:, n % 4, 0:w], LG[:, n % 4, 0:w], ACT.Exp, bias=NM[:, n % 4:n % 4 + 1],
                                   accum_out=RS[:, n % 4:n % 4 + 1]).then_inc(N["exp"], 1)

                def turned(u):
                    k = units[u][2]
                    act.wait_ge(N["pT"], u + 1)
                    if u >= 2:
                        act.wait_ge(N["v"], u - 1)
                    act.activation(PT[:, u % 2, 0:k], heads(K.ps[:, 4 + u % 2])[:, 0:k], ACT.Identity
                                   ).then_inc(N["pTe"], 1)

                def divide(n):
                    act.wait_ge(N["v"], of_tile[n][-1] + 1)
                    act.wait_ge(N["rs"], n + 1)
                    if n >= 2:
                        act.wait_ge(N["b"], n - 1)
                    act.activation(OQ[:, n % 2], K.ps[:, 6, 0:P], ACT.Identity,
                                   scale=RS[:, n % 4:n % 4 + 1]).then_inc(N["od"], 1)

                def out(n):
                    h, t = its[n]
                    act.wait_ge(N["b"], n + 1)
                    act.activation(K.OT[:, h, t * P:(t + 1) * P], K.ps[:, 3, 0:P], ACT.Identity).then_inc(N["oe"], 1)

                def decode(n):
                    if n == EXP:
                        act.wait_ge(M["max"], 1)
                        last = act.activation(DL, DL, ACT.Exp, bias=DM[:], accum_out=DS[:])
                        if fox:
                            a.step(last)
                            last = act.activation(SN[:, 1:2], SN[:, 0:1], ACT.Exp, bias=DM[:])
                        last.then_inc(M["exp"], 1)
                    if n == TURN:
                        act.wait_ge(M["pT"], 1)
                        act.activation(PC[:].rearrange("p g r -> p (g r)"), BANK[:, 0:NP * R], ACT.Identity
                                       ).then_inc(M["pTe"], 1)
                    if n == TAKE:
                        act.wait_ge(M["o"], NB)
                        dst = K.OT[:, :, SEQ:TOK].rearrange("p h b -> p b h")
                        act.activation(OA[:].rearrange("p (b h) -> p b h", b=NB) if fox else dst,
                                       BANK[:, 0:R].rearrange("p (b h) -> p b h", b=NB), ACT.Identity
                                       ).then_inc(M["oa"], 1)

                act.wait_ge(M["q"], 1)
                act.activation(QR, heads(BANK[0:NB]), ACT.Square).then_inc(M["qsq"], 1)
                exps(0)
                for n in range(len(its)):
                    if n + 1 < len(its):
                        exps(n + 1)
                    for u in of_tile[n]:
                        turned(u)
                        if n >= 1 and u == of_tile[n][0]:
                            divide(n - 1)
                    if n >= 2:
                        out(n - 2)
                    decode(n)
                divide(len(its) - 1)
                out(len(its) - 2)
                out(len(its) - 1)


def memory_norm(K, MH, ML):
    nc, i = K.nc, K.i
    with ExitStack() as c:
        sb = lambda n_, s, d=F32: c.enter_context(nc.sbuf_tensor("y" + n_, s, d))
        X = sb("_x", [P, 2, D])
        SQ = sb("_sq", [P, D])
        SS, RS, TM = sb("_ss", [P, 2]), sb("_rs", [P, 2]), sb("_tm", [P, 2])
        x_in, sq, sc = K.sem("mem_in"), K.sem("mem_sq"), K.sem("mem_scaled")
        tr, hi, lo = K.sem("mem_tr"), K.sem("mem_hi"), K.sem("mem_lo")
        with nc.Block(no_gpsimd_drain=True) as block:
            @block.sync
            def _(sp):
                for t in range(2):
                    sp.dma_start(X[:, t], i["mem_prompt"][0, t * P:(t + 1) * P]).then_inc(x_in, 16)

            @block.scalar
            def _(act):
                act.wait_ge(x_in, 32)
                for t in range(2):
                    act.activation(SQ[:], X[:, t], ACT.Square, accum_out=SS[:, t:t + 1]).then_inc(sq, 1)
                    act.wait_ge(sq, t + 1)
                for k in range(KD):
                    act.wait_ge(tr, k + 1)
                    w = K.par[:, PROW["mem_norm_w"] + k:PROW["mem_norm_w"] + k + 1]
                    act.activation(MH[:, k], K.ps[:, k % 4, 0:MEM], ACT.Identity, scale=w).then_inc(hi, 1)

            @block.vector
            def _(dve):
                v = K.V(dve)
                dve.wait_ge(sq, 2)
                v.do(dve.tensor_scalar(SS[:], SS[:], 1.0 / D, EPS, ALU.mult, ALU.add))
                rsqrt(v, SS[:], RS[:], TM[:])
                for t in range(2):
                    dve.tensor_scalar(X[:, t], X[:, t], RS[:, t:t + 1], None, ALU.mult).then_inc(sc, 1)
                for k in range(KD):
                    dve.wait_ge(hi, k + 1)
                    w = K.par[:, PROW["mem_norm_w"] + k:PROW["mem_norm_w"] + k + 1]
                    dve.scalar_tensor_tensor(ML[:, k], K.ps[:, k % 4, 0:MEM], w, MH[:, k].bitcast(F32), ALU.mult,
                                             ALU.subtract).then_inc(lo, 1)

            @block.tensor
            def _(pe):
                pe.wait_ge(sc, 2)
                for k in range(KD):
                    if k >= 4:
                        pe.wait_ge(lo, k - 3)
                    for t in range(2):
                        last = pe.transpose(K.ps[:, k % 4, t * P:(t + 1) * P], X[:, t, k * P:(k + 1) * P], K.ident[:])
                    last.then_inc(tr, 1)


def build(nc, ins, outs):
    with ExitStack() as ctx:
        K = Kernel(nc, ins, outs, ctx)
        dram = lambda name, shape: nc.dram_tensor(name, shape, F32).ap()
        K.d_rows = dram("rows_g_c_beta", (3, H, SEQ))
        K.d_ab = dram("decode_alpha_beta_rows", (2, H, NB))
        K.d_lf = dram("decode_logf", (NB, H))
        K.d_qk = dram("decode_qk", (2, NB, H, P))
        K.d_unit = dram("unit_factors_q_k", (2 * H, SEQ))
        K.d_q = dram("decode_q", (NB, H, P))

        at = {}

        def plan(name, n, label=None):
            at[label or name] = len(K.tiles)
            K.plan_in(name, n)

        def plan_merge(n):
            at[f"merge{n}"] = len(K.tiles)
            wb = ins["w_branch"][0, n]
            for d in range(KD):
                a = OFF["gate"] + n * D + d * P
                K.plan(ins["w_in"][0, :, a:a + P].rearrange("(k p) c -> p k c", p=P), KD, "act")
                K.plan(wb[:, d * P:(d + 1) * P].rearrange("(k p) c -> p k c", p=P), 4, "dve")

        plan("dn_qkv", 12)
        plan("dn_z", 4)
        plan_merge(0)
        plan("lru_x", 4)
        plan("lru_g", 4)
        plan_merge(1)
        plan("fk", 4)
        plan("fv", 4)
        plan("fq", 4)
        plan("fg", 4)
        plan_merge(2)
        at["mem_kv"] = len(K.tiles)
        for e in range(8):
            K.plan(ins["w_mem_kv"][0, :, e * P:(e + 1) * P].rearrange("(k p) c -> p k c", p=P), KD, "act")
        plan("mq", 4)
        plan("mg", 4)
        plan_merge(3)
        at["w_out"] = len(K.tiles)
        for e in range(KD):
            K.plan(ins["w_out"][0, :, e * P:(e + 1) * P].rearrange("(k p) c -> p k c", p=P), KD, "act")

        def branch_end(t_gate, name, n, tag, side=None):
            with nc.sbuf_tensor(tag + "_gate", [P, H, TOK], F32) as G:
                with ExitStack() as c:
                    gate_branch(K, t_gate, name, G, tag, side and side(K, c))
                merge_branch(K, at[f"merge{n}"], n, G)
            if n in (0, 2):
                K.stage_ends()

        setup(K)
        with ExitStack() as c:
            masks = DeltaMasks(K, lambda n_, s, d=F32: c.enter_context(nc.sbuf_tensor(n_, s, d)))
            conv_tiles(K, at["dn_qkv"], 12, "dn_conv_w", 0, K.hpar, True,
                       lambda j: K.OT[:, j] if j < H else K.merged[:, j - H], "ca", "dn_conv", "dn_conv_s",
                       masks=masks, squares=2 * H, small=True)
            unit_queries_and_keys(K)
            delta_rule(K, masks)
        branch_end(at["dn_z"], "dn_z", 0, "ga", DeltaDecode)
        conv_tiles(K, at["lru_x"], 4, "lru_conv_w", 12, K.par, False, lambda j: K.OT[:, j], "cb", "lru_conv",
                   "lru_conv_s")
        branch_end(at["lru_g"], "lru_g", 1, "gb", Lru)
        sizes = [P] * TT8 + [NB]
        cols = lambda j: slice(j * P, j * P + sizes[j])
        rows_of = lambda p, s: [outs[p][0, 0, t * P:(t + 1) * P] for t in range(TT8)] + [outs[s][0, :, 0]]
        with ExitStack() as c:
            sb = lambda n_, s: c.enter_context(nc.sbuf_tensor(n_, s, F32))
            KX = sb("fox_kT", [P, H, TOK])
            VR = sb("fox_v_rows", [P, TT8, H, P])
            RQ = sb("fox_rq", [P, H, TT8])
            with nc.sbuf_tensor("fox_vT", [P, H, TOK], F32) as VX, \
                    nc.sbuf_tensor("fox_v_new_rows", [NB, H, P], F32) as VS:
                with nc.sbuf_tensor("fox_k_new_rows", [NB, H, P], F32) as KS:
                    project_tiles(K, at["fk"], 4, BROW["fk"], KX, "fk")
                    KR = K.OT[:].rearrange("p h t -> p (h t)")[:, 0:SEQ * H].rearrange(
                        "p (t h d) -> p t h d", t=TT8, h=H)
                    k_rows = [KR[:, j] for j in range(TT8)] + [KS[:]]
                    turns = RowTurns(K, "fkr")
                    after = [turns.out(j // 5, KX[:, :, cols(j)], k_rows[j], n) for j, n in enumerate(sizes)]
                    w = K.par[:, PROW["fox_qn_w"]:PROW["fox_qn_w"] + 1]
                    for j, n in enumerate(sizes):
                        turns.back(2 + j // 5, k_rows[j], KX[:, :, cols(j)], n, w, j + 1)
                    project_tiles(K, at["fv"], 4, BROW["fv"], VX, "fv", turns=turns,
                                  rows=(k_rows, sizes, K.knw, after),
                                  stores=[((turns.normed, j + 1), d, k_rows[j])
                                          for j, d in enumerate(rows_of("fox_k", "fox_k_s"))])
                v_rows = [VR[:, j] for j in range(TT8)] + [VS[:]]
                turns = RowTurns(K, "fvr")
                after = [turns.out(j // 3, VX[:, :, cols(j)], v_rows[j], n) for j, n in enumerate(sizes)]
                project_tiles(K, at["fq"], 4, BROW["fq"], K.OT, "fq", turns=turns, RQ=RQ, preload=False,
                              stores=[((turns.moved, after[j]), d, v_rows[j])
                                      for j, d in enumerate(rows_of("fox_v", "fox_v_s"))])
            attend(K, KX, VR, RQ, "fa", True)
        branch_end(at["fg"], "fg", 2, "gc")
        with ExitStack() as c:
            sb = lambda n_, s, d=F32: c.enter_context(nc.sbuf_tensor(n_, s, d))
            KX, VX = sb("mem_kT", [P, H, MEM]), sb("mem_vT", [P, H, MEM])
            KR, VR = sb("mem_k_rows", [P, 2, H, P]), sb("mem_v_rows", [P, 2, H, P])
            RQ = sb("mem_rq", [P, H, TT8])
            with ExitStack() as c2:
                MH = c2.enter_context(nc.sbuf_tensor("memH", [P, KD, MEM], F32R))
                ML = c2.enter_context(nc.sbuf_tensor("memL", [P, KD, MEM], F32R))
                memory_norm(K, MH, ML)
                t = at["mem_kv"]
                project_tiles(K, t, 4, None, KX, "mk", x=(MH, ML), cols=MEM)
                project_tiles(K, t + 4, 4, None, VX, "mv", x=(MH, ML), cols=MEM)
            turns = RowTurns(K, "mr")
            cols = lambda j: slice(j * P, (j + 1) * P)
            after = [turns.out(0, KX[:, :, cols(j)], KR[:, j], P) for j in range(2)]
            v_after = [turns.out(1, VX[:, :, cols(j)], VR[:, j], P) for j in range(2)]
            w = K.par[:, PROW["mem_qn_w"]:PROW["mem_qn_w"] + 1]
            for j in range(2):
                turns.back(2, KR[:, j], KX[:, :, cols(j)], P, w, j + 1)
            tile = lambda p, j: outs[p][0, 0, j * P:(j + 1) * P]
            project_tiles(K, at["mq"], 4, BROW["mq"], K.OT, "mq", turns=turns, RQ=RQ, preload=False,
                          rows=([KR[:, j] for j in range(2)], [P, P], K.mknw, after),
                          stores=[((turns.normed, j + 1), tile("mem_k", j), KR[:, j]) for j in range(2)] +
                                 [((turns.moved, v_after[j]), tile("mem_v", j), VR[:, j]) for j in range(2)])
            attend(K, KX, VR, RQ, "ma", False)
        branch_end(at["mg"], "mg", 3, "gd")
        K.OT_space.close()
        output(K, at["w_out"])


INS = ["x_prompt", "x_sample", "cache_fox_k", "cache_fox_v", "cache_fox_logf", "cache_mem_k", "cache_mem_v",
       "state_dn", "state_dn_conv", "state_lru_h", "state_lru_conv", "page_table", "mem_prompt", "norm_w", "w_in",
       "b_in", "dn_conv_w", "dn_A_log", "dn_dt_bias", "dn_onorm_w", "lru_conv_w", "lru_conv_b", "lru_w_r",
       "lru_b_r", "lru_w_i", "lru_b_i", "lru_lambda", "fox_qn_w", "fox_kn_w", "mem_norm_w", "w_mem_kv",
       "mem_qn_w", "mem_kn_w", "w_branch", "w_out"]
OUTS = [("y", (1, SEQ, D)), ("y_s", (NB, 1, D)),
        ("fox_k", (1, 1, SEQ, H, P)), ("fox_v", (1, 1, SEQ, H, P)), ("fox_logf", (1, 1, SEQ, H)),
        ("mem_k", (1, 1, MEM, H, P)), ("mem_v", (1, 1, MEM, H, P)), ("dn_state", (1, 1, H, P, P)),
        ("dn_conv", (1, 1, 3, 1536)), ("lru_h", (1, 1, BW)), ("lru_conv", (1, 1, 3, BW)),
        ("fox_k_s", (1, NB, 1, H, P)), ("fox_v_s", (1, NB, 1, H, P)), ("fox_logf_s", (1, NB, 1, H)),
        ("dn_state_s", (1, NB, H, P, P)), ("dn_conv_s", (1, NB, 3, 1536)), ("lru_h_s", (1, NB, BW)),
        ("lru_conv_s", (1, NB, 3, BW))]


def kernel(**inputs):
    import concourse.bacc as bacc
    import numpy as np
    from concourse.bass_utils import run_bass_kernel_spmd

    nc = bacc.Bacc("TRN2", target_bir_lowering=False, num_devices=1)
    arrays, ins, outs = {}, {}, {}
    for name in INS:
        a = np.ascontiguousarray(inputs[name])
        arrays["in_" + name] = a
        ins[name] = nc.dram_tensor("in_" + name, a.shape, mybir.dt.from_np(a.dtype), kind="ExternalInput").ap()
    for name, shape in OUTS:
        outs[name] = nc.dram_tensor("out_" + name, shape, F32, kind="ExternalOutput").ap()
    build(nc, ins, outs)
    r = run_bass_kernel_spmd(nc, [arrays], core_ids=[0])
    return tuple(r.results[0]["out_" + name] for name, _ in OUTS)
```
